# Optimizing a Trainium2 kernel written in Bass

```python
import jax, jax.numpy as jnp
from jax import lax
import numpy as np

D_MODEL = 1024
BATCH = 1
SEQ = 1024
DEPTH = 1
DEC_BATCH = 8
DEC_SEQ = 8
PAST_LEN = 1024
PAGE_SIZE = 128

HEAD_DIM = 64
MIX_WIDTH = D_MODEL
N_HEADS = MIX_WIDTH // HEAD_DIM
H_A = N_HEADS // 2
R_A = 4
G_A = H_A // R_A
H_B = N_HEADS - H_A
ROT_DIM = HEAD_DIM // 4
ROPE_THETA = 500000.0
CMP_STRIDE = 16
CMP_LEN = 2 * CMP_STRIDE
CMP_HID = 2 * HEAD_DIM
SLC_BLK = 64
SLC_TOP = 16
N_LOCAL = 2
FORCE_BONUS = 1.0e4
WIN_A = 512
DIL_PAIRS = ((128, 1), (512, 4), (2048, 16))
DIL_MAX = 2048
Q_BLK = 128
WIN_PAD = -(-WIN_A // Q_BLK) * Q_BLK
CONV_W = 3
D_FF = ((8 * D_MODEL // 3 + 255) // 256) * 256
EPS = 1e-6
TINY = 1e-30
SCALE = HEAD_DIM ** -0.5
SPLITS = (H_A * HEAD_DIM, 2 * G_A * HEAD_DIM, 2 * G_A * HEAD_DIM, 2 * G_A * HEAD_DIM, 3 * H_A, H_B * HEAD_DIM, 2 * H_B * HEAD_DIM)
IN_DIM = sum(SPLITS)

kernel_name = 'hybrid_nsa_dilated_convglu_step'

def _rms_norm(x, g):
    xf = x.astype(jnp.float32)
    y = xf * lax.rsqrt(jnp.mean(xf * xf, axis=-1, keepdims=True) + EPS)
    return (y * g.astype(jnp.float32)).astype(x.dtype)

def _rope(x, pos):
    half = ROT_DIM // 2
    inv = ROPE_THETA ** (-2.0 * jnp.arange(half, dtype=jnp.float32) / ROT_DIM)
    ang = pos.astype(jnp.float32)[:, None] * inv[None, :]
    cos = jnp.cos(ang)[:, None, :]
    sin = jnp.sin(ang)[:, None, :]
    xf = x.astype(jnp.float32)
    x1 = xf[..., :half]
    x2 = xf[..., half:ROT_DIM]
    out = jnp.concatenate([x1 * cos - x2 * sin, x2 * cos + x1 * sin, xf[..., ROT_DIM:]], axis=-1)
    return out.astype(x.dtype)

def _masked_softmax(s, mask):
    s = jnp.where(mask, s.astype(jnp.float32), -jnp.inf)
    m = jnp.max(s, axis=-1, keepdims=True)
    m = jnp.where(jnp.isfinite(m), m, 0.0)
    e = jnp.exp(s - m)
    l = jnp.maximum(jnp.sum(e, axis=-1, keepdims=True), TINY)
    return e / l, (m + jnp.log(l))[..., 0]

def _prep_kv(z, gk, pos, n_kv):
    B, S = z.shape[:2]
    kv = z.reshape(B, S, 2, n_kv, HEAD_DIM)
    k = _rope(_rms_norm(kv[:, :, 0], gk), pos)
    return jnp.stack([k, kv[:, :, 1]], axis=2)

def _project(x, pos, g_attn, w_in, gq_a, gk_cmp, gk_slc, gk_win, gq_b, gk_b):
    B, S = x.shape[:2]
    z = _rms_norm(x, g_attn) @ w_in
    qa, zc, zs, zw, gl, qb, zb = jnp.split(z, np.cumsum(SPLITS)[:-1].tolist(), axis=-1)
    qa = _rope(_rms_norm(qa.reshape(B, S, H_A, HEAD_DIM), gq_a), pos)
    qb = _rope(_rms_norm(qb.reshape(B, S, H_B, HEAD_DIM), gq_b), pos)
    return (qa, _prep_kv(zc, gk_cmp, pos, G_A), _prep_kv(zs, gk_slc, pos, G_A), _prep_kv(zw, gk_win, pos, G_A),
            gl.reshape(B, S, H_A, 3), qb, _prep_kv(zb, gk_b, pos, H_B))

def _chunk_feats(rows, pe, w1):
    B, L, G = rows.shape[:3]
    c = rows.reshape(B, L // CMP_STRIDE, CMP_STRIDE, G, HEAD_DIM)
    pe2 = pe.reshape(2, CMP_STRIDE, 1, HEAD_DIM)
    w = w1.reshape(2, CMP_STRIDE, HEAD_DIM, CMP_HID)
    head = jnp.einsum('bnrge,ref->bngf', c + pe2[0], w[0])
    tail = jnp.einsum('bnrge,ref->bngf', c + pe2[1], w[1])
    return head, tail

def _compress_from_feats(head, tail, w2):
    return jnp.einsum('bngf,fe->bnge', jax.nn.gelu(head[:, :-1] + tail[:, 1:]), w2)

def _nsa_mix(q, gl, t, kc, vc, n_slc, select, kw, vw, sw):
    B, Q = q.shape[:2]
    qg = q.reshape(B, Q, G_A, R_A, HEAD_DIM)
    n_cmp = kc.shape[1]
    cmp_last = jnp.arange(n_cmp) * CMP_STRIDE + CMP_LEN - 1
    s = jnp.einsum('bqgre,bige->bqgri', qg, kc) * SCALE
    p_cmp, _ = _masked_softmax(s, (cmp_last[None, :] <= t[:, None])[:, None, None, :])
    o_cmp = jnp.einsum('bqgri,bige->bqgre', p_cmp.astype(vc.dtype), vc)
    ci = jnp.arange(n_cmp)[:, None] * CMP_STRIDE
    sj = jnp.arange(n_slc)[None, :] * SLC_BLK
    overlap = ((ci < sj + SLC_BLK) & (ci + CMP_LEN > sj)).astype(jnp.float32)
    imp = jnp.einsum('bqgri,ij->bqgj', p_cmp, overlap)
    back = (t // SLC_BLK)[:, None] - jnp.arange(n_slc)[None, :]
    forced = (jnp.arange(n_slc)[None, :] == 0) | ((back >= 0) & (back < N_LOCAL))
    score = jnp.where((back >= 0)[:, None, :], imp + FORCE_BONUS * forced[:, None, :], -jnp.inf)
    top, idx = lax.top_k(score, min(SLC_TOP, n_slc))
    ks, vs, ms = select(idx, top > -jnp.inf)
    s = jnp.einsum('bqgre,bqgke->bqgrk', qg, ks) * SCALE
    p, _ = _masked_softmax(s, ms[:, :, :, None, :])
    o_slc = jnp.einsum('bqgrk,bqgke->bqgre', p.astype(vs.dtype), vs)
    dw = t[:, None] - sw[None, :]
    s = jnp.einsum('bqgre,bkge->bqgrk', qg, kw) * SCALE
    p, _ = _masked_softmax(s, ((dw >= 0) & (dw < WIN_A) & (sw >= 0)[None, :])[:, None, None, :])
    o_win = jnp.einsum('bqgrk,bkge->bqgre', p.astype(vw.dtype), vw)
    g = jax.nn.sigmoid(gl.astype(jnp.float32)).reshape(B, Q, G_A, R_A, 3)
    o = g[..., 0:1] * o_cmp + g[..., 1:2] * o_slc + g[..., 2:3] * o_win
    return o.reshape(B, Q, H_A, HEAD_DIM).astype(q.dtype)

def _nsa_prompt(q, gl, kvc, kvs, kvw, pe_k, w1_k, w2_k, pe_v, w1_v, w2_v):
    B, S = q.shape[:2]
    kc = _compress_from_feats(*_chunk_feats(kvc[:, :, 0], pe_k, w1_k), w2_k)
    vc = _compress_from_feats(*_chunk_feats(kvc[:, :, 1], pe_v, w1_v), w2_v)
    n_slc = S // SLC_BLK
    kv_blocks = kvs.reshape(B, n_slc, SLC_BLK, 2, G_A, HEAD_DIM)
    kvw_pad = jnp.pad(kvw, ((0, 0), (WIN_PAD, 0), (0, 0), (0, 0), (0, 0)))
    bi = jnp.arange(B)[:, None, None, None]
    gi = jnp.arange(G_A)[None, None, :, None]

    def block(b):
        start = b * Q_BLK
        t = start + jnp.arange(Q_BLK)

        def select(idx, ok):
            rows = kv_blocks[bi, idx, :, :, gi]
            pos = idx[..., None] * SLC_BLK + jnp.arange(SLC_BLK)
            m = ok[..., None] & (pos <= t[None, :, None, None, None])
            shp = (B, Q_BLK, G_A, idx.shape[-1] * SLC_BLK)
            return (rows[..., 0, :].reshape(shp + (HEAD_DIM,)), rows[..., 1, :].reshape(shp + (HEAD_DIM,)),
                    m.reshape(shp))

        kvw_b = lax.dynamic_slice_in_dim(kvw_pad, start, Q_BLK + WIN_PAD, axis=1)
        sw = start - WIN_PAD + jnp.arange(Q_BLK + WIN_PAD)
        return _nsa_mix(lax.dynamic_slice_in_dim(q, start, Q_BLK, axis=1),
                        lax.dynamic_slice_in_dim(gl, start, Q_BLK, axis=1),
                        t, kc, vc, n_slc, select, kvw_b[:, :, 0], kvw_b[:, :, 1], sw)

    o = lax.map(block, jnp.arange(S // Q_BLK))
    return jnp.moveaxis(o, 0, 1).reshape(B, S, H_A, HEAD_DIM)

def _nsa_sample(q, gl, kvc_new, kvs_new, kvw_new, cache_cmp, cache_slc, state_win, page_table,
                pe_k, w1_k, w2_k, pe_v, w1_v, w2_v):
    DB, T = q.shape[:2]
    t = PAST_LEN + jnp.arange(T)
    past_cmp = cache_cmp[page_table].reshape(DB, PAST_LEN, 2, G_A, HEAD_DIM)
    n_new_chunks = T // CMP_STRIDE

    def compressed(c, pe, w1, w2):
        head, tail = _chunk_feats(past_cmp[:, :, c], pe, w1)
        if n_new_chunks > 0:
            hn, tn = _chunk_feats(kvc_new[:, :n_new_chunks * CMP_STRIDE, c], pe, w1)
            head = jnp.concatenate([head, hn], axis=1)
            tail = jnp.concatenate([tail, tn], axis=1)
        return _compress_from_feats(head, tail, w2)

    kc = compressed(0, pe_k, w1_k, w2_k)
    vc = compressed(1, pe_v, w1_v, w2_v)
    n_past_blk = PAST_LEN // SLC_BLK
    n_slc = -(-(PAST_LEN + T) // SLC_BLK)
    bpp = PAGE_SIZE // SLC_BLK
    pool = cache_slc.reshape(cache_slc.shape[0], bpp, SLC_BLK, 2, G_A, HEAD_DIM)
    bi = jnp.arange(DB)[:, None, None, None]
    gi = jnp.arange(G_A)[None, None, :, None]
    blk_new = t // SLC_BLK
    k_new = jnp.broadcast_to(jnp.swapaxes(kvs_new[:, :, 0], 1, 2)[:, None], (DB, T, G_A, T, HEAD_DIM))
    v_new = jnp.broadcast_to(jnp.swapaxes(kvs_new[:, :, 1], 1, 2)[:, None], (DB, T, G_A, T, HEAD_DIM))

    def select(idx, ok):
        jp = jnp.minimum(idx, n_past_blk - 1)
        page = page_table[bi, jp // bpp]
        rows = pool[page, jp % bpp, :, :, gi]
        shp = (DB, T, G_A, idx.shape[-1] * SLC_BLK)
        past_ok = jnp.broadcast_to((ok & (idx < n_past_blk))[..., None], idx.shape + (SLC_BLK,)).reshape(shp)
        sel_new = jnp.any((idx[..., None] == blk_new) & ok[..., None], axis=-2)
        new_ok = sel_new & (t[None, None, None, :] <= t[None, :, None, None])
        ks = jnp.concatenate([rows[..., 0, :].reshape(shp + (HEAD_DIM,)), k_new], axis=3)
        vs = jnp.concatenate([rows[..., 1, :].reshape(shp + (HEAD_DIM,)), v_new], axis=3)
        return ks, vs, jnp.concatenate([past_ok, new_ok], axis=3)

    kvw = jnp.concatenate([state_win, kvw_new], axis=1)
    sw = PAST_LEN - state_win.shape[1] + jnp.arange(kvw.shape[1])
    return _nsa_mix(q, gl, t, kc, vc, n_slc, select, kvw[:, :, 0], kvw[:, :, 1], sw)

def _merge_dilations(outs, lses):
    w = jax.nn.softmax(jnp.stack(lses, axis=0), axis=0)
    return jnp.einsum('ibsh,ibshe->bshe', w, jnp.stack(outs, axis=0).astype(jnp.float32))

def _dil_branch_prompt(q, kv, w, d):
    B, S, H, E = q.shape
    L = S // d
    nb = -(-L // Q_BLK)
    Lp = nb * Q_BLK
    span = w // d

    def classes(x, left):
        xc = x.reshape(B, L, d, H, E).transpose(0, 2, 1, 3, 4)
        return jnp.pad(xc, ((0, 0), (0, 0), (left, Lp - L), (0, 0), (0, 0)))

    def band(x):
        xb = classes(x, Q_BLK).reshape(B, d, nb + 1, Q_BLK, H, E)
        return jnp.concatenate([xb[:, :, :-1], xb[:, :, 1:]], axis=3)

    qc = classes(q, 0).reshape(B, d, nb, Q_BLK, H, E)
    kb = band(kv[:, :, 0])
    vb = band(kv[:, :, 1])
    s = jnp.einsum('bcnqhe,bcnkhe->bcnhqk', qc, kb) * SCALE
    ki = jnp.arange(2 * Q_BLK)[None, :]
    rel = jnp.arange(Q_BLK)[:, None] + Q_BLK - ki
    mask = (rel >= 0) & (rel <= span) & ((jnp.arange(nb)[:, None, None] > 0) | (ki >= Q_BLK))
    p, lse = _masked_softmax(s, mask[:, None])
    o = jnp.einsum('bcnhqk,bcnkhe->bcnqhe', p.astype(vb.dtype), vb)
    o = o.reshape(B, d, Lp, H, E)[:, :, :L].transpose(0, 2, 1, 3, 4).reshape(B, S, H, E)
    lse = lse.transpose(0, 1, 2, 4, 3).reshape(B, d, Lp, H)[:, :, :L].transpose(0, 2, 1, 3).reshape(B, S, H)
    return o, lse

def _dil_prompt(q, kv):
    res = [_dil_branch_prompt(q, kv, w, d) for (w, d) in DIL_PAIRS]
    return _merge_dilations([r[0] for r in res], [r[1] for r in res])

def _dil_sample(q, kv_all):
    DB, T = q.shape[:2]
    Lk = kv_all.shape[1]
    base = PAST_LEN + T - Lk
    t = PAST_LEN + jnp.arange(T)
    outs, lses = [], []
    for w, d in DIL_PAIRS:
        key_pos = t[:, None] - (jnp.arange(w // d + 1) * d)[None, :]
        g = kv_all[:, jnp.clip(key_pos - base, 0, Lk - 1)]
        s = jnp.einsum('bthe,btnhe->bhtn', q, g[:, :, :, 0]) * SCALE
        p, lse = _masked_softmax(s, key_pos >= base)
        outs.append(jnp.einsum('bhtn,btnhe->bthe', p.astype(g.dtype), g[:, :, :, 1]))
        lses.append(jnp.swapaxes(lse, 1, 2))
    return _merge_dilations(outs, lses)

def _finish(x, o_a, o_b, conv_prev, w_o, g_ffn, w_gate, w_up, conv_w, conv_b, w_down):
    B, S = x.shape[:2]
    o = jnp.concatenate([o_a.reshape(B, S, -1), o_b.reshape(B, S, -1)], axis=-1).astype(x.dtype)
    x = x + o @ w_o
    h = _rms_norm(x, g_ffn)
    a = h @ w_gate
    ext = jnp.concatenate([conv_prev.astype(a.dtype), a], axis=1)
    c = conv_b
    for k in range(CONV_W):
        c = c + conv_w[k] * ext[:, k:k + S]
    y = x + (jax.nn.silu(c) * (h @ w_up)) @ w_down
    return y, ext[:, S:]

def setup_inputs(seed: int = 0) -> dict:
    key = jax.random.key(seed)
    ks = jax.random.split(key, 32)
    f32 = jnp.float32
    n_pages = PAST_LEN // PAGE_SIZE
    n_pool = (5 * DEC_BATCH * n_pages + 3) // 4
    nrm = lambda k, shape, scale: scale * jax.random.normal(k, shape, f32)
    gain = lambda k, n: 1.0 + 0.01 * jax.random.normal(k, (n,), f32)
    page_table = jax.random.permutation(ks[7], n_pool)[:DEC_BATCH * n_pages].reshape(DEC_BATCH, n_pages).astype(jnp.int32)
    return {
        'x_prompt': nrm(ks[0], (BATCH, SEQ, D_MODEL), 1.0),
        'x_sample': nrm(ks[1], (DEC_BATCH, DEC_SEQ, D_MODEL), 1.0),
        'cache_cmp': nrm(ks[2], (n_pool, PAGE_SIZE, 2, G_A, HEAD_DIM), 1.0),
        'cache_slc': nrm(ks[3], (n_pool, PAGE_SIZE, 2, G_A, HEAD_DIM), 1.0),
        'state_win': nrm(ks[4], (DEC_BATCH, min(WIN_A, PAST_LEN), 2, G_A, HEAD_DIM), 1.0),
        'state_dil': nrm(ks[5], (DEC_BATCH, min(DIL_MAX, PAST_LEN), 2, H_B, HEAD_DIM), 1.0),
        'state_conv': nrm(ks[6], (DEC_BATCH, CONV_W - 1, D_FF), 1.0),
        'page_table': page_table,
        'g_attn': gain(ks[8], D_MODEL),
        'w_in': nrm(ks[9], (D_MODEL, IN_DIM), D_MODEL ** -0.5),
        'gq_a': gain(ks[10], HEAD_DIM),
        'gk_cmp': gain(ks[11], HEAD_DIM),
        'gk_slc': gain(ks[12], HEAD_DIM),
        'gk_win': gain(ks[13], HEAD_DIM),
        'gq_b': gain(ks[14], HEAD_DIM),
        'gk_b': gain(ks[15], HEAD_DIM),
        'pe_cmp_k': nrm(ks[16], (CMP_LEN, HEAD_DIM), 0.1),
        'w1_cmp_k': nrm(ks[17], (CMP_LEN * HEAD_DIM, CMP_HID), (CMP_LEN * HEAD_DIM) ** -0.5),
        'w2_cmp_k': nrm(ks[18], (CMP_HID, HEAD_DIM), CMP_HID ** -0.5),
        'pe_cmp_v': nrm(ks[19], (CMP_LEN, HEAD_DIM), 0.1),
        'w1_cmp_v': nrm(ks[20], (CMP_LEN * HEAD_DIM, CMP_HID), (CMP_LEN * HEAD_DIM) ** -0.5),
        'w2_cmp_v': nrm(ks[21], (CMP_HID, HEAD_DIM), CMP_HID ** -0.5),
        'w_o': nrm(ks[22], (MIX_WIDTH, D_MODEL), MIX_WIDTH ** -0.5),
        'g_ffn': gain(ks[23], D_MODEL),
        'w_gate': nrm(ks[24], (D_MODEL, D_FF), D_MODEL ** -0.5),
        'w_up': nrm(ks[25], (D_MODEL, D_FF), D_MODEL ** -0.5),
        'conv_w': nrm(ks[26], (CONV_W, D_FF), CONV_W ** -0.5),
        'conv_b': nrm(ks[27], (D_FF,), 0.01),
        'w_down': nrm(ks[28], (D_FF, D_MODEL), D_FF ** -0.5),
    }

def reference(x_prompt, x_sample, cache_cmp, cache_slc, state_win, state_dil, state_conv, page_table,
              g_attn, w_in, gq_a, gk_cmp, gk_slc, gk_win, gq_b, gk_b,
              pe_cmp_k, w1_cmp_k, w2_cmp_k, pe_cmp_v, w1_cmp_v, w2_cmp_v,
              w_o, g_ffn, w_gate, w_up, conv_w, conv_b, w_down):
    proj = (g_attn, w_in, gq_a, gk_cmp, gk_slc, gk_win, gq_b, gk_b)
    phi = (pe_cmp_k, w1_cmp_k, w2_cmp_k, pe_cmp_v, w1_cmp_v, w2_cmp_v)
    ffn = (w_o, g_ffn, w_gate, w_up, conv_w, conv_b, w_down)
    B, S = x_prompt.shape[:2]
    qa, kvc, kvs, kvw, gl, qb, kvb = _project(x_prompt, jnp.arange(S), *proj)
    o_a = _nsa_prompt(qa, gl, kvc, kvs, kvw, *phi)
    o_b = _dil_prompt(qb, kvb)
    y_prompt, conv_p = _finish(x_prompt, o_a, o_b, jnp.zeros((B, CONV_W - 1, D_FF), x_prompt.dtype), *ffn)
    T = x_sample.shape[1]
    qa_s, kvc_s, kvs_s, kvw_s, gl_s, qb_s, kvb_s = _project(x_sample, PAST_LEN + jnp.arange(T), *proj)
    o_a_s = _nsa_sample(qa_s, gl_s, kvc_s, kvs_s, kvw_s, cache_cmp, cache_slc, state_win, page_table, *phi)
    dil_all = jnp.concatenate([state_dil, kvb_s], axis=1)
    o_b_s = _dil_sample(qb_s, dil_all)
    y_sample, conv_s = _finish(x_sample, o_a_s, o_b_s, state_conv, *ffn)
    win_all = jnp.concatenate([state_win, kvw_s], axis=1)
    L_new = PAST_LEN + T
    return (y_prompt, y_sample, kvc, kvc_s, kvs, kvs_s,
            kvw[:, -min(WIN_A, S):], win_all[:, -min(WIN_A, L_new):],
            kvb[:, -min(DIL_MAX, S):], dil_all[:, -min(DIL_MAX, L_new):],
            conv_p, conv_s)


_drawn_inputs = setup_inputs


def setup_inputs(seed=0):
    import zlib

    import numpy as np

    out = dict(_drawn_inputs(seed))
    spreads = {}
    factors = {'g_attn': 5.846,
     'gq_a': 8.0,
     'gk_cmp': 7.811,
     'gk_slc': 8.0,
     'gk_win': 7.911,
     'gq_b': 8.0,
     'gk_b': 8.0,
     'pe_cmp_k': 8.0,
     'g_ffn': 5.682,
     'conv_b': 8.0}
    for name, (base, spread) in spreads.items():
        noise = np.random.default_rng([zlib.crc32(name.encode()), seed]).standard_normal(out[name].shape)
        drawn = base * np.exp(spread * noise) if base else spread * noise
        out[name] = __import__('jax').numpy.asarray(drawn.astype(out[name].dtype))
    for name, factor in factors.items():
        out[name] = (out[name] * factor).astype(out[name].dtype)
    return out
```

```python
from contextlib import ExitStack

import numpy as np

import concourse.bass as bass
from concourse import mybir

F32 = mybir.dt.float32
F32R = mybir.dt.float32r
I32 = mybir.dt.int32
ALU = mybir.AluOpType
ACT = mybir.ActivationFunctionType
AX = mybir.AxisListType.X

P = 128
D = 1024
SEQ = 1024
DB = 8
DT = 8
PAST = 1024
NS = DB * DT
E = 64
HA = 8
HB = 8
GA = 2
RA = HA // GA
ROT = 16
EPS = 1e-6
DFF = 2816
IN_DIM = 2840
PAGE = 128
PAGES = PAST // PAGE
WIN = 512
CMP_STRIDE = 16
CMP_LEN = 32
SLC_BLK = 64
NCMP = PAST // CMP_STRIDE - 1
KC = D // P
TILES = SEQ // P
TOK = SEQ + NS
BIG = 1.0e30
CLAMP = 1.0e20
TINY = 1.0e-30


class Chain:

    def __init__(self, eng, sem):
        self.eng, self.sem, self.n, self.i, self.per = eng, sem, 0, None, 0

    def value(self):
        return self.n if self.i is None else self.i * self.per + self.n

    def step(self, ins):
        self.n += 1
        ins.then_inc(self.sem, 1)
        self.eng.wait_ge(self.sem, self.value())

    def enter(self, i, per):
        self.i, self.per, self.start = i, per, self.n

    def leave(self, trips):
        assert self.n - self.start == self.per, (self.n - self.start, self.per)
        self.n = self.start + trips * self.per
        self.i = None


GROUPS = [
    ("qa", 0, 512, (2, 4), (0, 1)),
    ("cmp_slc", 512, 512, (2, 2), (1, 3)),
    ("win_gate", 1024, 280, (1, 2), (3, 4)),
    ("qb", 1304, 512, (2, 4), (4, 5)),
    ("kb", 1816, 512, (2, 4), (5, 6)),
    ("vb", 2328, 512, None, None),
]
NG = len(GROUPS)
STEPS = TILES + 1


def project(nc, t, o, scratch):
    with ExitStack() as ctx:
        sb = lambda name, shape, dt=F32: ctx.enter_context(nc.sbuf_tensor(name, shape, dt))
        ps = lambda name, shape: ctx.enter_context(nc.psum_tensor(name, shape, F32))
        sem = lambda name: ctx.enter_context(nc.semaphore(name))

        ident = sb("p_ident", [P, P])
        xin = sb("p_x", [P, 2, D])
        xsq = sb("p_xsq", [P, D])
        xss = sb("p_xss", [P, 2])
        xrt = sb("p_xrt", [P, 2])
        xrr = sb("p_xrr", [P, 2])
        xnT = sb("p_xnT", [P, KC, TOK])
        g_in = sb("p_gin", [P, KC])
        gains = sb("p_gains", [P, 6, E])
        rope = sb("p_rope", [P, STEPS, 2 * ROT])
        epst = sb("p_eps", [P, 1])
        raw = sb("p_raw", [P, KC, 512])
        w_hi = sb("p_whi", [P, 2, KC, 512], F32R)
        w_lo = sb("p_wlo", [P, 2, KC, 512], F32R)
        x_hi = sb("p_xhi", [P, 2, KC, P], F32R)
        x_lo = sb("p_xlo", [P, 2, KC, P], F32R)
        z = sb("p_z", [P, 2, 512])
        zsq = sb("p_zsq", [P, 2, 512])
        zss = sb("p_zss", [P, 2, 8])
        zrt = sb("p_zrt", [P, 2, 8])
        zrr = sb("p_zrr", [P, 2, 8])
        ra = sb("p_ra", [P, 8 * ROT])
        rb = sb("p_rb", [P, 8 * ROT])
        pt = [ps(f"p_pt{k}", [P, D]) for k in range(2)]
        pz = [ps(f"p_pz{k}", [P, 512]) for k in range(2)]

        const_in = sem("p_const_in")
        x_in = [sem(f"p_x_in{k}") for k in range(2)]
        x_square = sem("p_x_square")
        x_root = sem("p_x_root")
        x_normed = sem("p_x_normed")
        x_turned = sem("p_x_turned")
        x_stored = sem("p_x_stored")
        eps_set = sem("p_eps_set")
        raw_in = sem("p_raw_in")
        w_hi_done = sem("p_w_hi_done")
        w_lo_done = sem("p_w_lo_done")
        x_hi_done = sem("p_x_hi_done")
        x_lo_done = sem("p_x_lo_done")
        z_summed = sem("p_z_summed")
        z_copied = sem("p_z_copied")
        z_squared = sem("p_z_squared")
        z_reduced = sem("p_z_reduced")
        z_root = sem("p_z_root")
        z_done = sem("p_z_done")
        z_out = [sem(f"p_z_out{k}") for k in range(2)]
        vchain = sem("p_vchain")

        SAMPLE = TILES // 2

        def rows(i):
            return NS if isinstance(i, int) and i == SAMPLE else P

        def tokens(i, k):
            if isinstance(i, int):
                return slice((2 * i + k) * P, (2 * i + k) * P + rows(i))
            return bass.ds(i * (2 * P) + k * P, P)

        def loop_tiles(eng, body, chain=None, per=0):
            with eng.Fori(0, 3) as i:
                if chain:
                    chain.enter(i, per)
                body(i, 0)
                body(i, 1)
            if chain:
                chain.leave(3)
            body(3, 0)
            body(3, 1)
            body(SAMPLE, 0)

        def normed(G, i, k):
            return sum(g[3] is not None for g in GROUPS[:G]) * STEPS + i * 2 + k + 1

        def stores(G):
            return 1 if GROUPS[G][3] is not None and GROUPS[G][0] in ("qa", "qb", "kb") or GROUPS[G][0] == "vb" else 2

        def stored_before(G, i, k):
            slot = (G + k) % 2
            before = sum(16 * stores(g) * (5 if (slot - g) % 2 == 0 else 4) for g in range(G))
            return i * (16 * stores(G)) + (before + 1)

        block = ctx.enter_context(nc.Block())

        @block.sync
        def _(sp):
            sp.sem_inc(z_out[0], 1)
            sp.sem_inc(z_out[1], 1)
            sp.dma_start(ident[:], t["ident"]).then_inc(const_in, 16)
            sp.dma_start(g_in[:], t["g_attn"]).then_inc(const_in, 16)
            sp.dma_start(gains[:], t["gains"]).then_inc(const_in, 16)
            sp.dma_start(rope[:, 0:TILES, :], t["rope"][0:SEQ, :].rearrange("(a p) c -> p a c", p=P)).then_inc(const_in, 16)
            sp.dma_start(rope[0:NS, TILES, :], t["rope"][SEQ:TOK, :]).then_inc(const_in, 16)
            for n in range(STEPS):
                r = P if n < TILES else NS
                src = t["x_prompt"][0, n * P:(n + 1) * P, :] if n < TILES else t["x_sample"].rearrange("b t d -> (b t) d")
                if n >= 2:
                    sp.wait_ge(x_turned, n - 1)
                sp.dma_start(xin[0:r, n % 2, :], src).then_inc(x_in[n % 2], 16)
                if n == 1:
                    sp.dma_start(raw[:], t["w_in"][:, 0:512].rearrange("(c p) n -> p c n", p=P)).then_inc(raw_in, 16)
            for G, (name, c0, wd, heads, _) in enumerate(GROUPS):
                if G + 1 < NG:
                    sp.wait_ge(w_lo_done, KC * (G + 1))
                    c1, w1 = GROUPS[G + 1][1:3]
                    sp.dma_start(raw[:, :, 0:w1], t["w_in"][:, c1:c1 + w1].rearrange("(c p) n -> p c n", p=P)).then_inc(raw_in, 16)

                def store_tile(i, k, G=G, name=name, heads=heads):
                    slot = (G + k) % 2
                    r = rows(i)
                    last = r == NS
                    if heads is not None:
                        sp.wait_ge(z_done, normed(G, i, k))
                    else:
                        sp.wait_ge(z_copied, i * 2 + (k + G * STEPS + 3))
                    tok = slice(0, NS) if last else tokens(i, k)
                    src = z[0:r, slot, :]
                    if name in ("qa", "qb"):
                        sp.dma_start(scratch[name][tokens(i, k), :], src).then_inc(z_out[slot], 16)
                    elif name == "win_gate":
                        sp.dma_start(scratch["kvw"][tokens(i, k), :], src[:, 0:256]).then_inc(z_out[slot], 16)
                        sp.dma_start(scratch["gl"][tokens(i, k), :], src[:, 256:280]).then_inc(z_out[slot], 16)
                    elif name == "cmp_slc":
                        for j, x in enumerate(("cmp", "slc")):
                            dst = o[x + ("_sample" if last else "_prompt")].rearrange("b s c g e -> (b s) (c g e)")
                            sp.dma_start(dst[tok, :], src[:, 256 * j:256 * j + 256]).then_inc(z_out[slot], 16)
                    else:
                        c = 0 if name == "kb" else 1
                        if last:
                            sp.dma_start(o["dil_sample"][:, PAST:PAST + DT, c, :, :].rearrange("b s h e -> b s (h e)"),
                                         src).then_inc(z_out[slot], 16)
                        else:
                            sp.dma_start(o["dil_prompt"][0, tok, c, :, :].rearrange("s h e -> s (h e)"), src).then_inc(z_out[slot], 16)

                loop_tiles(sp, store_tile)
            for k in range(2):
                sp.wait_ge(z_out[k], 1 + sum(16 * stores(g) * (5 if (k - g) % 2 == 0 else 4) for g in range(NG)))

        @block.gpsimd
        def _(pool):
            nc.gpsimd.memset(epst[:], EPS).then_inc(eps_set, 1)

        @block.scalar
        def _(act):
            act.sem_inc(z_copied, 2)
            act.wait_ge(eps_set, 1)
            for n in range(STEPS):
                r, s = (P if n < TILES else NS), slice(n % 2, n % 2 + 1)
                act.wait_ge(x_in[n % 2], 16 * (n // 2 + 1))
                if n >= 2:
                    act.wait_ge(x_normed, n - 1)
                if n >= 1:
                    act.wait_ge(x_square, n)
                nc.scalar.activation(xsq[0:r, :], xin[0:r, n % 2, :], ACT.Square, accum_out=xss[0:r, s]).then_inc(x_square, 1)
                act.wait_ge(x_square, n + 1)
                nc.scalar.activation(xrt[0:r, s], xss[0:r, s], ACT.Sqrt, bias=epst[0:r, :], scale=1.0 / D).then_inc(x_root, 1)
            act.wait_ge(raw_in, 16)
            for c in range(KC):
                nc.scalar.activation(w_hi[:, 0, c, :], raw[:, c, :], ACT.Copy).then_inc(w_hi_done, 1)

            def split_x(slot, i, k):
                r = rows(i)
                nc.scalar.activation(x_hi[:, slot, :, 0:r], xnT[:, :, tokens(i, k)], ACT.Copy).then_inc(x_hi_done, 1)

            act.wait_ge(x_stored, STEPS)
            split_x(0, 0, 0)
            split_x(1, 0, 1)
            for G, (name, c0, wd, heads, _) in enumerate(GROUPS):
                def tile(i, k, G=G, heads=heads, wd=wd):
                    slot = (G + k) % 2
                    r = rows(i)
                    act.wait_ge(z_summed, i * 2 + (k + G * STEPS + 1))
                    act.wait_ge(z_out[slot], stored_before(G, i, k))
                    nc.scalar.activation(z[0:r, slot, 0:wd], pz[slot][0:r, 0:wd], ACT.Copy).then_inc(z_copied, 1)
                    if r == NS:
                        i2, k2, more = 0, 1, G + 1 < NG
                    elif isinstance(i, int) and k == 1:
                        i2, k2, more = 0, 0, G + 1 < NG
                    else:
                        i2, k2, more = i + 1, k, True
                    if more:
                        split_x(slot, i2, k2)
                    if heads is not None:
                        a, h = heads
                        act.wait_ge(z_copied, i * 2 + (k + G * STEPS + 3))
                        nc.scalar.activation(zsq[0:r, slot, 0:a * h * E].rearrange("p (a h e) -> p a h e", h=h, e=E),
                                             z[0:r, slot, 0:a * 256].rearrange("p (a h e) -> p a h e", h=4, e=E)[:, :, 0:h, :],
                                             ACT.Square).then_inc(z_squared, 1)
                    if G + 1 < NG and r == P:
                        w = GROUPS[G + 1][2]
                        if k == 0:
                            act.wait_ge(raw_in, 16 * (G + 2))
                        cs = bass.ds(i * 2 + k, 1)
                        nc.scalar.activation(w_hi[:, (G + 1) % 2, cs, 0:w], raw[:, cs, 0:w], ACT.Copy).then_inc(w_hi_done, 1)
                    if heads is not None:
                        a, h = heads
                        act.wait_ge(z_reduced, normed(G, i, k))
                        nc.scalar.activation(zrt[0:r, slot, 0:a * h], zss[0:r, slot, 0:a * h], ACT.Sqrt,
                                             bias=epst[0:r, :], scale=1.0 / E).then_inc(z_root, 1)

                loop_tiles(act, tile)

        @block.tensor
        def _(pe):
            pe.wait_ge(const_in, 80)
            for n in range(STEPS):
                r = P if n < TILES else NS
                pe.wait_ge(x_normed, n + 1)
                if n >= 2:
                    pe.wait_ge(x_stored, n - 1)
                for c in range(KC):
                    last = nc.tensor.transpose(pt[n % 2][:, c * P:c * P + r], xin[0:r, n % 2, c * P:(c + 1) * P], ident[0:r, 0:r])
                last.then_inc(x_turned, 1)
            for G, (name, c0, wd, heads, _) in enumerate(GROUPS):
                pe.wait_ge(w_lo_done, KC * (G + 1))

                def tile(i, k, G=G, wd=wd):
                    slot = (G + k) % 2
                    r = rows(i)
                    pe.wait_ge(x_lo_done, i * 2 + (k + G * STEPS + 1))
                    pe.wait_ge(z_copied, i * 2 + (k + G * STEPS + 1))
                    for j, (xs, ws) in enumerate(((x_hi, w_hi), (x_hi, w_lo), (x_lo, w_hi))):
                        for c in range(KC):
                            last = nc.tensor.matmul(pz[slot][0:r, 0:wd], xs[:, slot, c, 0:r], ws[:, G % 2, c, 0:wd],
                                                    start=(j == 0 and c == 0), stop=(j == 2 and c == KC - 1))
                    last.then_inc(z_summed, 1)

                loop_tiles(pe, tile)

        @block.vector
        def _(dve):
            chain = Chain(dve, vchain)
            dve.wait_ge(const_in, 80)
            for g in (0, 4):
                chain.step(nc.vector.tensor_scalar(gains[:, g, :], gains[:, g, :], -(E ** -0.5), None, ALU.mult))
            for n in range(STEPS):
                r, s = (P if n < TILES else NS), slice(n % 2, n % 2 + 1)
                dve.wait_ge(x_root, n + 1)
                chain.step(nc.vector.reciprocal(xrr[0:r, s], xrt[0:r, s]))
                nc.vector.tensor_scalar(xin[0:r, n % 2, :], xin[0:r, n % 2, :], xrr[0:r, s], None, ALU.mult).then_inc(x_normed, 1)
                dve.wait_ge(x_turned, n + 1)
                nc.vector.tensor_tensor(xnT[:, :, n * P:n * P + r], pt[n % 2][:, :].rearrange("p (c q) -> p c q", c=KC)[:, :, 0:r],
                                        g_in[:, :].unsqueeze(2).to_broadcast([P, KC, r]), ALU.mult).then_inc(x_stored, 1)
            for c in range(KC):
                dve.wait_ge(w_hi_done, c + 1)
                nc.vector.tensor_tensor(w_lo[:, 0, c, :], raw[:, c, :], w_hi[:, 0, c, :].bitcast(F32), ALU.subtract).then_inc(w_lo_done, 1)

            def split_x(slot, i, k, n):
                r = rows(i)
                dve.wait_ge(x_hi_done, n)
                nc.vector.tensor_tensor(x_lo[:, slot, :, 0:r], xnT[:, :, tokens(i, k)], x_hi[:, slot, :, 0:r].bitcast(F32),
                                        ALU.subtract).then_inc(x_lo_done, 1)

            dve.wait_ge(x_stored, STEPS)
            split_x(0, 0, 0, 1)
            split_x(1, 0, 1, 2)
            for G, (name, c0, wd, heads, grow) in enumerate(GROUPS):
                def tile(i, k, G=G, heads=heads, wd=wd, grow=grow):
                    slot = (G + k) % 2
                    r = rows(i)
                    if r == NS:
                        i2, k2, more = 0, 1, G + 1 < NG
                    elif isinstance(i, int) and k == 1:
                        i2, k2, more = 0, 0, G + 1 < NG
                    else:
                        i2, k2, more = i + 1, k, True
                    if more:
                        split_x(slot, i2, k2, i * 2 + (k + G * STEPS + 3))
                    if heads is not None:
                        a, h = heads
                        zs3 = zss[0:r, slot, 0:a * h]
                        dve.wait_ge(z_squared, normed(G, i, k))
                        nc.vector.reduce_sum(zs3, zsq[0:r, slot, 0:a * h * E].rearrange("p (h e) -> p h e", e=E), AX).then_inc(z_reduced, 1)
                    if G + 1 < NG and r == P:
                        w = GROUPS[G + 1][2]
                        cs = bass.ds(i * 2 + k, 1)
                        dve.wait_ge(w_hi_done, i * 2 + (k + KC * (G + 1) + 1))
                        nc.vector.tensor_tensor(w_lo[:, (G + 1) % 2, cs, 0:w], raw[:, cs, 0:w], w_hi[:, (G + 1) % 2, cs, 0:w].bitcast(F32),
                                                ALU.subtract).then_inc(w_lo_done, 1)
                    if heads is not None:
                        zv = z[0:r, slot, 0:a * 256].rearrange("p (a h e) -> p a h e", h=4, e=E)[:, :, 0:h, :]
                        dve.wait_ge(z_root, normed(G, i, k))
                        chain.step(nc.vector.reciprocal(zrr[0:r, slot, 0:a * h], zrt[0:r, slot, 0:a * h]))
                        rr = zrr[0:r, slot, 0:a * h].rearrange("p (a h) -> p a h", a=a).unsqueeze(3)
                        chain.step(nc.vector.tensor_tensor(zv, zv, rr.to_broadcast([r, a, h, E]), ALU.mult))
                        gv = gains[0:r, grow[0]:grow[1], :].unsqueeze(2)
                        if grow[1] - grow[0] == 1 and a == 2:
                            for b in range(2):
                                ins = nc.vector.tensor_tensor(zv[:, b], zv[:, b], gv[:, 0].to_broadcast([r, h, E]), ALU.mult)
                                if b == 1:
                                    chain.step(ins)
                        else:
                            chain.step(nc.vector.tensor_tensor(zv, zv, gv.to_broadcast([r, a, h, E]), ALU.mult))
                        tile_at = (2 * i + k) if isinstance(i, int) else None
                        ct = rope[0:r, tile_at if tile_at is not None else bass.ds(i * 2 + k, 1), :]
                        if tile_at is None:
                            ct = ct.rearrange("p a c -> p (a c)")
                        bc = lambda x, w: x.unsqueeze(1).to_broadcast([r, h, w])
                        n_ops = []
                        for b in range(a):
                            v = zv[:, b]
                            va = ra[0:r, b * 4 * ROT:b * 4 * ROT + h * ROT].rearrange("p (h c) -> p h c", c=ROT)
                            vb = rb[0:r, b * 4 * ROT:b * 4 * ROT + h * ROT].rearrange("p (h c) -> p h c", c=ROT)
                            nc.vector.tensor_tensor(va, v[:, :, 0:ROT], bc(ct[:, 0:ROT], ROT), ALU.mult)
                            nc.vector.tensor_tensor(vb[:, :, 0:8], v[:, :, 8:16], bc(ct[:, 16:24], 8), ALU.mult)
                            ins = nc.vector.tensor_tensor(vb[:, :, 8:16], v[:, :, 0:8], bc(ct[:, 24:32], 8), ALU.mult)
                            if b == a - 1:
                                chain.step(ins)
                            n_ops.append((v, va, vb))
                        for b, (v, va, vb) in enumerate(n_ops):
                            ins = nc.vector.tensor_tensor(v[:, :, 0:ROT], va, vb, ALU.add)
                            if b == a - 1:
                                ins.then_inc(z_done, 1)

                loop_tiles(dve, tile, chain, per=8 if heads is not None else 0)

def dil_bias(delta):
    mult = sum(((delta >= 0) & (delta <= w) & (delta % d == 0)).astype(np.float64) for w, d in ((128, 1), (512, 4), (2048, 16)))
    return np.where(mult > 0, -np.log(np.maximum(mult, 1.0)), BIG).astype(np.float32)


def tables():
    p = np.arange(P)[:, None]
    c = np.arange(SEQ)[None, :]
    d = p + (SEQ - P) - c
    m_dil = dil_bias(d)
    m_slc = np.where(d >= 0, 0.0, BIG)
    dw = p + WIN - np.arange(WIN + P)[None, :]
    m_win = np.where((dw >= 0) & (dw < WIN), 0.0, BIG)
    t = (np.arange(TILES)[None, :, None] * P + np.arange(P)[:, None, None])
    n = np.arange(NCMP + 1)[None, None, :]
    m_cmp = np.where((n < NCMP) & (n * CMP_STRIDE + CMP_LEN - 1 <= t), 0.0, BIG).reshape(P, -1)
    masks = np.concatenate([m_dil, m_slc, m_win, m_cmp], 1).astype(np.float32)
    tt = np.tile(np.arange(DT), 8)[:, None]
    col = np.arange(PAST)[None, :]
    key = (col % P) * (PAST // P) + col // P
    s_dil = dil_bias(PAST + tt - np.concatenate([key, PAST + np.arange(DT)[None, :]], 1))
    wc = np.arange(WIN)[None, :]
    widx = np.concatenate([(wc % P) * (WIN // P) + wc // P, WIN + np.arange(DT)[None, :]], 1)
    dw = PAST + tt - (PAST - WIN + widx)
    s_win = np.where((dw >= 0) & (dw < WIN), 0.0, BIG)
    s_new = np.where(np.arange(DT)[None, :] <= tt, 0.0, BIG)
    s_zero = np.zeros((NS, NCMP + 1))
    blocks = np.tile(np.arange(PAST // SLC_BLK)[None, :], (NS, 1))
    ci = np.arange(NS)[:, None] * CMP_STRIDE
    sj = np.arange(PAST // SLC_BLK)[None, :] * SLC_BLK
    overlap = ((ci < sj + SLC_BLK) & (ci + CMP_LEN > sj) & (np.arange(NS)[:, None] < NCMP))
    row = np.arange(NS)
    same = (row[:, None] // (RA * DT) == row[None, :] // (RA * DT)) & (row[:, None] % DT == row[None, :] % DT)
    sample = np.concatenate([s_dil, s_win, s_new, s_zero, blocks, overlap, same], 1).astype(np.float32)
    return masks, sample


M_SLC, M_WIN, M_CMP = SEQ, 2 * SEQ, 2 * SEQ + WIN + P
M_ALL = M_CMP + TILES * (NCMP + 1)
S_WIN = PAST + DT
S_NEW = S_WIN + WIN + DT
S_ZERO = S_NEW + DT
S_BLK = S_ZERO + NCMP + 1
S_OVER = S_BLK + PAST // SLC_BLK
S_SAME = S_OVER + PAST // SLC_BLK
S_ALL = S_SAME + NS
NBLK = PAST // SLC_BLK
GELU_C = 0.7978845608028654


def attend(nc, t, o, scratch):
    with ExitStack() as outer:
        osb = lambda name, shape, dt=F32: outer.enter_context(nc.sbuf_tensor(name, shape, dt))
        ident = osb("a_ident", [P, P])
        w1 = osb("a_w1", [P, 2, 16, P])
        w2 = osb("a_w2", [P, 2, E])
        pe_bias = osb("a_pe_bias", [P, 2])
        q_dil_T = osb("a_q_dil_T", [P, 4, NS])
        q_nsa_T = osb("a_q_nsa_T", [P, RA, NS])
        gate_p = osb("a_gate_p", [P, TILES, 3 * HA])
        gate_s = osb("a_gate_s", [NS, DB, 3])
        compress_prompt(nc, t, o, scratch, ident, w1, w2, pe_bias, q_dil_T, q_nsa_T, gate_p, gate_s)
        attend_loop(nc, t, o, scratch, ident, w1, w2, pe_bias, q_dil_T, q_nsa_T, gate_p, gate_s)


def compress_prompt(nc, t, o, scratch, ident, w1, w2, pe_bias, q_dil_T, q_nsa_T, gate_p, gate_s):
    with ExitStack() as ctx:
        sb = lambda name, shape, dt=F32: ctx.enter_context(nc.sbuf_tensor(name, shape, dt))
        sem = lambda name: ctx.enter_context(nc.semaphore(name))
        rows16 = sb("c_rows16", [NS, 4096])
        xT = sb("c_xT", [P, 2, GA, 8, NS])
        peT = sb("c_peT", [P, 2, 16])
        qn = sb("c_qn", [NS, 2, 512])
        h = sb("c_h", [P, 2, GA * NS])
        u = sb("c_u", [P, 2, GA * NS])
        kv = sb("c_kv", [NS, 2, GA, E])
        turned = [ctx.enter_context(nc.psum_tensor(f"c_turned{k}", [P, 512], F32)) for k in range(6)]
        hidden = ctx.enter_context(nc.psum_tensor("c_hidden", [P, 2, GA, NS], F32))
        small = ctx.enter_context(nc.psum_tensor("c_small", [P, 512], F32))
        loaded, rows_in, t_filled, v = sem("c_loaded"), sem("c_rows_in"), sem("c_t_filled"), sem("c_v")
        pe_done, hid_done, tanh_in, tanh_done, kv_done, kv_copied, kv_out, gates_in = (
            sem("c_" + x) for x in ("pe_done", "hid_done", "tanh_in", "tanh_done", "kv_done", "kv_copied", "kv_out", "gates_in"))
        block = ctx.enter_context(nc.Block())

        @block.sync
        def _(sp):
            for c in range(4):
                sp.dma_start(rows16[:, c * 1024:(c + 1) * 1024].rearrange("n (r e) -> n r e", e=E),
                             o["cmp_prompt"].rearrange("b (n r) c g e -> (b n) r (c g) e", r=CMP_STRIDE)[:, :, c, :]).then_inc(rows_in, 16)
            sp.dma_start(ident[:], t["ident"]).then_inc(loaded, 16)
            for c, x in enumerate("kv"):
                sp.dma_start(w1[:, c], t["w1_cmp_" + x].rearrange("(j p) f -> p j f", p=P)).then_inc(loaded, 16)
                sp.dma_start(w2[:, c], t["w2_cmp_" + x]).then_inc(loaded, 16)
            sp.dma_start(peT[:], t["peT"]).then_inc(loaded, 16)
            sp.dma_start(qn[:, 0, :], scratch["qb"][SEQ:TOK, :]).then_inc(loaded, 16)
            for g in range(GA):
                sp.dma_start(qn[:, 1, :].rearrange("p (r g e) -> p r g e", g=GA, e=E)[:, :, g, :],
                             scratch["qa"][SEQ:TOK, g * RA * E:(g + 1) * RA * E].rearrange("p (r e) -> p r e", e=E)).then_inc(loaded, 16)
            sp.dma_start(gate_p[:], scratch["gl"][0:SEQ, :].rearrange("(a p) c -> p a c", p=P)).then_inc(gates_in, 16)
            for b in range(DB):
                sp.dma_start(gate_s[:, b, :], scratch["gl"][SEQ + b * DT:SEQ + (b + 1) * DT, :].rearrange("s (h c) -> h s c", c=3)).then_inc(gates_in, 16)
            sp.wait_ge(kv_copied, 4)
            sp.dma_start(scratch["kvc"], kv[:]).then_inc(kv_out, 16)
            sp.wait_ge(kv_out, 16)

        LOADS = 16 * 9

        @block.tensor
        def _(pe):
            pe.wait_ge(loaded, LOADS)
            for n in range(2):
                for j in range(4):
                    src = qn[:, n, j * P:(j + 1) * P]
                    last = nc.tensor.transpose(turned[4 + n][:, j * NS:(j + 1) * NS], src, ident[0:NS, 0:NS])
                last.then_inc(t_filled, 1)
            pe.wait_ge(rows_in, 64)
            for n in range(4):
                c, g = n // 2, n % 2
                for rp in range(8):
                    src = rows16[:, n * 1024 + rp * P:n * 1024 + (rp + 1) * P]
                    last = nc.tensor.transpose(turned[n][:, rp * NS:(rp + 1) * NS], src, ident[0:NS, 0:NS])
                last.then_inc(t_filled, 1)
            for c in range(2):
                for j in range(16):
                    last = nc.tensor.matmul(small[:, c:c + 1], w1[:, c, j, :], peT[:, c, j:j + 1], start=(j == 0), stop=(j == 15))
            last.then_inc(pe_done, 1)
            pe.wait_ge(v, 6)
            for c in range(2):
                for j in range(16):
                    at = j // 8
                    last = nc.tensor.matmul(hidden[:, c, :, 0:NCMP], w1[:, c, j, :], xT[:, c, :, j % 8, at:at + NCMP],
                                            start=(j == 0), stop=(j == 15))
            last.then_inc(hid_done, 1)
            pe.wait_ge(v, 13)
            for c in range(2):
                for g in range(GA):
                    hg = u[:, c, :].rearrange("p (g n) -> p g n", g=GA)[:, g, 0:NCMP]
                    last = nc.tensor.matmul(small[0:NCMP, 128 + (c * GA + g) * E:128 + (c * GA + g + 1) * E], hg, w2[:, c, :], start=True, stop=True)
            last.then_inc(kv_done, 1)

        @block.scalar
        def _(act):
            act.wait_ge(tanh_in, 1)
            uv = u[:].rearrange("p c (g n) -> p (c g) n", g=GA)[:, :, 0:NCMP]
            nc.scalar.activation(uv, uv, ACT.Tanh, scale=GELU_C).then_inc(tanh_done, 1)
            act.wait_ge(gates_in, 16 * (1 + DB))
            nc.scalar.activation(gate_p[:], gate_p[:], ACT.Exp, scale=-1.0).then_inc(tanh_done, 1)
            nc.scalar.activation(gate_s[:], gate_s[:], ACT.Exp, scale=-1.0).then_inc(tanh_done, 1)

        @block.vector
        def _(dve):
            ch = Chain(dve, v)
            nc.vector.memset(kv[:], 0.0).then_inc(kv_copied, 1)
            dve.wait_ge(t_filled, 2)
            ch.step(nc.vector.tensor_copy(q_dil_T[:].rearrange("p a n -> p (a n)"), turned[4][:, 0:4 * NS]))
            ch.step(nc.vector.tensor_copy(q_nsa_T[:].rearrange("p a n -> p (a n)"), turned[5][:, 0:4 * NS]))
            for n in range(4):
                dve.wait_ge(t_filled, 3 + n)
                ch.step(nc.vector.tensor_copy(xT[:, n // 2, n % 2].rearrange("p a n -> p (a n)"), turned[n][:, :]))
            dve.wait_ge(pe_done, 1)
            ch.step(nc.vector.tensor_copy(pe_bias[:], small[:, 0:2]))
            ch.step(nc.vector.tensor_scalar(w2[:], w2[:], 0.5, None, ALU.mult))
            dve.wait_ge(hid_done, 1)
            hv = [x[:].rearrange("p c (g n) -> p c g n", g=GA)[:, :, :, 0:NCMP] for x in (h, u)]
            for c in range(2):
                ins = nc.vector.tensor_scalar(hv[0][:, c], hidden[:, c, :, 0:NCMP], pe_bias[:, c:c + 1], None, ALU.add)
            ch.step(ins)
            hv = [x.rearrange("p c g n -> p (c g) n") for x in hv]
            ch.step(nc.vector.tensor_tensor(hv[1], hv[0], hv[0], ALU.mult))
            ch.step(nc.vector.tensor_scalar(hv[1], hv[1], 0.044715, 1.0, ALU.mult, ALU.add))
            nc.vector.tensor_tensor(hv[1], hv[1], hv[0], ALU.mult).then_inc(tanh_in, 1)
            dve.wait_ge(tanh_done, 1)
            ch.step(nc.vector.tensor_scalar(hv[1], hv[1], 1.0, None, ALU.add))
            ch.step(nc.vector.tensor_tensor(hv[1], hv[1], hv[0], ALU.mult))
            dve.wait_ge(kv_done, 1)
            dve.wait_ge(kv_copied, 1)
            nc.vector.tensor_copy(kv[0:NCMP].rearrange("p c g e -> p (c g e)"), small[0:NCMP, 128:384]).then_inc(kv_copied, 1)
            dve.wait_ge(tanh_done, 3)
            for x in (gate_p, gate_s):
                ch.step(nc.vector.tensor_scalar(x[:], x[:], 1.0, None, ALU.add))
                nc.vector.reciprocal(x[:], x[:]).then_inc(kv_copied, 1)


UNITS = ([("d", j) for j in range(8)] + [("sd", 0)] + [("l", j) for j in range(8)]
         + [("w", 0), ("w", 1), ("sc", 0)] + [("w", j) for j in range(2, 8)]
         + [("c", 0), ("c", 1), ("sl", 0)] + [("c", j) for j in range(2, 6)] + [("sw", 0), ("c", 6), ("c", 7)])
NU = len(UNITS)
BRANCH = {"d": 0, "l": 1, "w": 2, "c": 3}
EXTRAS = {
    -1: [("prep", 0)],
    0: [("kd", 0)], 1: [("kd", 1)], 2: [("kd", 2)], 3: [("kd", 3), ("new", 0)], 4: [("kd", 4)],
    5: [("kd", 5)], 6: [("kd", 6), ("prep", 1)], 7: [("kd", 7)],
    9: [("ksw", 0)], 10: [("ksw", 1)], 11: [("ksw", 2)],
    12: [("xt", 0)], 13: [("xt", 1)], 14: [("xt", 2), ("prep", 2)], 15: [("xt", 3)], 16: [("hid", 0)], 18: [("ckv", 0)],
    22: [("sel1", 0)], 23: [("sel2", 0)], 24: [("prep", 3)],
}
SPLIT_AT = {-1: 0, 4: 1, 12: 2, 21: 3}
PREP_CHUNKS = {0: 6, 1: 6, 2: 4, 3: 2}


def key_blocks(kind, j):
    if kind in "dl":
        return 0, j + 1
    if kind == "w":
        return max(0, j - WIN // P), j + 1
    return 0, 1


def plan():
    T, S, U = {}, {}, {}
    nt = ns = nu = 0
    for s in range(-1, NU + 3):
        if 0 <= s < NU:
            kind, j = UNITS[s]
            for part in range(2 if kind in ("sd", "sl") else 1):
                S["qk", s, part] = ns
                ns += 1
        if 0 <= s - 2 < NU:
            kind, j = UNITS[s - 2]
            if kind[0] == "s":
                k = 2
            else:
                a, b = key_blocks(kind, j)
                k = -(-(b - a) // 4)
            for q in range(k):
                T["tr", s - 2, q] = nt
                U[s - 2, q] = nu
                nt, nu = nt + 1, nu + 1
        for name, j in EXTRAS.get(s, ()):
            for q in range(PREP_CHUNKS[j] if name == "prep" else 0 if name in ("hid", "ckv", "sel1", "sel2") else 1):
                T[name, j, q] = nt
                nt += 1
            if name in ("hid", "ckv", "sel1", "sel2"):
                S[name, j, 0] = ns
                ns += 1
    assert nt % 2 == 0 and ns % 2 == 0 and nu % 4 == 0 and NU % 4 == 0, (nt, ns, nu)
    return T, S, U, nt, ns


def attend_loop(nc, t, o, scratch, ident, w1, w2, pe_bias, q_dil_T, q_nsa_T, gate_p, gate_s):
    T, S, U, NT, NSC = plan()
    with ExitStack() as ctx:
        sb = lambda name, shape, dt=F32: ctx.enter_context(nc.sbuf_tensor(name, shape, dt))
        sem = lambda name: ctx.enter_context(nc.semaphore(name))
        masks = sb("l_masks", [P, M_ALL])
        smask = sb("l_smask", [NS, S_ALL])
        q_nat = [sb(f"l_q_nat{k}", [P, TILES, E]) for k in range(2)]
        kv_nat = [sb(f"l_kv_nat{k}", [P if k < 3 else NS, TILES if k < 3 else 1, 2, E]) for k in range(4)]
        q_split = sb("l_q_split", [P, TILES, 2 * E], F32R)
        k_split = sb("l_k_split", [P, TILES, 3 * E], F32R)
        qT = [sb(f"l_qT{k}", [P, SEQ], F32R) for k in range(2)]
        kA = [sb(f"l_kA{k}", [P, SEQ], F32R) for k in range(2)]
        kB = [sb(f"l_kB{k}", [P, SEQ], F32R) for k in range(2)]
        e_ring = sb("l_e", [P, 4, PAST + DT])
        e_gated = sb("l_e_gated", [NS, NS])
        p_ring = sb("l_p", [P, 4, 512])
        nmin = sb("l_nmin", [P, 4])
        nmin2 = sb("l_nmin2", [NS, 1])
        total = sb("l_total", [P, 4])
        rtot = sb("l_rtot", [P, 4])
        acc = [sb(f"l_acc{k}", [P, TILES, E]) for k in range(2)]
        gate_h = sb("l_gate_h", [P, TILES, 3])
        gate_b = sb("l_gate_b", [NS, 3])
        kd_k = sb("l_kd_k", [P, 8, 512])
        kd_v = sb("l_kd_v", [P, 8, 512])
        rows16 = kd_k[0:NS].rearrange("p j n -> p (j n)")
        kd_new = sb("l_kd_new", [DT, 1024])
        ks = sb("l_ks", [P, PAGES, 256])
        kw = sb("l_kw", [P, WIN // P, 256])
        ks_new = sb("l_ks_new", [DT, 256])
        kw_new = sb("l_kw_new", [DT, 256])
        kd_T = sb("l_kd_T", [P, 4, PAST])
        ks_T = sb("l_ks_T", [P, PAST])
        kw_T = sb("l_kw_T", [P, WIN])
        new_T = sb("l_new_T", [P, 6, DT])
        xT = sb("l_xT", [P, 2, GA, 8, NS])
        hh = sb("l_hh", [P, 2 * GA, NS])
        hu = sb("l_hu", [P, 2 * GA, NS])
        kc_T = sb("l_kc_T", [P, NCMP])
        vc = sb("l_vc", [NCMP, P])
        bd_dil = sb("l_bd_dil", [P, 4 * 80])
        bd_nsa = sb("l_bd_nsa", [P, NS])
        sel = sb("l_sel", [NS, 3, NBLK])
        selm = sb("l_selm", [NS, 2])
        oa_s = sb("l_oa_s", [P, RA * DT])
        oT_s = sb("l_oT_s", [P, 8, NS])
        pages = sb("l_pages", [1, DB * PAGES], I32)
        s_ps = [ctx.enter_context(nc.psum_tensor(f"l_s{k}", [P, 1024], F32)) for k in range(2)]
        t_ps = [ctx.enter_context(nc.psum_tensor(f"l_t{k}", [P, 512], F32)) for k in range(2)]
        o_ps = [ctx.enter_context(nc.psum_tensor(f"l_o{k}", [P, 512], F32)) for k in range(2)]

        const_in = sem("l_const_in")
        passed = sem("l_passed")
        pages_in, win_out = sem("l_pages_in"), sem("l_win_out")
        q_in = [sem(f"l_q_in{k}") for k in range(2)]
        kv_in = [sem(f"l_kv_in{k}") for k in range(4)]
        kdk_in, kdv_in, new_in, ks_in, kw_in, rows_in = (sem("l_" + x) for x in ("kdk_in", "kdv_in", "new_in", "ks_in", "kw_in", "rows_in"))
        kdk_out, kdv_out, kw_out, acc_out, oT_out = (sem("l_" + x) for x in ("kdk_out", "kdv_out", "kw_out", "acc_out", "oT_out"))
        s_filled, s_free = sem("l_s_filled"), sem("l_s_free")
        t_filled = sem("l_t_filled")
        t_evac = [sem("l_t_evac_act"), sem("l_t_evac_dve")]
        o_filled, o_free = sem("l_o_filled"), sem("l_o_free")
        masked, exped, scaled = sem("l_masked"), sem("l_exped"), sem("l_scaled")
        hi_done, lo_done = sem("l_hi_done"), sem("l_lo_done")
        dve_c, pool_c = sem("l_dve_c"), sem("l_pool_c")
        bd_zero, bd_ready = sem("l_bd_zero"), sem("l_bd_ready")
        tanh_in, tanh_done, hid_ready, ckv_ready, sel_ready = (sem("l_" + x) for x in ("tanh_in", "tanh_done", "hid_ready", "ckv_ready", "sel_ready"))

        CREDIT_O = 8
        at_s = lambda i, n: i * NSC + (n + 1)
        at_t = lambda i, n: i * NT + (n + 1)
        at_o = lambda i, n: i * NU + (n + 1 + CREDIT_O)
        at_u = lambda i, n: i * NU + (n + 1)
        at_evac = lambda i, n: i * (NT // 2) + (n // 2 + 2)
        last_t = lambda name, j: max(v for (a, b, _), v in T.items() if a == name and b == j)

        def wait_turned(eng, i, name, j=None):
            qs = [v for (a, b, _), v in T.items() if a == name and (j is None or b == j)]
            for par in range(2):
                mine = [q for q in qs if q % 2 == par]
                if mine:
                    eng.wait_ge(t_evac[par], at_evac(i, max(mine)))

        def loop(eng, body):
            with eng.Fori(0, DB) as i:
                body(i)

        block = ctx.enter_context(nc.Block())

        dil_rows = o["dil_prompt"].rearrange("b s c h e -> (b s) (c h e)").rearrange("(a p) n -> p a n", p=P)
        slc_rows = o["slc_prompt"].rearrange("b s c g e -> (b s) (c g e)").rearrange("(a p) n -> p a n", p=P)
        win_rows = scratch["kvw"][0:SEQ, :].rearrange("(a p) n -> p a n", p=P)
        q_rows = [scratch[x][0:SEQ, :].rearrange("(a p) n -> p a n", p=P) for x in ("qb", "qa")]
        o_rows = scratch["o"].rearrange("(a p) n -> p a n", p=P)
        unit = {u: n for n, u in enumerate(UNITS)}

        @block.sync
        def _(sp):
            sp.dma_start(masks[:], t["masks"]).then_inc(const_in, 16)
            sp.dma_start(smask[:], t["smask"]).then_inc(const_in, 16)
            sp.dma_start(pages[:], t["page_table"].rearrange("(o b) n -> o (b n)", o=1)).then_inc(pages_in, 16)
            sp.dma_start(o["win_prompt"].rearrange("b s c g e -> (b s) (c g e)"), scratch["kvw"][SEQ - WIN:SEQ, :]).then_inc(win_out, 16)
            sp.wait_ge(pages_in, 16)

            sp.sem_inc(acc_out, 1)

            def load_dil(i):
                sp.dma_start(q_nat[0][:], q_rows[0][:, :, bass.ds(i * E, E)]).then_inc(q_in[0], 16)
                sp.dma_start(kv_nat[0][:, :, 0, :], dil_rows[:, :, bass.ds(i * E, E)]).then_inc(kv_in[0], 16)
                sp.dma_start(kv_nat[0][:, :, 1, :], dil_rows[:, :, bass.ds(i * E + 512, E)]).then_inc(kv_in[0], 16)

            def load_q_nsa(i):
                sp.dma_start(q_nat[1][:], q_rows[1][:, :, bass.ds(i * E, E)]).then_inc(q_in[1], 16)

            def load_kv_nsa(i, k):
                g = (i // RA) * E
                for c in range(2):
                    if k == 3:
                        dst, src = kv_nat[3][:, 0, c, :], scratch["kvc"][:, c, :, :].rearrange("n g e -> n (g e)")[:, bass.ds(g, E)]
                    else:
                        dst, src = kv_nat[k][:, :, c, :], (slc_rows if k == 1 else win_rows)[:, :, bass.ds(g + c * P, E)]
                    sp.dma_start(dst, src).then_inc(kv_in[k], 16)

            def load_kd(i, c):
                src = t["state_dil"][bass.ds(i, 1), :, c, :, :].rearrange("b (p j) h e -> (b p) j (h e)", j=8)
                sp.dma_start((kd_k, kd_v)[c][:], src).then_inc((kdk_in, kdv_in)[c], 16)

            def load_new(i):
                sp.dma_start(kd_new[:], o["dil_sample"][bass.ds(i, 1), PAST:PAST + DT].rearrange("b s c h e -> (b s) (c h e)")).then_inc(new_in, 16)
                sp.dma_start(ks_new[:], o["slc_sample"][bass.ds(i, 1)].rearrange("b s c g e -> (b s) (c g e)")).then_inc(new_in, 16)
                sp.dma_start(kw_new[:], scratch["kvw"][bass.ds(i * DT + SEQ, DT), :]).then_inc(new_in, 16)

            def page(i, n):
                return sp.value_load(pages[0:1, bass.ds(i * PAGES + n, 1)], min_val=0, max_val=t["cache_slc"].shape[0] - 1)

            def load_ks(i):
                for n in range(PAGES):
                    sp.dma_start(ks[:, n, :], t["cache_slc"][bass.ds(page(i, n), 1)].rearrange("b p c g e -> (b p) (c g e)")).then_inc(ks_in, 16)

            def load_rows16(i):
                for n in range(PAGES):
                    pg = page(i, n)
                    for c in range(4):
                        sp.dma_start(rows16[8 * n:8 * n + 8, c * 1024:(c + 1) * 1024].rearrange("n (r e) -> n r e", e=E),
                                     t["cache_cmp"][bass.ds(pg, 1)].rearrange("b (n r) c g e -> (b n) r (c g) e", r=CMP_STRIDE)[:, :, c, :]).then_inc(rows_in, 16)

            def load_kw(i):
                sp.dma_start(kw[:], t["state_win"][bass.ds(i, 1)].rearrange("b (p j) c g e -> (b p) j (c g e)", j=WIN // P)).then_inc(kw_in, 16)

            load_dil(0)
            load_q_nsa(0)
            load_kd(0, 0)
            load_new(0)
            load_kv_nsa(0, 1)
            load_kd(0, 1)
            load_kw(0)
            load_ks(0)
            load_kv_nsa(0, 2)
            load_kv_nsa(0, 3)

            def body(i, more):
                sp.wait_ge(kdk_in, i * 16 + 16)
                sp.sem_inc(passed, 1)
                sp.dma_start(o["dil_sample"][bass.ds(i, 1), 0:PAST, 0, :, :].rearrange("b (p j) h e -> (b p) j (h e)", j=8), kd_k[:]).then_inc(kdk_out, 16)
                sp.wait_ge(kdv_in, i * 16 + 16)
                sp.sem_inc(passed, 1)
                sp.dma_start(o["dil_sample"][bass.ds(i, 1), 0:PAST, 1, :, :].rearrange("b (p j) h e -> (b p) j (h e)", j=8), kd_v[:]).then_inc(kdv_out, 16)
                sp.wait_ge(kw_in, i * 16 + 16)
                sp.sem_inc(passed, 1)
                sp.dma_start(o["win_sample"][bass.ds(i, 1), 0:WIN - DT].rearrange("b (p j) c g e -> (b p) j (c g e)", j=WIN // P), kw[2:P]).then_inc(kw_out, 16)
                sp.wait_ge(new_in, i * 48 + 48)
                sp.sem_inc(passed, 1)
                sp.dma_start(o["win_sample"][bass.ds(i, 1), WIN - DT:WIN].rearrange("b s c g e -> (b s) (c g e)"), kw_new[:]).then_inc(kw_out, 16)
                sp.wait_ge(t_filled, at_t(i, last_t("kd", 7)))
                sp.sem_inc(passed, 1)
                sp.wait_ge(kdk_out, i * 16 + 16)
                sp.sem_inc(passed, 1)
                load_rows16(i)
                sp.wait_ge(o_filled, at_o(i, unit["d", 7]))
                sp.sem_inc(passed, 1)
                if more:
                    load_dil(i + 1)
                sp.wait_ge(o_filled, at_o(i, unit["sd", 0]))
                sp.sem_inc(passed, 1)
                sp.wait_ge(kdv_out, i * 16 + 16)
                sp.sem_inc(passed, 1)
                if more:
                    load_kd(i + 1, 1)
                sp.wait_ge(o_free, at_u(i, unit["d", 7]) + 2)
                sp.sem_inc(passed, 1)
                sp.dma_start(o_rows[:, :, bass.ds(i * E + 512, E)], acc[0][:]).then_inc(acc_out, 16)
                sp.wait_ge(t_filled, at_t(i, last_t("xt", 3)))
                sp.sem_inc(passed, 1)
                if more:
                    load_kd(i + 1, 0)
                sp.wait_ge(o_filled, at_o(i, unit["l", 7]))
                sp.sem_inc(passed, 1)
                if more:
                    load_q_nsa(i + 1)
                    load_kv_nsa(i + 1, 1)
                sp.wait_ge(o_filled, at_o(i, unit["w", 7]))
                sp.sem_inc(passed, 1)
                if more:
                    load_kv_nsa(i + 1, 2)
                sp.wait_ge(o_filled, at_o(i, unit["sl", 0]))
                sp.sem_inc(passed, 1)
                if more:
                    load_ks(i + 1)
                sp.wait_ge(o_filled, at_o(i, unit["sw", 0]))
                sp.sem_inc(passed, 1)
                sp.wait_ge(kw_out, i * 32 + 32)
                sp.sem_inc(passed, 1)
                if more:
                    load_new(i + 1)
                    load_kw(i + 1)
                sp.wait_ge(o_filled, at_o(i, unit["c", 7]))
                sp.sem_inc(passed, 1)
                if more:
                    load_kv_nsa(i + 1, 3)
                sp.wait_ge(o_free, at_u(i, NU - 1) + 2)
                sp.sem_inc(passed, 1)
                sp.dma_start(o_rows[:, :, bass.ds((i % RA) * (GA * E) + (i // RA) * E, E)], acc[1][:]).then_inc(acc_out, 16)

            with sp.Fori(0, DB - 1) as i:
                body(i, True)
            body(DB - 1, False)
            sp.dma_start(scratch["oT"], oT_s[:]).then_inc(oT_out, 16)
            sp.wait_ge(acc_out, 32 * DB + 1)
            sp.wait_ge(oT_out, 16)
            sp.wait_ge(win_out, 16)
            sp.wait_ge(kw_out, 32 * DB)

        @block.gpsimd
        def _(pool):
            nc.gpsimd.memset(bd_dil[:], 0.0).then_inc(bd_zero, 1)
            nc.gpsimd.memset(bd_nsa[:], 0.0).then_inc(bd_zero, 1)
            pool.wait_ge(bd_zero, 2)

            ch = Chain(pool, pool_c)

            def body(i):
                ch.enter(i, 5)
                pool.wait_ge(o_free, at_u(i, -1) + 2)
                for g in range(2):
                    hp = slice(g * E, (g + 1) * E)
                    ch.step(nc.gpsimd.tensor_copy(bd_dil[hp, :].rearrange("p (a c) -> p a c", c=80)[:, :, g * DT:(g + 1) * DT],
                                                  q_dil_T[hp, :, bass.ds(i * DT, DT)]))
                    ch.step(nc.gpsimd.tensor_copy(bd_nsa[hp, g * RA * DT:(g + 1) * RA * DT].rearrange("p (a c) -> p a c", c=DT),
                                                  q_nsa_T[hp, :, bass.ds(i * DT, DT)]))
                ch.step(nc.gpsimd.tensor_copy(gate_h[:], gate_p[:, :, bass.ds(i * 3, 3)]))
                nc.gpsimd.tensor_copy(gate_b[:].unsqueeze(1), gate_s[:, bass.ds(i, 1), :]).then_inc(bd_ready, 1)

            loop(pool, body)

        @block.tensor
        def _(pe):
            pe.wait_ge(const_in, 32)

            def body(i):
                def qk(n):
                    kind, j = UNITS[n]
                    if kind[0] != "s":
                        b = BRANCH[kind]
                        a0, a1 = key_blocks(kind, j)
                        w = (a1 - a0) * P if kind != "c" else NS
                        if j == 0:
                            wait_turned(pe, i, "prep", b)
                        slot = S["qk", n, 0]
                        pe.wait_ge(s_free, at_s(i, slot))
                        lhs = qT[b > 0][:, j * P:(j + 1) * P]
                        for c in range(0, w, 512):
                            cw = min(512, w - c)
                            ks_ = slice(a0 * P + c, a0 * P + c + cw)
                            out = s_ps[slot % 2][:, c:c + cw]
                            nc.tensor.matmul(out, lhs, kB[b % 2][:, ks_], start=True, stop=False)
                            last = nc.tensor.matmul(out, lhs, kA[b % 2][:, ks_], start=False, stop=True)
                        last.then_inc(s_filled, 1)
                        return
                    if kind == "sd":
                        pe.wait_ge(bd_ready, i + 1)
                        wait_turned(pe, i, "kd")
                    if kind == "sl":
                        wait_turned(pe, i, "ksw")
                    if kind == "sc":
                        pe.wait_ge(ckv_ready, i + 1)
                    parts = {"sd": [(kd_T, PAST), (0, DT)], "sc": [(kc_T, NCMP)], "sl": [(ks_T, PAST), (4, DT)], "sw": [(kw_T, WIN)]}[kind]
                    for part, (src, w) in enumerate(parts):
                        slot = S["qk", n, part]
                        pe.wait_ge(s_free, at_s(i, slot))
                        out = s_ps[slot % 2]
                        for c in range(0, w, 512):
                            cw = min(512, w - c)
                            if kind == "sd":
                                for a in range(4):
                                    rhs = kd_T[:, a, c:c + cw] if part == 0 else new_T[:, a, :]
                                    last = nc.tensor.matmul(out[0:NS, c:c + cw], bd_dil[:, a * NS:(a + 1) * NS], rhs, start=(a == 0), stop=(a == 3))
                            else:
                                rhs = src[:, c:c + cw] if part == 0 else new_T[:, 4, :]
                                last = nc.tensor.matmul(out[0:NS, c:c + cw], bd_nsa[:], rhs, start=True, stop=True)
                        if kind == "sw":
                            last = nc.tensor.matmul(out[0:NS, WIN:WIN + DT], bd_nsa[:], new_T[:, 5, :], start=True, stop=True)
                        last.then_inc(s_filled, 1)

                def turn_slot(q):
                    pe.wait_ge(t_evac[q % 2], i * (NT // 2) + (q // 2 + 1))
                    pe.sem_inc(passed, 1)
                    return t_ps[q % 2]

                def tr(n):
                    kind, j = UNITS[n]
                    if kind[0] != "s":
                        a0, a1 = key_blocks(kind, j)
                        w = (a1 - a0) * P if kind != "c" else NS
                        pe.wait_ge(exped, at_u(i, n))
                        for c in range(0, w, 512):
                            q = T["tr", n, c // 512]
                            dst = turn_slot(q)
                            for k in range(c, min(w, c + 512), P):
                                kw_ = min(P, w - k)
                                last = nc.tensor.transpose(dst[0:kw_, k - c:k - c + P], e_ring[:, n % 4, k:k + kw_], ident[:])
                            last.then_inc(t_filled, 1)
                        return
                    nth = [u for u in range(NU) if UNITS[u][0][0] == "s"].index(n)
                    w = {"sd": PAST, "sc": NCMP, "sl": PAST, "sw": WIN}[kind]
                    if kind == "sc":
                        pe.wait_ge(exped, at_u(i, n))
                    else:
                        pe.wait_ge(scaled, i * 4 + (nth + 1))
                    dst = turn_slot(T["tr", n, 0])
                    for k in range(0, w, P):
                        kw_ = min(P, w - k)
                        last = nc.tensor.transpose(dst[0:kw_, k // P * NS:(k // P + 1) * NS], e_ring[0:NS, n % 4, k:k + kw_], ident[0:NS, 0:NS])
                    last.then_inc(t_filled, 1)
                    dst = turn_slot(T["tr", n, 1])
                    if kind == "sc":
                        pe.wait_ge(scaled, i * 4 + (nth + 1))
                        pe.sem_inc(passed, 1)
                        last = nc.tensor.transpose(dst[0:NCMP, 0:NS], e_gated[:, 0:NCMP], ident[0:NS, 0:NS])
                    else:
                        last = nc.tensor.transpose(dst[0:DT, 0:NS], e_ring[0:NS, n % 4, w:w + DT], ident[0:NS, 0:NS])
                    last.then_inc(t_filled, 1)

                def pv(n):
                    kind, j = UNITS[n]
                    pe.wait_ge(o_free, at_u(i, n))
                    out = o_ps[n % 2]
                    if kind[0] != "s":
                        b = BRANCH[kind]
                        a0, a1 = key_blocks(kind, j)
                        if j == 0:
                            pe.wait_ge(kv_in[b], i * 32 + 32)
                        for k in range(a1 - a0):
                            if k % 4 == 0:
                                q = T["tr", n, k // 4]
                                pe.wait_ge(t_evac[q % 2], at_evac(i, q))
                                probs = p_ring[:, U[n, k // 4] % 4, :]
                            r = P if kind != "c" else NS
                            last = nc.tensor.matmul(out[:, 0:E], probs[0:r, (k % 4) * P:(k % 4 + 1) * P], kv_nat[b][0:r, a0 + k, 1, :],
                                                    start=(k == 0), stop=(k == a1 - a0 - 1))
                        last.then_inc(o_filled, 1)
                        return
                    for q in range(2):
                        pe.wait_ge(t_evac[T["tr", n, q] % 2], at_evac(i, T["tr", n, q]))
                    p0, p1 = (p_ring[:, U[n, q] % 4, :] for q in range(2))
                    if kind == "sd":
                        pe.wait_ge(kdv_in, i * 16 + 16)
                        for a in range(4):
                            for k in range(8):
                                nc.tensor.matmul(out[:, a * 16:(a + 1) * 16], kd_v[:, k, a * P:(a + 1) * P], p0[:, k * NS + a * 16:k * NS + (a + 1) * 16],
                                                 start=(k == 0), stop=False)
                            last = nc.tensor.matmul(out[:, a * 16:(a + 1) * 16], kd_new[:, 512 + a * P:512 + (a + 1) * P], p1[0:DT, a * 16:(a + 1) * 16],
                                                    start=False, stop=True)
                        last.then_inc(o_filled, 1)
                    elif kind == "sc":
                        slot = S["sel1", 0, 0]
                        pe.wait_ge(s_free, at_s(i, slot))
                        pe.sem_inc(passed, 1)
                        nc.tensor.matmul(s_ps[slot % 2][0:NS, 0:NBLK], p0[0:NCMP, 0:NS], smask[0:NCMP, S_OVER:S_OVER + NBLK],
                                         start=True, stop=True).then_inc(s_filled, 1)
                        nc.tensor.matmul(out[:, 0:NS], vc[:], p1[0:NCMP, 0:NS], start=True, stop=True).then_inc(o_filled, 1)
                    else:
                        src, new, m = (ks, ks_new, PAGES) if kind == "sl" else (kw, kw_new, WIN // P)
                        for k in range(m):
                            nc.tensor.matmul(out[:, 0:NS], src[:, k, P:2 * P], p0[:, k * NS:(k + 1) * NS], start=(k == 0), stop=False)
                        nc.tensor.matmul(out[:, 0:NS], new[:, P:2 * P], p1[0:DT, 0:NS], start=False, stop=True).then_inc(o_filled, 1)

                def prep(b):
                    pe.wait_ge(lo_done, i * 4 + (b + 1))
                    jobs = []
                    if b < 2:
                        jobs += [[(q_split[:, k, :], P) for k in range(c, c + 4)] for c in (0, 4)]
                    if b < 3:
                        for at in (0, E):
                            jobs += [[(k_split[:, k, at:at + 2 * E], P) for k in range(c, c + 4)] for c in (0, 4)]
                    else:
                        jobs += [[(k_split[0:NS, 0, at:at + 2 * E], NS)] for at in (0, E)]
                    for q, job in enumerate(jobs):
                        dst = turn_slot(T["prep", b, q])
                        for k, (src, r) in enumerate(job):
                            last = nc.tensor.transpose(dst[:, k * P:k * P + r], src.bitcast(F32), ident[0:r, 0:r])
                        last.then_inc(t_filled, 1)

                def extra(name, j):
                    if name == "prep":
                        prep(j)
                    elif name == "kd":
                        if j == 0:
                            pe.wait_ge(kdk_in, i * 16 + 16)
                        dst = turn_slot(T[name, j, 0])
                        for a in range(4):
                            last = nc.tensor.transpose(dst[:, a * P:(a + 1) * P], kd_k[:, j, a * P:(a + 1) * P], ident[:])
                        last.then_inc(t_filled, 1)
                    elif name == "new":
                        pe.wait_ge(new_in, i * 48 + 48)
                        dst = turn_slot(T[name, j, 0])
                        for a in range(6):
                            src = kd_new[:, a * P:(a + 1) * P] if a < 4 else (ks_new, kw_new)[a - 4][:, 0:P]
                            last = nc.tensor.transpose(dst[:, a * DT:(a + 1) * DT], src, ident[0:DT, 0:DT])
                        last.then_inc(t_filled, 1)
                    elif name == "ksw":
                        if j < 2:
                            pe.wait_ge(ks_in, i * 16 * PAGES + 16 * PAGES)
                        else:
                            pe.wait_ge(kw_in, i * 16 + 16)
                        dst = turn_slot(T[name, j, 0])
                        for a in range(4):
                            src = ks[:, j * 4 + a, 0:P] if j < 2 else kw[:, a, 0:P]
                            last = nc.tensor.transpose(dst[:, a * P:(a + 1) * P], src, ident[:])
                        last.then_inc(t_filled, 1)
                    elif name == "xt":
                        if j == 0:
                            pe.wait_ge(rows_in, i * 64 * PAGES + 64 * PAGES)
                        dst = turn_slot(T[name, j, 0])
                        for rp in range(8):
                            last = nc.tensor.transpose(dst[:, rp * NS:(rp + 1) * NS], rows16[:, j * 1024 + rp * P:j * 1024 + (rp + 1) * P], ident[0:NS, 0:NS])
                        last.then_inc(t_filled, 1)
                    elif name == "hid":
                        wait_turned(pe, i, "xt")
                        slot = S[name, j, 0]
                        pe.wait_ge(s_free, at_s(i, slot))
                        for c in range(2):
                            out = s_ps[slot % 2][:, c * P:(c + 1) * P].rearrange("p (g n) -> p g n", g=GA)[:, :, 0:NCMP]
                            for k in range(16):
                                last = nc.tensor.matmul(out, w1[:, c, k, :], xT[:, c, :, k % 8, k // 8:k // 8 + NCMP], start=(k == 0), stop=(k == 15))
                        last.then_inc(s_filled, 1)
                    elif name == "ckv":
                        pe.wait_ge(hid_ready, i + 1)
                        slot = S[name, j, 0]
                        pe.wait_ge(s_free, at_s(i, slot))
                        for g in range(GA):
                            nc.tensor.matmul(s_ps[slot % 2][g * E:(g + 1) * E, 0:NCMP], w2[:, 0, :], hu[:, g, 0:NCMP], start=True, stop=True)
                            last = nc.tensor.matmul(s_ps[slot % 2][0:NCMP, P + g * E:P + (g + 1) * E], hu[:, 2 + g, 0:NCMP], w2[:, 1, :], start=True, stop=True)
                        last.then_inc(s_filled, 1)
                    elif name == "sel2":
                        pe.wait_ge(sel_ready, i + 1)
                        slot = S[name, j, 0]
                        pe.wait_ge(s_free, at_s(i, slot))
                        pe.sem_inc(passed, 1)
                        nc.tensor.matmul(s_ps[slot % 2][0:NS, 0:NBLK], smask[:, S_SAME:S_SAME + NS], sel[:, 0, :], start=True, stop=True).then_inc(s_filled, 1)

                for s in range(-1, NU + 3):
                    if 0 <= s < NU:
                        qk(s)
                    if 0 <= s - 2 < NU:
                        tr(s - 2)
                    if 0 <= s - 3 < NU:
                        pv(s - 3)
                    for name, j in EXTRAS.get(s, ()):
                        extra(name, j)

            pe.sem_inc(o_filled, CREDIT_O)
            loop(pe, body)

        def copy_dst(i, name, j, q):
            if name == "tr":
                kind, jj = UNITS[j]
                dst = p_ring[:, U[j, q] % 4, :]
                if kind[0] != "s":
                    a0, a1 = key_blocks(kind, jj)
                    w = min(4, a1 - a0 - 4 * q) * P
                    r = P if kind != "c" else NS
                elif q == 1:
                    w, r = NS, (NCMP if kind == "sc" else DT)
                else:
                    w, r = {"sd": 512, "sc": NS, "sl": 512, "sw": 4 * NS}[kind], (NCMP if kind == "sc" else P)
                return dst[0:r, 0:w], r, w
            if name == "prep":
                if j < 2:
                    if q < 2:
                        return qT[j][:, q * 512:(q + 1) * 512], P, 512
                    q -= 2
                if j == 3:
                    return (kA, kB)[q][1][:, 0:NS], P, NS
                return (kA, kB)[q // 2][j % 2][:, (q % 2) * 512:(q % 2 + 1) * 512], P, 512
            if name == "kd":
                return kd_T[:, :, j * P:(j + 1) * P], P, 512
            if name == "new":
                return new_T[:].rearrange("p a n -> p (a n)"), P, 6 * DT
            if name == "ksw":
                return (ks_T[:, j * 512:(j + 1) * 512] if j < 2 else kw_T[:, :]), P, 512
            return xT[:, j // 2, j % 2].rearrange("p a n -> p (a n)"), P, 512

        def evacuate(eng, par, i, name, j, copy):
            for q in range(8):
                n = T.get((name, j, q))
                if n is None or n % 2 != par:
                    continue
                eng.wait_ge(t_filled, at_t(i, n))
                if name == "tr":
                    u = U[j, q] - 4
                    back = max((m for (m, _), v in U.items() if v == u), default=None) if u >= 0 else None
                    if back is None:
                        eng.wait_ge(o_filled, at_o(i, -1))
                    else:
                        eng.wait_ge(o_filled, at_o(i, back))
                dst, r, w = copy_dst(i, name, j, q)
                src = t_ps[par][0:r, 0:w]
                if name == "kd":
                    src = src.rearrange("p (a n) -> p a n", a=4)
                copy(dst, src).then_inc(t_evac[par], 1)

        @block.scalar
        def _(act):
            act.sem_inc(t_evac[0], 1)
            copy = lambda dst, src: nc.scalar.activation(dst, src, ACT.Copy)

            def body(i):
                def split(b):
                    if b == 0:
                        act.wait_ge(t_evac[1], i * (NT // 2) + 1)
                    else:
                        act.wait_ge(t_filled, at_t(i, last_t("prep", b - 1)))
                    act.wait_ge(kv_in[b], i * 32 + 32)
                    r, m = (P, TILES) if b < 3 else (NS, 1)
                    if b < 2:
                        act.wait_ge(q_in[b], i * 16 + 16)
                        copy(q_split[:, :, 0:E], q_nat[b][:])
                    copy(k_split[0:r, 0:m, 0:E], kv_nat[b][0:r, 0:m, 0, :])
                    copy(k_split[0:r, 0:m, 2 * E:3 * E], kv_nat[b][0:r, 0:m, 0, :]).then_inc(hi_done, 1)

                def exp(n):
                    kind, j = UNITS[n]
                    if kind[0] != "s":
                        a0, a1 = key_blocks(kind, j)
                        r, w = P, ((a1 - a0) * P if kind != "c" else NS)
                    else:
                        r, w = NS, {"sd": PAST + DT, "sc": NCMP, "sl": PAST + DT, "sw": WIN + DT}[kind]
                    act.wait_ge(masked, at_u(i, n))
                    k = n % 4
                    nc.scalar.activation(e_ring[0:r, k, 0:w], e_ring[0:r, k, 0:w], ACT.Exp, bias=nmin[0:r, k:k + 1], scale=-1.0,
                                         accum_out=total[0:r, k:k + 1]).then_inc(exped, 1)

                for s in range(-1, NU + 3):
                    if 0 <= s - 1 < NU:
                        exp(s - 1)
                    if 0 <= s - 2 < NU:
                        evacuate(act, 0, i, "tr", s - 2, copy)
                    if s in SPLIT_AT:
                        split(SPLIT_AT[s])
                    for name, j in EXTRAS.get(s, ()):
                        evacuate(act, 0, i, name, j, copy)
                        if name == "hid":
                            act.wait_ge(tanh_in, i + 1)
                            nc.scalar.activation(hu[:, :, 0:NCMP], hu[:, :, 0:NCMP], ACT.Tanh, scale=GELU_C).then_inc(tanh_done, 1)

            loop(act, body)

        @block.vector
        def _(dve):
            dve.sem_inc(t_evac[1], 1)
            dve.sem_inc(s_free, 2)
            dve.sem_inc(o_free, 2)
            ch = Chain(dve, dve_c)
            dve.wait_ge(const_in, 32)
            dve.wait_ge(const_in, 32)
            copy = lambda dst, src: nc.vector.tensor_copy(dst, src)

            def body(i):
                ch.enter(i, CHAIN_PER_PASS)

                def split(b):
                    dve.wait_ge(hi_done, i * 4 + (b + 1))
                    r, m = (P, TILES) if b < 3 else (NS, 1)
                    if b < 2:
                        nc.vector.tensor_tensor(q_split[:, :, E:2 * E], q_nat[b][:], q_split[:, :, 0:E].bitcast(F32), ALU.subtract)
                    nc.vector.tensor_tensor(k_split[0:r, 0:m, E:2 * E], kv_nat[b][0:r, 0:m, 0, :], k_split[0:r, 0:m, 0:E].bitcast(F32),
                                            ALU.subtract).then_inc(lo_done, 1)

                def mask(dst, src, m, acc_, last):
                    return nc.vector.tensor_tensor_reduce(out=dst, in0=src, in1=m, scale=1.0, scalar=CLAMP, op0=ALU.add, op1=ALU.min, accum_out=acc_)

                def low(n):
                    kind, j = UNITS[n]
                    k = n % 4
                    slot = S["qk", n, 0]
                    dve.wait_ge(s_filled, at_s(i, slot))
                    dve.sem_inc(passed, 1)
                    sp_ = s_ps[slot % 2]
                    if kind[0] != "s":
                        a0, a1 = key_blocks(kind, j)
                        w = (a1 - a0) * P if kind != "c" else NS
                        end = {"d": SEQ, "l": 2 * SEQ, "w": M_CMP, "c": M_CMP + (j + 1) * NS}[kind]
                        ins = mask(e_ring[:, k, 0:w], sp_[:, 0:w], masks[:, end - w:end], nmin[:, k:k + 1], True)
                        ins.then_inc(s_free, 1)
                        dve.wait_ge(s_free, at_s(i, slot) + 2)
                        dve.sem_inc(masked, 1)
                        return
                    if kind in ("sc", "sw"):
                        w, m0 = (NCMP, S_ZERO) if kind == "sc" else (WIN + DT, S_WIN)
                        ins = mask(e_ring[0:NS, k, 0:w], sp_[0:NS, 0:w], smask[:, m0:m0 + w], nmin[0:NS, k:k + 1], True)
                        ins.then_inc(s_free, 1)
                        dve.wait_ge(s_free, at_s(i, slot) + 2)
                        dve.sem_inc(masked, 1)
                        return
                    if kind == "sd":
                        ins = mask(e_ring[0:NS, k, 0:PAST], sp_[0:NS, 0:PAST], smask[:, 0:PAST], nmin[0:NS, k:k + 1], False)
                        m1 = smask[:, PAST:PAST + DT]
                    else:
                        ins = mask(e_ring[0:NS, k, 0:PAST].rearrange("p (b c) -> p b c", c=SLC_BLK), sp_[0:NS, 0:PAST].rearrange("p (b c) -> p b c", c=SLC_BLK),
                                   sel[:, 2, :].unsqueeze(2).to_broadcast([NS, NBLK, SLC_BLK]), nmin[0:NS, k:k + 1], False)
                        m1 = smask[:, S_NEW:S_NEW + DT]
                    ins.then_inc(s_free, 1)
                    slot = S["qk", n, 1]
                    dve.wait_ge(s_filled, at_s(i, slot))
                    dve.sem_inc(passed, 1)
                    mask(e_ring[0:NS, k, PAST:PAST + DT], s_ps[slot % 2][0:NS, 0:DT], m1, nmin2[:], True).then_inc(s_free, 1)
                    dve.wait_ge(s_free, at_s(i, slot) + 2)
                    nc.vector.tensor_tensor(nmin[0:NS, k:k + 1], nmin[0:NS, k:k + 1], nmin2[:], ALU.min).then_inc(masked, 1)

                def scale(n):
                    kind, _ = UNITS[n]
                    k = n % 4
                    dve.wait_ge(exped, at_u(i, n))
                    rt = rtot[0:NS, k:k + 1]
                    ch.step(nc.vector.reciprocal(rt, total[0:NS, k:k + 1]))
                    w = {"sd": PAST + DT, "sc": NCMP, "sl": PAST + DT, "sw": WIN + DT}[kind]
                    e = e_ring[0:NS, k, 0:w]
                    if kind == "sd":
                        nc.vector.tensor_scalar(e, e, rt, None, ALU.mult).then_inc(scaled, 1)
                    else:
                        b = {"sc": 0, "sl": 1, "sw": 2}[kind]
                        out = e_gated[:, 0:w] if kind == "sc" else e
                        nc.vector.tensor_scalar(out, e, rt, gate_b[:, b:b + 1], ALU.mult, ALU.mult).then_inc(scaled, 1)

                def out(n):
                    kind, j = UNITS[n]
                    k = n % 4
                    dve.wait_ge(o_filled, at_o(i, n))
                    src = o_ps[n % 2]
                    if kind[0] != "s":
                        rt = rtot[:, k:k + 1]
                        if kind == "c":
                            ch.step(nc.vector.tensor_scalar(total[:, k:k + 1], total[:, k:k + 1], TINY, None, ALU.max))
                        ch.step(nc.vector.reciprocal(rt, total[:, k:k + 1]))
                        if kind == "d":
                            if j == 0:
                                dve.wait_ge(acc_out, i * 32 + 1)
                            nc.vector.tensor_scalar(acc[0][:, j, :], src[:, 0:E], rt, None, ALU.mult).then_inc(o_free, 1)
                            return
                        g = gate_h[:, j, {"l": 1, "w": 2, "c": 0}[kind]:][:, 0:1]
                        if kind == "l":
                            nc.vector.tensor_scalar(acc[1][:, j, :], src[:, 0:E], rt, g, ALU.mult, ALU.mult).then_inc(o_free, 1)
                            return
                        ch.step(nc.vector.tensor_tensor(rt, rt, g, ALU.mult))
                        nc.vector.scalar_tensor_tensor(out=acc[1][:, j, :], in0=src[:, 0:E], scalar=rt, in1=acc[1][:, j, :], op0=ALU.mult, op1=ALU.add).then_inc(o_free, 1)
                        return
                    for g in range(2):
                        hp = slice(g * E, (g + 1) * E)
                        if kind == "sd":
                            ins = nc.vector.tensor_copy(oT_s[hp, 4:8, bass.ds(i * DT, DT)],
                                                        src[hp, 0:64].rearrange("p (a c) -> p a c", c=16)[:, :, g * DT:(g + 1) * DT])
                        else:
                            v = src[hp, g * 32:(g + 1) * 32]
                            if kind == "sc":
                                ins = nc.vector.tensor_copy(oa_s[hp, :], v)
                            elif kind == "sl":
                                ins = nc.vector.tensor_tensor(oa_s[hp, :], v, oa_s[hp, :], ALU.add)
                            else:
                                ins = nc.vector.tensor_tensor(oT_s[hp, 0:4, bass.ds(i * DT, DT)], v.rearrange("p (a c) -> p a c", c=DT),
                                                              oa_s[hp, :].rearrange("p (a c) -> p a c", c=DT), ALU.add)
                    ins.then_inc(o_free, 1)

                def extra(name, j):
                    if name == "hid":
                        slot = S[name, j, 0]
                        dve.wait_ge(s_filled, at_s(i, slot))
                        for c in range(2):
                            ins = nc.vector.tensor_scalar(hh[:, 2 * c:2 * c + 2, 0:NCMP], s_ps[slot % 2][:, c * P:(c + 1) * P].rearrange("p (g n) -> p g n", g=GA)[:, :, 0:NCMP],
                                                          pe_bias[:, c:c + 1], None, ALU.add)
                        ins.then_inc(s_free, 1)
                        dve.wait_ge(s_free, at_s(i, slot) + 2)
                        a, b = hh[:, :, 0:NCMP], hu[:, :, 0:NCMP]
                        ch.step(nc.vector.tensor_tensor(b, a, a, ALU.mult))
                        ch.step(nc.vector.tensor_scalar(b, b, 0.044715, 1.0, ALU.mult, ALU.add))
                        nc.vector.tensor_tensor(b, b, a, ALU.mult).then_inc(tanh_in, 1)
                        dve.wait_ge(tanh_done, i + 1)
                        ch.step(nc.vector.tensor_scalar(b, b, 1.0, None, ALU.add))
                        nc.vector.tensor_tensor(b, b, a, ALU.mult).then_inc(hid_ready, 1)
                    elif name == "ckv":
                        slot = S[name, j, 0]
                        dve.wait_ge(s_filled, at_s(i, slot))
                        nc.vector.tensor_copy(kc_T[:], s_ps[slot % 2][:, 0:NCMP]).then_inc(s_free, 1)
                        nc.vector.tensor_copy(vc[:], s_ps[slot % 2][0:NCMP, P:2 * P]).then_inc(ckv_ready, 1)
                    elif name == "sel1":
                        slot = S[name, j, 0]
                        k = unit["sc", 0] % 4
                        dve.wait_ge(s_filled, at_s(i, slot))
                        nc.vector.tensor_scalar(sel[:, 0, :], s_ps[slot % 2][0:NS, 0:NBLK], rtot[0:NS, k:k + 1], None, ALU.mult).then_inc(s_free, 1)
                        dve.wait_ge(s_free, at_s(i, slot) + 2)
                        dve.sem_inc(sel_ready, 1)
                    elif name == "sel2":
                        slot = S[name, j, 0]
                        dve.wait_ge(s_filled, at_s(i, slot))
                        nc.vector.tensor_copy(sel[:, 1, :], s_ps[slot % 2][0:NS, 0:NBLK]).then_inc(s_free, 1)
                        dve.wait_ge(s_free, at_s(i, slot) + 2)
                        free = slice(1, NBLK - 1)
                        blk = smask[:, S_BLK:S_BLK + NBLK]
                        ch.step(nc.vector.tensor_reduce(selm[:, 0:1], sel[:, 1, free], AX, ALU.min))
                        ch.step(nc.vector.tensor_scalar(sel[:, 1, free], sel[:, 1, free], selm[:, 0:1], None, ALU.is_equal))
                        ch.step(nc.vector.tensor_tensor(sel[:, 1, free], sel[:, 1, free], blk[:, free], ALU.mult))
                        ch.step(nc.vector.tensor_reduce(selm[:, 1:2], sel[:, 1, free], AX, ALU.max))
                        ch.step(nc.vector.tensor_scalar(sel[:, 2, :], blk, selm[:, 1:2], BIG, ALU.is_equal, ALU.mult))

                for s in range(-1, NU + 4):
                    if 0 <= s - 4 < NU:
                        out(s - 4)
                    if 0 <= s < NU:
                        low(s)
                    if 0 <= s - 1 < NU and UNITS[s - 1][0][0] == "s":
                        scale(s - 1)
                    if 0 <= s - 2 < NU:
                        evacuate(dve, 1, i, "tr", s - 2, copy)
                    if s in SPLIT_AT:
                        split(SPLIT_AT[s])
                    for name, j in EXTRAS.get(s, ()):
                        evacuate(dve, 1, i, name, j, copy)
                        extra(name, j)
                if ch.n - ch.start != CHAIN_PER_PASS:
                    raise ValueError(f"chain steps in a pass: {ch.n - ch.start}")

            loop(dve, body)


CHAIN_PER_PASS = 68
CHUNKS = DFF // P
PAIRS = CHUNKS // 2
CONV_W = 3
HALF = D // 2
PARTS = [(0, 512), (512, 512), (SEQ, NS)]
KEPT = (CONV_W - 1) * (1 + DB)


def finish(nc, t, o, scratch):
    with ExitStack() as outer:
        osb = lambda name, shape, dt=F32: outer.enter_context(nc.sbuf_tensor(name, shape, dt))
        ident = osb("f_ident", [P, P])
        x = osb("f_x", [P, STEPS, D])
        h_hi = osb("f_h_hi", [P, KC, TOK], F32R)
        h_lo = osb("f_h_lo", [P, KC, TOK], F32R)
        out_project(nc, t, scratch, ident, x, h_hi, h_lo)
        mix_channels(nc, t, o, ident, x, h_hi, h_lo)


def out_project(nc, t, scratch, ident, x, h_hi, h_lo):
    with ExitStack() as ctx:
        sb = lambda name, shape, dt=F32: ctx.enter_context(nc.sbuf_tensor(name, shape, dt))
        ps = lambda name, shape: ctx.enter_context(nc.psum_tensor(name, shape, F32))
        sem = lambda name: ctx.enter_context(nc.semaphore(name))
        w_hi = sb("o_w_hi", [P, KC, D], F32R)
        w_lo = sb("o_w_lo", [P, KC, D], F32R)
        rows = sb("o_rows", [P, 2, D])
        heads_s = sb("o_heads_s", [P, KC, NS])
        hn = sb("o_hn", [P, 2, D])
        o_hi = sb("o_o_hi", [P, 2, KC, P], F32R)
        o_lo = sb("o_o_lo", [P, 2, KC, P], F32R)
        gain = sb("o_gain", [P, D])
        ss = sb("o_ss", [P, 2])
        root = sb("o_root", [P, 2])
        rroot = sb("o_rroot", [P, 2])
        epst = sb("o_eps", [P, 1])
        po = ps("o_po", [P, D])
        ph = ps("o_ph", [P, D])
        py = [ps(f"o_py{k}", [P, D]) for k in range(2)]
        const_in, x_in, eps_set, vchain = sem("o_const_in"), sem("o_x_in"), sem("o_eps_set"), sem("o_vchain")
        w_in = [sem(f"o_w_in{k}") for k in range(2)]
        rows_in = [sem(f"o_rows_in{k}") for k in range(2)]
        w_hi_done, w_lo_done = sem("o_w_hi_done"), sem("o_w_lo_done")
        o_turned, o_hi_done, o_lo_done = sem("o_o_turned"), sem("o_o_hi_done"), sem("o_o_lo_done")
        y_filled, y_added = sem("o_y_filled"), sem("o_y_added")
        squared, rooted, h_ready = sem("o_squared"), sem("o_rooted"), sem("o_h_ready")
        h_turned, h_hi_done, h_lo_done = sem("o_h_turned"), sem("o_h_hi_done"), sem("o_h_lo_done")
        block = ctx.enter_context(nc.Block())

        def tile_rows(i):
            return NS if isinstance(i, int) and i == STEPS // 2 else P

        def tokens(i, k):
            if tile_rows(i) == NS:
                return slice(SEQ, TOK)
            return bass.ds(i * 2 * P + k * P, P) if not isinstance(i, int) else slice((2 * i + k) * P, (2 * i + k + 1) * P)

        def x_rows(i, k):
            r = tile_rows(i)
            if isinstance(i, int):
                return x[0:r, 2 * i + k, :]
            return x[0:r, bass.ds(i * 2 + k, 1), :].rearrange("p a n -> p (a n)")

        def loop_tiles(eng, tile):
            tile(0, 0)
            tile(0, 1)
            with eng.Fori(1, TILES // 2 - 1) as i:
                tile(i, 0)
                tile(i, 1)
            tile(TILES // 2 - 1, 0)
            tile(TILES // 2 - 1, 1)
            tile(TILES // 2, 0)

        def after(i, k, n):
            if isinstance(i, int):
                s = 2 * i + k + n
                return (s // 2, s % 2) if 0 <= s < STEPS else None
            return i + (k + n) // 2, (k + n) % 2

        chunks = lambda ap: ap.rearrange("p (c q) -> p c q", c=KC)

        @block.sync
        def _(sp):
            sp.dma_start(ident[:], t["ident"]).then_inc(const_in, 16)
            for n in range(2):
                sp.dma_start(rows[:, n, :], scratch["o"][n * P:(n + 1) * P, :]).then_inc(rows_in[n], 16)
            for c in range(KC):
                if c >= 2:
                    sp.wait_ge(w_lo_done, c - 1)
                for dst, src in w_o_rows(t, c):
                    sp.dma_start(hn[dst, c % 2, :], src).then_inc(w_in[c % 2], 16)
                if c == 1:
                    sp.dma_start(heads_s[:], scratch["oT"]).then_inc(const_in, 16)
                    sp.dma_start(gain[:], t["g_ffn"]).then_inc(const_in, 16)
                    sp.dma_start(x[:, 0:TILES, :], t["x_prompt"].rearrange("b (a p) d -> p (b a) d", p=P)).then_inc(x_in, 16)
                    sp.dma_start(x[0:NS, TILES, :], t["x_sample"].rearrange("b s d -> (b s) d")).then_inc(x_in, 16)

            def load(i, k):
                nxt = after(i, k, 2)
                if nxt is None or tile_rows(nxt[0]) == NS:
                    return
                sp.wait_ge(o_turned, i * 2 + (k + 1))
                sp.dma_start(rows[:, k, :], scratch["o"][tokens(*nxt), :]).then_inc(rows_in[k], 16)

            loop_tiles(sp, load)

        @block.gpsimd
        def _(pool):
            nc.gpsimd.memset(epst[:], EPS).then_inc(eps_set, 1)

        @block.tensor
        def _(pe):
            pe.sem_inc(h_turned, 1)
            pe.wait_ge(const_in, 48)

            def turn_o(i, k):
                if tile_rows(i) == NS:
                    return
                pe.wait_ge(rows_in[k], i * 16 + 16)
                if not (isinstance(i, int) and i == 0 and k == 0):
                    pe.wait_ge(o_lo_done, i * 2 + k)
                for c in range(KC):
                    last = nc.tensor.transpose(po[:, c * P:(c + 1) * P], rows[:, k, c * P:(c + 1) * P], ident[:])
                last.then_inc(o_turned, 1)

            def turn_h(i, k):
                r = tile_rows(i)
                pe.wait_ge(h_ready, i * 2 + (k + 1))
                pe.wait_ge(h_lo_done, i * 2 + (k + 0))
                for c in range(KC):
                    last = nc.tensor.transpose(ph[:, c * P:c * P + r], hn[0:r, k, c * P:(c + 1) * P], ident[0:r, 0:r])
                last.then_inc(h_turned, 1)

            turn_o(0, 0)
            pe.wait_ge(w_lo_done, KC)

            def tile(i, k):
                r = tile_rows(i)
                nxt, prev = after(i, k, 1), after(i, k, -1)
                if nxt is not None:
                    turn_o(*nxt)
                pe.wait_ge(o_lo_done, i * 2 + (k + 1))
                pe.wait_ge(y_added, i * 2 + (k + 1))
                for half in range(2):
                    hs = slice(half * HALF, (half + 1) * HALF)
                    for j, (a, w) in enumerate(((o_hi, w_hi), (o_hi, w_lo), (o_lo, w_hi))):
                        for c in range(KC):
                            last = nc.tensor.matmul(py[k][0:r, hs], a[:, k, c, 0:r], w[:, c, hs], start=(j == 0 and c == 0), stop=(j == 2 and c == KC - 1))
                last.then_inc(y_filled, 1)
                if prev is not None:
                    turn_h(*prev)

            loop_tiles(pe, tile)
            turn_h(TILES // 2, 0)

        @block.scalar
        def _(act):
            act.wait_ge(eps_set, 1)

            def split_o(i, k):
                r = tile_rows(i)
                if r == NS:
                    src = heads_s[:]
                    act.wait_ge(const_in, 48)
                else:
                    act.wait_ge(o_turned, i * 2 + (k + 1))
                    src = chunks(po[:])
                if not (isinstance(i, int) and i == 0):
                    act.wait_ge(y_filled, i * 2 + k - 1)
                nc.scalar.activation(o_hi[:, k, :, 0:r], src, ACT.Copy).then_inc(o_hi_done, 1)

            def split_h(i, k):
                r = tile_rows(i)
                act.wait_ge(h_turned, i * 2 + (k + 2))
                nc.scalar.activation(h_hi[:, :, tokens(i, k)], chunks(ph[:])[:, :, 0:r], ACT.Copy).then_inc(h_hi_done, 1)

            for c in range(KC):
                act.wait_ge(w_in[c % 2], 16 * sum(len(w_o_rows(t, d)) for d in range(c % 2, c + 1, 2)))
                nc.scalar.activation(w_hi[:, c, :], hn[:, c % 2, :], ACT.Copy).then_inc(w_hi_done, 1)
            split_o(0, 0)

            def tile(i, k):
                r = tile_rows(i)
                nxt, prev = after(i, k, 1), after(i, k, -1)
                if nxt is not None:
                    split_o(*nxt)
                act.wait_ge(y_added, i * 2 + (k + 3))
                if isinstance(i, int) and i == 0:
                    act.wait_ge(w_lo_done, KC)
                else:
                    act.wait_ge(h_turned, i * 2 + k)
                nc.scalar.activation(hn[0:r, k, :], x_rows(i, k), ACT.Square, accum_out=ss[0:r, k:k + 1]).then_inc(squared, 1)
                act.wait_ge(squared, i * 2 + (k + 1))
                nc.scalar.activation(root[0:r, k:k + 1], ss[0:r, k:k + 1], ACT.Sqrt, bias=epst[0:r, :], scale=1.0 / D).then_inc(rooted, 1)
                if prev is not None:
                    split_h(*prev)

            loop_tiles(act, tile)
            split_h(TILES // 2, 0)

        @block.vector
        def _(dve):
            dve.sem_inc(y_added, 2)
            dve.wait_ge(const_in, 48)
            for c in range(KC):
                dve.wait_ge(w_hi_done, c + 1)
                nc.vector.tensor_tensor(w_lo[:, c, :], hn[:, c % 2, :], w_hi[:, c, :].bitcast(F32), ALU.subtract).then_inc(w_lo_done, 1)

            def split_o(i, k):
                r = tile_rows(i)
                src = heads_s[:] if r == NS else chunks(po[:])
                dve.wait_ge(o_hi_done, i * 2 + (k + 1))
                nc.vector.tensor_tensor(o_lo[:, k, :, 0:r], src, o_hi[:, k, :, 0:r].bitcast(F32), ALU.subtract).then_inc(o_lo_done, 1)

            def split_h(i, k):
                r, tok = tile_rows(i), tokens(i, k)
                dve.wait_ge(h_hi_done, i * 2 + (k + 1))
                nc.vector.tensor_tensor(h_lo[:, :, tok], chunks(ph[:])[:, :, 0:r], h_hi[:, :, tok].bitcast(F32), ALU.subtract).then_inc(h_lo_done, 1)

            split_o(0, 0)
            dve.wait_ge(x_in, 32)

            def tile(i, k):
                r = tile_rows(i)
                nxt, prev = after(i, k, 1), after(i, k, -1)
                if nxt is not None:
                    split_o(*nxt)
                dve.wait_ge(y_filled, i * 2 + (k + 1))
                xr = x_rows(i, k)
                nc.vector.tensor_tensor(xr, py[k][0:r, :], xr, ALU.add).then_inc(y_added, 1)
                dve.wait_ge(rooted, i * 2 + (k + 1))
                rr = rroot[0:r, k:k + 1]
                nc.vector.reciprocal(rr, root[0:r, k:k + 1]).then_inc(vchain, 1)
                dve.wait_ge(vchain, i * 2 + (k + 1))
                nc.vector.scalar_tensor_tensor(out=hn[0:r, k, :], in0=xr, scalar=rr, in1=gain[0:r, :], op0=ALU.mult, op1=ALU.mult).then_inc(h_ready, 1)
                if prev is not None:
                    split_h(*prev)

            loop_tiles(dve, tile)
            split_h(TILES // 2, 0)


def w_o_rows(t, c):
    w = t["w_o"]
    if c >= RA:
        return [(slice(0, P), w[c * P:(c + 1) * P, :])]
    return [(slice(g * E, (g + 1) * E), w[(g * RA + c) * E:(g * RA + c + 1) * E, :]) for g in range(GA)]


def mix_channels(nc, t, o, ident, x, h_hi, h_lo):
    with ExitStack() as ctx:
        sb = lambda name, shape, dt=F32: ctx.enter_context(nc.sbuf_tensor(name, shape, dt))
        ps = lambda name, shape: ctx.enter_context(nc.psum_tensor(name, shape, F32))
        sem = lambda name: ctx.enter_context(nc.semaphore(name))
        raw = sb("m_raw", [P, 4 * D])
        raw_gu = raw[:, 0:2 * D].rearrange("p (m c n) -> p m c n", m=2, c=KC)
        raw_d = raw[:, 2 * D:4 * D].rearrange("p (k n) -> p k n", k=2)
        gu_hi = [sb(f"m_gu_hi{k}", [P, 2, KC, P], F32R) for k in range(2)]
        gu_lo = [sb(f"m_gu_lo{k}", [P, 2, KC, P], F32R) for k in range(2)]
        wd_hi = sb("m_wd_hi", [P, 2, D], F32R)
        wd_lo = sb("m_wd_lo", [P, 2, D], F32R)
        ext = sb("m_ext", [P, CONV_W - 1 + SEQ])
        ext_s = sb("m_ext_s", [P, DB, CONV_W - 1 + DT])
        conv = [sb(f"m_conv{k}", [P, 512]) for k in range(2)]
        gated = [sb(f"m_gated{k}", [P, 512]) for k in range(2)]
        g_hi = sb("m_g_hi", [P, 2, TOK], F32R)
        g_lo = sb("m_g_lo", [P, 2, TOK], F32R)
        past = sb("m_past", [P, CHUNKS, (CONV_W - 1) * DB])
        kept = sb("m_kept", [P, CHUNKS, KEPT])
        taps_all = sb("m_taps_all", [P, CHUNKS, 4])
        taps = sb("m_taps", [P, 2, 4])
        pa = [ps(f"m_pa{k}", [P, 512]) for k in range(2)]
        pu = [ps(f"m_pu{k}", [P, 512]) for k in range(2)]
        pd = [ps(f"m_pd{k}", [P, 512]) for k in range(3)]
        (taps_in, state_in, state_turned, past_done, gu_in, wd_in, gu_hi_done, gu_lo_done, wd_hi_done, wd_lo_done, filled, copied,
         convolved, silu_done, g_made, g_hi_done, g_lo_done, d_filled, d_added, taps_ready, vchain, zeroed, kept_turned, kept_rows, y_out) = (
            sem("m_" + n) for n in ("taps_in state_in state_turned past_done gu_in wd_in gu_hi_done gu_lo_done wd_hi_done wd_lo_done filled "
                                    "copied convolved silu_done g_made g_hi_done g_lo_done d_filled d_added taps_ready vchain zeroed kept_turned kept_rows y_out").split())
        UNITS_D = 2 * STEPS
        NP = 6
        block = ctx.enter_context(nc.Block())

        DOWN_AFTER = {0: range(0, 8), 1: range(8, 16), 2: range(16, 18)}

        def chunk_in(i, k):
            return bass.ds(i * 2 + k, 1) if not isinstance(i, int) else slice(2 * i + k, 2 * i + k + 1)

        def loop_pairs(eng, body):
            body(0, True, False)
            with eng.Fori(1, PAIRS - 1) as i:
                body(i, False, False)
            body(PAIRS - 1, False, True)

        @block.sync
        def _(sp):
            sp.dma_start(taps_all[:], t["taps"]).then_inc(taps_in, 16)
            sp.dma_start(raw[0:(CONV_W - 1) * DB, 0:DFF], t["state_conv"].rearrange("b w f -> (b w) f")).then_inc(state_in, 16)

            def load_gu(i, k):
                for m, name in enumerate(("w_gate", "w_up")):
                    n0 = i * 2 * P + k * P
                    cols = bass.ds(n0, P) if not isinstance(i, int) else slice(n0, n0 + P)
                    sp.dma_start(raw_gu[:, m], t[name][:, cols].rearrange("(c p) n -> p c n", p=P)).then_inc(gu_in, 16)

            def load_wd(i):
                at = i * 2 * P
                rows = bass.ds(at, 2 * P) if not isinstance(i, int) else slice(at, at + 2 * P)
                sp.dma_start(raw_d, t["w_down"][rows, :].rearrange("(k p) n -> p k n", p=P)).then_inc(wd_in, 16)

            sp.wait_ge(state_turned, 1)
            load_gu(0, 0)
            load_wd(0)

            def body(i, more):
                sp.wait_ge(gu_lo_done, i * 2 + 1)
                load_gu(i, 1)
                if more:
                    sp.wait_ge(gu_lo_done, i * 2 + 2)
                    load_gu(i + 1, 0)
                    sp.wait_ge(wd_lo_done, i + 1)
                    load_wd(i + 1)

            with sp.Fori(0, PAIRS - 1) as i:
                body(i, True)
            body(PAIRS - 1, False)
            for n in range(STEPS):
                sp.wait_ge(d_added, 3 + (PAIRS - 1) * UNITS_D + 2 * n + 2)
                if n < TILES:
                    sp.dma_start(o["y_prompt"][0, n * P:(n + 1) * P, :], x[:, n, :]).then_inc(y_out, 16)
                else:
                    sp.dma_start(o["y_sample"].rearrange("b s d -> (b s) d"), x[0:NS, n, :]).then_inc(y_out, 16)
            sp.wait_ge(kept_rows, 6)
            sp.dma_start(o["conv_prompt"].rearrange("b w f -> (b w) f"), raw[0:CONV_W - 1, 0:DFF]).then_inc(y_out, 16)
            sp.dma_start(o["conv_sample"].rearrange("b w f -> (b w) f"), raw[CONV_W - 1:KEPT, 0:DFF]).then_inc(y_out, 16)
            sp.wait_ge(y_out, 16 * (STEPS + 2))

        @block.gpsimd
        def _(pool):
            nc.gpsimd.memset(ext[:, 0:CONV_W - 1], 0.0).then_inc(zeroed, 1)
            pool.wait_ge(taps_in, 16)
            with pool.Fori(0, PAIRS) as i:
                pool.wait_ge(g_made, i * NP + 2)
                nc.gpsimd.tensor_copy(taps[:], taps_all[:, bass.ds(i * 2, 2), :]).then_inc(taps_ready, 1)

        @block.tensor
        def _(pe):
            pe.wait_ge(state_in, 16)
            for c in range(CHUNKS):
                last = nc.tensor.transpose(pd[0][:, c * 16:(c + 1) * 16], raw[0:16, c * P:(c + 1) * P], ident[0:16, 0:16])
            last.then_inc(state_turned, 1)
            pe.wait_ge(past_done, 1)

            def part(i, q):
                k, (t0, w) = q // 3, PARTS[q % 3]
                if q % 3 == 0:
                    pe.wait_ge(gu_lo_done, i * 2 + (k + 1))
                pe.wait_ge(g_made, i * NP + (q + 1))
                for m, bank in enumerate((pa, pu)):
                    for j, (ws, hs) in enumerate(((gu_hi, h_hi), (gu_hi, h_lo), (gu_lo, h_hi))):
                        for c in range(KC):
                            last = nc.tensor.matmul(bank[q % 2][:, 0:w], ws[k][:, m, c, :], hs[:, c, t0:t0 + w], start=(j == 0 and c == 0), stop=(j == 2 and c == KC - 1))
                last.then_inc(filled, 1)

            def down(i, units):
                for d in units:
                    tile, half = d // 2, d % 2
                    r = P if tile < TILES else NS
                    tok, hs = slice(tile * P, tile * P + r), slice(half * HALF, (half + 1) * HALF)
                    if d == 0:
                        pe.wait_ge(wd_lo_done, i + 1)
                    if d % 8 == 0:
                        pe.wait_ge(g_lo_done, i * NP + (4 + d // 8))
                    pe.wait_ge(d_added, i * UNITS_D + (d + 1))
                    for n in range(6):
                        k, j = n // 3, n % 3
                        a, w = ((g_hi, wd_hi), (g_hi, wd_lo), (g_lo, wd_hi))[j]
                        last = nc.tensor.matmul(pd[d % 3][0:r, :], a[:, k, tok], w[:, k, hs], start=(n == 0), stop=(n == 5))
                    last.then_inc(d_filled, 1)

            def body(i, first, last):
                for q in range(NP):
                    part(i, q)
                    if not first and q in DOWN_AFTER:
                        down(i - 1, DOWN_AFTER[q])

            loop_pairs(pe, body)
            down(PAIRS - 1, range(UNITS_D))
            for n in range(6):
                if n < 4:
                    bank = (pa + pu)[n]
                else:
                    bank = pa[n - 4]
                    pe.wait_ge(kept_rows, n - 3)
                for c in range(4 * n, min(4 * n + 4, CHUNKS)):
                    last = nc.tensor.transpose(bank[0:KEPT, (c % 4) * P:(c % 4 + 1) * P], kept[:, c, :], ident[:])
                last.then_inc(kept_turned, 1)

        @block.scalar
        def _(act):
            act.wait_ge(past_done, 1)
            act.wait_ge(zeroed, 1)

            def split_gu(i, k):
                act.wait_ge(gu_in, i * 64 + (k + 1) * 32)
                nc.scalar.activation(gu_hi[k][:], raw_gu, ACT.Copy).then_inc(gu_hi_done, 1)

            def split_g(i, q):
                k, (t0, w) = q // 3, PARTS[q % 3]
                act.wait_ge(g_made, i * NP + (q + 3))
                nc.scalar.activation(g_hi[:, k, t0:t0 + w], gated[q % 2][:, 0:w], ACT.Copy).then_inc(g_hi_done, 1)

            split_gu(0, 0)

            def body(i, first, last):
                for q in range(NP):
                    k, (t0, w) = q // 3, PARTS[q % 3]
                    a, c = pa[q % 2][:, 0:w], conv[q % 2][:, 0:w]
                    if q == 0:
                        act.wait_ge(taps_ready, i + 1)
                    act.wait_ge(filled, i * NP + (q + 1))
                    nc.scalar.activation(c, a, ACT.Identity, bias=taps[:, k, 3:4], scale=taps[:, k, 2:3])
                    if q % 3 < 2:
                        ins = nc.scalar.activation(ext[:, CONV_W - 1 + t0:CONV_W - 1 + t0 + w], a, ACT.Copy)
                    else:
                        nc.scalar.activation(ext_s[:, :, 0:CONV_W - 1], past[:, chunk_in(i, k), :].rearrange("p a (b w) -> p (a b) w", w=CONV_W - 1), ACT.Copy)
                        ins = nc.scalar.activation(ext_s[:, :, CONV_W - 1:], a.rearrange("p (b s) -> p b s", s=DT), ACT.Copy)
                    ins.then_inc(copied, 1)
                    if q % 3 == 1:
                        nc.scalar.activation(kept[:, chunk_in(i, k), 0:CONV_W - 1], a[:, w - CONV_W + 1:w].unsqueeze(1), ACT.Copy)
                    if q % 3 == 2:
                        nc.scalar.activation(kept[:, chunk_in(i, k), CONV_W - 1:KEPT].rearrange("p a (b w) -> p (a b) w", w=CONV_W - 1),
                                             a.rearrange("p (b s) -> p b s", s=DT)[:, :, DT - CONV_W + 1:], ACT.Copy)
                    act.wait_ge(convolved, i * NP + (q + 1))
                    nc.scalar.activation(c, c, ACT.Silu).then_inc(silu_done, 1)
                    if q == 0:
                        if not first:
                            split_g(i - 1, NP - 1)
                        split_gu(i, 1)
                    else:
                        if not first and q - 1 in DOWN_AFTER:
                            act.wait_ge(d_filled, (i - 1) * UNITS_D + (DOWN_AFTER[q - 1][-1] + 1))
                        split_g(i, q - 1)
                    if q == 3 and not last:
                        split_gu(i + 1, 0)
                    if q == 4:
                        act.wait_ge(wd_in, i * 16 + 16)
                        nc.scalar.activation(wd_hi[:], raw_d, ACT.Copy).then_inc(wd_hi_done, 1)

            loop_pairs(act, body)
            split_g(PAIRS - 1, NP - 1)

        @block.vector
        def _(dve):
            dve.sem_inc(g_made, 2)
            dve.sem_inc(d_added, 3)
            dve.wait_ge(state_turned, 1)
            nc.vector.tensor_copy(past[:].rearrange("p c n -> p (c n)"), pd[0][:, 0:CHUNKS * 16]).then_inc(past_done, 1)

            def split_gu(i, k):
                dve.wait_ge(gu_hi_done, i * 2 + (k + 1))
                nc.vector.tensor_tensor(gu_lo[k][:], raw_gu, gu_hi[k][:].bitcast(F32), ALU.subtract).then_inc(gu_lo_done, 1)

            def split_g(i, q):
                k, (t0, w) = q // 3, PARTS[q % 3]
                dve.wait_ge(g_hi_done, i * NP + (q + 1))
                nc.vector.tensor_tensor(g_lo[:, k, t0:t0 + w], gated[q % 2][:, 0:w], g_hi[:, k, t0:t0 + w].bitcast(F32), ALU.subtract).then_inc(g_lo_done, 1)

            def add(i, units):
                for d in units:
                    tile, half = d // 2, d % 2
                    r = P if tile < TILES else NS
                    xs = x[0:r, tile, half * HALF:(half + 1) * HALF]
                    dve.wait_ge(d_filled, i * UNITS_D + (d + 1))
                    nc.vector.tensor_tensor(xs, pd[d % 3][0:r, :], xs, ALU.add).then_inc(d_added, 1)

            split_gu(0, 0)

            def body(i, first, last):
                for q in range(NP):
                    k, (t0, w) = q // 3, PARTS[q % 3]
                    c, u = conv[q % 2][:, 0:w], pu[q % 2][:, 0:w]
                    dve.wait_ge(copied, i * NP + (q + 1))
                    if q % 3 < 2:
                        taps_at = [ext[:, t0 + n:t0 + n + w] for n in range(2)]
                        cv = c
                    else:
                        taps_at = [ext_s[:, :, n:n + DT] for n in range(2)]
                        cv = c.rearrange("p (b s) -> p b s", s=DT)
                    nc.vector.scalar_tensor_tensor(out=cv, in0=taps_at[1], scalar=taps[:, k, 1:2], in1=cv, op0=ALU.mult, op1=ALU.add).then_inc(vchain, 1)
                    dve.wait_ge(vchain, i * NP + (q + 1))
                    nc.vector.scalar_tensor_tensor(out=cv, in0=taps_at[0], scalar=taps[:, k, 0:1], in1=cv, op0=ALU.mult, op1=ALU.add).then_inc(convolved, 1)
                    dve.wait_ge(silu_done, i * NP + (q + 1))
                    nc.vector.tensor_tensor(gated[q % 2][:, 0:w], c, u, ALU.mult).then_inc(g_made, 1)
                    if not first and q in DOWN_AFTER and q == 0:
                        split_g(i - 1, NP - 1)
                    if q > 0:
                        split_g(i, q - 1)
                    if not first and q in DOWN_AFTER:
                        add(i - 1, DOWN_AFTER[q])
                    if q == 0:
                        split_gu(i, 1)
                    if q == 3 and not last:
                        split_gu(i + 1, 0)
                    if q == 4:
                        dve.wait_ge(wd_hi_done, i + 1)
                        nc.vector.tensor_tensor(wd_lo[:], raw_d, wd_hi[:].bitcast(F32), ALU.subtract).then_inc(wd_lo_done, 1)

            loop_pairs(dve, body)
            split_g(PAIRS - 1, NP - 1)
            add(PAIRS - 1, range(UNITS_D))
            for n in range(6):
                w = (min(4 * n + 4, CHUNKS) - 4 * n) * P
                bank = (pa + pu)[n] if n < 4 else pa[n - 4]
                dve.wait_ge(kept_turned, n + 1)
                nc.vector.tensor_copy(raw[0:KEPT, 4 * n * P:4 * n * P + w], bank[0:KEPT, 0:w]).then_inc(kept_rows, 1)


def rope_table():
    half = ROT // 2
    inv = np.float32(500000.0) ** (np.float32(-2.0) * np.arange(half, dtype=np.float32) / np.float32(ROT))
    pos = np.concatenate([np.arange(SEQ), np.tile(PAST + np.arange(DT), DB)]).astype(np.float32)
    ang = (pos[:, None] * inv.astype(np.float32)[None, :]).astype(np.float64)
    c, s = np.cos(ang), np.sin(ang)
    return np.concatenate([c, c, -s, s], 1).astype(np.float32)


OUTS = {
    "y_prompt": (1, SEQ, D), "y_sample": (DB, DT, D),
    "cmp_prompt": (1, SEQ, 2, GA, E), "cmp_sample": (DB, DT, 2, GA, E),
    "slc_prompt": (1, SEQ, 2, GA, E), "slc_sample": (DB, DT, 2, GA, E),
    "win_prompt": (1, WIN, 2, GA, E), "win_sample": (DB, WIN, 2, GA, E),
    "dil_prompt": (1, SEQ, 2, HB, E), "dil_sample": (DB, PAST + DT, 2, HB, E),
    "conv_prompt": (1, CONV_W - 1, DFF), "conv_sample": (DB, CONV_W - 1, DFF),
}
SCRATCH = {"qa": (TOK, HA * E), "qb": (TOK, HB * E), "kvw": (TOK, 2 * GA * E), "gl": (TOK, 3 * HA), "kvc": (NS, 2, GA, E),
           "o": (SEQ, D), "oT": (P, KC, NS)}


def build(nc, t, o):
    scratch = {n: nc.dram_tensor("scratch_" + n, s, F32, kind="Internal").ap() for n, s in SCRATCH.items()}
    project(nc, t, o, scratch)
    attend(nc, t, o, scratch)
    finish(nc, t, o, scratch)


def kernel(**inputs):
    import concourse.bacc as bacc
    from concourse.bass_utils import run_bass_kernel_spmd

    x = {n: np.asarray(a) for n, a in inputs.items()}
    masks, smask = tables()
    across = lambda a, n: np.broadcast_to(a, (n,) + a.shape)
    gains = np.stack([x[n] for n in ("gq_a", "gk_cmp", "gk_slc", "gk_win", "gq_b", "gk_b")])
    data = {n: x[n] for n in ("x_prompt", "x_sample", "cache_cmp", "cache_slc", "state_win", "state_dil", "state_conv", "page_table",
                              "w_in", "w1_cmp_k", "w2_cmp_k", "w1_cmp_v", "w2_cmp_v", "w_o", "w_gate", "w_up", "w_down")}
    data.update(
        ident=np.eye(P, dtype=np.float32), rope=rope_table(), masks=masks, smask=smask,
        g_attn=x["g_attn"].reshape(KC, P).T, gains=across(gains, P), g_ffn=across(x["g_ffn"], P),
        peT=np.stack([x["pe_cmp_" + n].reshape(CMP_LEN * E // P, P).T for n in "kv"], 1),
        taps=np.concatenate([x["conv_w"], x["conv_b"][None]], 0).reshape(CONV_W + 1, CHUNKS, P).transpose(2, 1, 0))
    data = {n: np.ascontiguousarray(a) for n, a in data.items()}
    nc = bacc.Bacc("TRN2", target_bir_lowering=False, num_devices=1)
    t = {n: nc.dram_tensor("in_" + n, a.shape, mybir.dt.from_np(a.dtype), kind="ExternalInput").ap() for n, a in data.items()}
    o = {n: nc.dram_tensor("out_" + n, s, F32, kind="ExternalOutput").ap() for n, s in OUTS.items()}
    build(nc, t, o)
    r = run_bass_kernel_spmd(nc, [{"in_" + n: a for n, a in data.items()}], core_ids=[0])
    return tuple(r.results[0]["out_" + n] for n in OUTS)
```

```python
from contextlib import ExitStack

import numpy as np

import concourse.bass as bass
from concourse import mybir

F32 = mybir.dt.float32
F32R = mybir.dt.float32r
I32 = mybir.dt.int32
ALU = mybir.AluOpType
ACT = mybir.ActivationFunctionType
AX = mybir.AxisListType.X

P = 128
D = 1024
SEQ = 1024
DB = 8
DT = 8
PAST = 1024
NS = DB * DT
E = 64
HA = 8
HB = 8
GA = 2
RA = HA // GA
ROT = 16
EPS = 1e-6
DFF = 2816
IN_DIM = 2840
PAGE = 128
PAGES = PAST // PAGE
WIN = 512
CMP_STRIDE = 16
CMP_LEN = 32
SLC_BLK = 64
NCMP = PAST // CMP_STRIDE - 1
KC = D // P
TILES = SEQ // P
TOK = SEQ + NS
BIG = 1.0e30
CLAMP = 1.0e20
TINY = 1.0e-30


class Chain:

    def __init__(self, eng, sem):
        self.eng, self.sem, self.n, self.i, self.per = eng, sem, 0, None, 0

    def value(self):
        return self.n if self.i is None else self.i * self.per + self.n

    def step(self, ins):
        self.n += 1
        ins.then_inc(self.sem, 1)
        self.eng.wait_ge(self.sem, self.value())

    def enter(self, i, per, first=0):
        self.n -= first * per
        self.i, self.per, self.start = i, per, self.n

    def leave(self, trips):
        if self.n - self.start != self.per:
            raise ValueError(f"chain steps in a trip: {self.n - self.start}, not {self.per}")
        self.n = self.start + trips * self.per
        self.i = None


GROUPS = [
    ("qa", 0, 512, (2, 4), (0, 1)),
    ("cmp_slc", 512, 512, (2, 2), (1, 3)),
    ("win_gate", 1024, 280, (1, 2), (3, 4)),
    ("qb", 1304, 512, (2, 4), (4, 5)),
    ("kb", 1816, 512, (2, 4), (5, 6)),
    ("vb", 2328, 512, None, None),
]
NG = len(GROUPS)
STEPS = TILES + 1


def project(nc, t, o, scratch):
    with ExitStack() as ctx:
        sb = lambda name, shape, dt=F32: ctx.enter_context(nc.sbuf_tensor(name, shape, dt))
        ps = lambda name, shape: ctx.enter_context(nc.psum_tensor(name, shape, F32))
        sem = lambda name: ctx.enter_context(nc.semaphore(name))

        ident = sb("p_ident", [P, P])
        xin = sb("p_x", [P, 2, D])
        xsq = sb("p_xsq", [P, D])
        xss = sb("p_xss", [P, 2])
        xrt = sb("p_xrt", [P, 2])
        xrr = sb("p_xrr", [P, 2])
        xnT = sb("p_xnT", [P, KC, TOK])
        g_in = sb("p_gin", [P, KC])
        gains = sb("p_gains", [P, 6, E])
        rope = sb("p_rope", [P, STEPS, 2 * ROT])
        epst = sb("p_eps", [P, 1])
        raw = sb("p_raw", [P, KC, 512])
        w_hi = sb("p_whi", [P, 2, KC, 512], F32R)
        w_lo = sb("p_wlo", [P, 2, KC, 512], F32R)
        x_hi = sb("p_xhi", [P, 2, KC, P], F32R)
        x_lo = sb("p_xlo", [P, 2, KC, P], F32R)
        z = sb("p_z", [P, 2, 512])
        zsq = sb("p_zsq", [P, 2, 512])
        zss = sb("p_zss", [P, 2, 8])
        zrt = sb("p_zrt", [P, 2, 8])
        zrr = sb("p_zrr", [P, 2, 8])
        ra = sb("p_ra", [P, 8 * ROT])
        rb = sb("p_rb", [P, 8 * ROT])
        pt = [ps(f"p_pt{k}", [P, D]) for k in range(2)]
        pz = [ps(f"p_pz{k}", [P, 512]) for k in range(2)]

        const_in = sem("p_const_in")
        x_in = [sem(f"p_x_in{k}") for k in range(2)]
        x_square = sem("p_x_square")
        x_root = sem("p_x_root")
        x_normed = sem("p_x_normed")
        x_turned = sem("p_x_turned")
        x_stored = sem("p_x_stored")
        eps_set = sem("p_eps_set")
        raw_in = sem("p_raw_in")
        w_hi_done = sem("p_w_hi_done")
        w_lo_done = sem("p_w_lo_done")
        x_hi_done = sem("p_x_hi_done")
        x_lo_done = sem("p_x_lo_done")
        z_summed = sem("p_z_summed")
        z_copied = sem("p_z_copied")
        z_squared = sem("p_z_squared")
        z_reduced = sem("p_z_reduced")
        z_root = sem("p_z_root")
        z_done = sem("p_z_done")
        z_out = [sem(f"p_z_out{k}") for k in range(2)]
        vchain = sem("p_vchain")

        SAMPLE = TILES // 2

        def rows(i):
            return NS if isinstance(i, int) and i == SAMPLE else P

        def tokens(i, k):
            if isinstance(i, int):
                return slice((2 * i + k) * P, (2 * i + k) * P + rows(i))
            return bass.ds(i * (2 * P) + k * P, P)

        def loop_tiles(eng, body, chain=None, per=0):
            with eng.Fori(0, 3) as i:
                if chain:
                    chain.enter(i, per)
                body(i, 0)
                body(i, 1)
            if chain:
                chain.leave(3)
            body(3, 0)
            body(3, 1)
            body(SAMPLE, 0)

        def normed(G, i, k):
            return sum(g[3] is not None for g in GROUPS[:G]) * STEPS + i * 2 + k + 1

        def stores(G):
            return 1 if GROUPS[G][3] is not None and GROUPS[G][0] in ("qa", "qb", "kb") or GROUPS[G][0] == "vb" else 2

        def stored_before(G, i, k):
            slot = (G + k) % 2
            before = sum(16 * stores(g) * (5 if (slot - g) % 2 == 0 else 4) for g in range(G))
            return i * (16 * stores(G)) + (before + 1)

        block = ctx.enter_context(nc.Block())

        @block.sync
        def _(sp):
            sp.sem_inc(z_out[0], 1)
            sp.sem_inc(z_out[1], 1)
            sp.dma_start(ident[:], t["ident"]).then_inc(const_in, 16)
            sp.dma_start(g_in[:], t["g_attn"]).then_inc(const_in, 16)
            sp.dma_start(gains[:], t["gains"]).then_inc(const_in, 16)
            sp.dma_start(rope[:, 0:TILES, :], t["rope"][0:SEQ, :].rearrange("(a p) c -> p a c", p=P)).then_inc(const_in, 16)
            sp.dma_start(rope[0:NS, TILES, :], t["rope"][SEQ:TOK, :]).then_inc(const_in, 16)
            for n in range(STEPS):
                r = P if n < TILES else NS
                src = t["x_prompt"][0, n * P:(n + 1) * P, :] if n < TILES else t["x_sample"].rearrange("b t d -> (b t) d")
                if n >= 2:
                    sp.wait_ge(x_turned, n - 1)
                sp.dma_start(xin[0:r, n % 2, :], src).then_inc(x_in[n % 2], 16)
                if n == 1:
                    sp.dma_start(raw[:], t["w_in"][:, 0:512].rearrange("(c p) n -> p c n", p=P)).then_inc(raw_in, 16)
            for G, (name, c0, wd, heads, _) in enumerate(GROUPS):
                if G + 1 < NG:
                    sp.wait_ge(w_lo_done, KC * (G + 1))
                    c1, w1 = GROUPS[G + 1][1:3]
                    sp.dma_start(raw[:, :, 0:w1], t["w_in"][:, c1:c1 + w1].rearrange("(c p) n -> p c n", p=P)).then_inc(raw_in, 16)

                def store_tile(i, k, G=G, name=name, heads=heads):
                    slot = (G + k) % 2
                    r = rows(i)
                    last = r == NS
                    if heads is not None:
                        sp.wait_ge(z_done, normed(G, i, k))
                    else:
                        sp.wait_ge(z_copied, i * 2 + (k + G * STEPS + 3))
                    tok = slice(0, NS) if last else tokens(i, k)
                    src = z[0:r, slot, :]
                    if name in ("qa", "qb"):
                        sp.dma_start(scratch[name][tokens(i, k), :], src).then_inc(z_out[slot], 16)
                    elif name == "win_gate":
                        sp.dma_start(scratch["kvw"][tokens(i, k), :], src[:, 0:256]).then_inc(z_out[slot], 16)
                        sp.dma_start(scratch["gl"][tokens(i, k), :], src[:, 256:280]).then_inc(z_out[slot], 16)
                    elif name == "cmp_slc":
                        for j, x in enumerate(("cmp", "slc")):
                            dst = o[x + ("_sample" if last else "_prompt")].rearrange("b s c g e -> (b s) (c g e)")
                            sp.dma_start(dst[tok, :], src[:, 256 * j:256 * j + 256]).then_inc(z_out[slot], 16)
                    else:
                        c = 0 if name == "kb" else 1
                        if last:
                            sp.dma_start(o["dil_sample"][:, PAST:PAST + DT, c, :, :].rearrange("b s h e -> b s (h e)"),
                                         src).then_inc(z_out[slot], 16)
                        else:
                            sp.dma_start(o["dil_prompt"][0, tok, c, :, :].rearrange("s h e -> s (h e)"), src).then_inc(z_out[slot], 16)

                loop_tiles(sp, store_tile)
            for k in range(2):
                sp.wait_ge(z_out[k], 1 + sum(16 * stores(g) * (5 if (k - g) % 2 == 0 else 4) for g in range(NG)))

        @block.gpsimd
        def _(pool):
            nc.gpsimd.memset(epst[:], EPS).then_inc(eps_set, 1)

        @block.scalar
        def _(act):
            act.sem_inc(z_copied, 2)
            act.wait_ge(eps_set, 1)
            for n in range(STEPS):
                r, s = (P if n < TILES else NS), slice(n % 2, n % 2 + 1)
                act.wait_ge(x_in[n % 2], 16 * (n // 2 + 1))
                if n >= 2:
                    act.wait_ge(x_normed, n - 1)
                if n >= 1:
                    act.wait_ge(x_square, n)
                nc.scalar.activation(xsq[0:r, :], xin[0:r, n % 2, :], ACT.Square, accum_out=xss[0:r, s]).then_inc(x_square, 1)
                act.wait_ge(x_square, n + 1)
                nc.scalar.activation(xrt[0:r, s], xss[0:r, s], ACT.Sqrt, bias=epst[0:r, :], scale=1.0 / D).then_inc(x_root, 1)
            act.wait_ge(raw_in, 16)
            for c in range(KC):
                nc.scalar.activation(w_hi[:, 0, c, :], raw[:, c, :], ACT.Copy).then_inc(w_hi_done, 1)

            def split_x(slot, i, k):
                r = rows(i)
                nc.scalar.activation(x_hi[:, slot, :, 0:r], xnT[:, :, tokens(i, k)], ACT.Copy).then_inc(x_hi_done, 1)

            act.wait_ge(x_stored, STEPS)
            split_x(0, 0, 0)
            split_x(1, 0, 1)
            for G, (name, c0, wd, heads, _) in enumerate(GROUPS):
                def tile(i, k, G=G, heads=heads, wd=wd):
                    slot = (G + k) % 2
                    r = rows(i)
                    act.wait_ge(z_summed, i * 2 + (k + G * STEPS + 1))
                    act.wait_ge(z_out[slot], stored_before(G, i, k))
                    nc.scalar.activation(z[0:r, slot, 0:wd], pz[slot][0:r, 0:wd], ACT.Copy).then_inc(z_copied, 1)
                    if r == NS:
                        i2, k2, more = 0, 1, G + 1 < NG
                    elif isinstance(i, int) and k == 1:
                        i2, k2, more = 0, 0, G + 1 < NG
                    else:
                        i2, k2, more = i + 1, k, True
                    if more:
                        split_x(slot, i2, k2)
                    if heads is not None:
                        a, h = heads
                        act.wait_ge(z_copied, i * 2 + (k + G * STEPS + 3))
                        nc.scalar.activation(zsq[0:r, slot, 0:a * h * E].rearrange("p (a h e) -> p a h e", h=h, e=E),
                                             z[0:r, slot, 0:a * 256].rearrange("p (a h e) -> p a h e", h=4, e=E)[:, :, 0:h, :],
                                             ACT.Square).then_inc(z_squared, 1)
                    if G + 1 < NG and r == P:
                        w = GROUPS[G + 1][2]
                        if k == 0:
                            act.wait_ge(raw_in, 16 * (G + 2))
                        cs = bass.ds(i * 2 + k, 1)
                        nc.scalar.activation(w_hi[:, (G + 1) % 2, cs, 0:w], raw[:, cs, 0:w], ACT.Copy).then_inc(w_hi_done, 1)
                    if heads is not None:
                        a, h = heads
                        act.wait_ge(z_reduced, normed(G, i, k))
                        nc.scalar.activation(zrt[0:r, slot, 0:a * h], zss[0:r, slot, 0:a * h], ACT.Sqrt,
                                             bias=epst[0:r, :], scale=1.0 / E).then_inc(z_root, 1)

                loop_tiles(act, tile)

        @block.tensor
        def _(pe):
            pe.wait_ge(const_in, 80)
            for n in range(STEPS):
                r = P if n < TILES else NS
                pe.wait_ge(x_normed, n + 1)
                if n >= 2:
                    pe.wait_ge(x_stored, n - 1)
                for c in range(KC):
                    last = nc.tensor.transpose(pt[n % 2][:, c * P:c * P + r], xin[0:r, n % 2, c * P:(c + 1) * P], ident[0:r, 0:r])
                last.then_inc(x_turned, 1)
            for G, (name, c0, wd, heads, _) in enumerate(GROUPS):
                pe.wait_ge(w_lo_done, KC * (G + 1))

                def tile(i, k, G=G, wd=wd):
                    slot = (G + k) % 2
                    r = rows(i)
                    pe.wait_ge(x_lo_done, i * 2 + (k + G * STEPS + 1))
                    pe.wait_ge(z_copied, i * 2 + (k + G * STEPS + 1))
                    for j, (xs, ws) in enumerate(((x_hi, w_hi), (x_hi, w_lo), (x_lo, w_hi))):
                        for c in range(KC):
                            last = nc.tensor.matmul(pz[slot][0:r, 0:wd], xs[:, slot, c, 0:r], ws[:, G % 2, c, 0:wd],
                                                    start=(j == 0 and c == 0), stop=(j == 2 and c == KC - 1))
                    last.then_inc(z_summed, 1)

                loop_tiles(pe, tile)

        @block.vector
        def _(dve):
            chain = Chain(dve, vchain)
            dve.wait_ge(const_in, 80)
            for g in (0, 4):
                chain.step(nc.vector.tensor_scalar(gains[:, g, :], gains[:, g, :], -(E ** -0.5), None, ALU.mult))
            for n in range(STEPS):
                r, s = (P if n < TILES else NS), slice(n % 2, n % 2 + 1)
                dve.wait_ge(x_root, n + 1)
                chain.step(nc.vector.reciprocal(xrr[0:r, s], xrt[0:r, s]))
                nc.vector.tensor_scalar(xin[0:r, n % 2, :], xin[0:r, n % 2, :], xrr[0:r, s], None, ALU.mult).then_inc(x_normed, 1)
                dve.wait_ge(x_turned, n + 1)
                nc.vector.tensor_tensor(xnT[:, :, n * P:n * P + r], pt[n % 2][:, :].rearrange("p (c q) -> p c q", c=KC)[:, :, 0:r],
                                        g_in[:, :].unsqueeze(2).to_broadcast([P, KC, r]), ALU.mult).then_inc(x_stored, 1)
            for c in range(KC):
                dve.wait_ge(w_hi_done, c + 1)
                nc.vector.tensor_tensor(w_lo[:, 0, c, :], raw[:, c, :], w_hi[:, 0, c, :].bitcast(F32), ALU.subtract).then_inc(w_lo_done, 1)

            def split_x(slot, i, k, n):
                r = rows(i)
                dve.wait_ge(x_hi_done, n)
                nc.vector.tensor_tensor(x_lo[:, slot, :, 0:r], xnT[:, :, tokens(i, k)], x_hi[:, slot, :, 0:r].bitcast(F32),
                                        ALU.subtract).then_inc(x_lo_done, 1)

            dve.wait_ge(x_stored, STEPS)
            split_x(0, 0, 0, 1)
            split_x(1, 0, 1, 2)
            for G, (name, c0, wd, heads, grow) in enumerate(GROUPS):
                def tile(i, k, G=G, heads=heads, wd=wd, grow=grow):
                    slot = (G + k) % 2
                    r = rows(i)
                    if r == NS:
                        i2, k2, more = 0, 1, G + 1 < NG
                    elif isinstance(i, int) and k == 1:
                        i2, k2, more = 0, 0, G + 1 < NG
                    else:
                        i2, k2, more = i + 1, k, True
                    if more:
                        split_x(slot, i2, k2, i * 2 + (k + G * STEPS + 3))
                    if heads is not None:
                        a, h = heads
                        zs3 = zss[0:r, slot, 0:a * h]
                        dve.wait_ge(z_squared, normed(G, i, k))
                        nc.vector.reduce_sum(zs3, zsq[0:r, slot, 0:a * h * E].rearrange("p (h e) -> p h e", e=E), AX).then_inc(z_reduced, 1)
                    if G + 1 < NG and r == P:
                        w = GROUPS[G + 1][2]
                        cs = bass.ds(i * 2 + k, 1)
                        dve.wait_ge(w_hi_done, i * 2 + (k + KC * (G + 1) + 1))
                        nc.vector.tensor_tensor(w_lo[:, (G + 1) % 2, cs, 0:w], raw[:, cs, 0:w], w_hi[:, (G + 1) % 2, cs, 0:w].bitcast(F32),
                                                ALU.subtract).then_inc(w_lo_done, 1)
                    if heads is not None:
                        zv = z[0:r, slot, 0:a * 256].rearrange("p (a h e) -> p a h e", h=4, e=E)[:, :, 0:h, :]
                        dve.wait_ge(z_root, normed(G, i, k))
                        chain.step(nc.vector.reciprocal(zrr[0:r, slot, 0:a * h], zrt[0:r, slot, 0:a * h]))
                        rr = zrr[0:r, slot, 0:a * h].rearrange("p (a h) -> p a h", a=a).unsqueeze(3)
                        chain.step(nc.vector.tensor_tensor(zv, zv, rr.to_broadcast([r, a, h, E]), ALU.mult))
                        gv = gains[0:r, grow[0]:grow[1], :].unsqueeze(2)
                        if grow[1] - grow[0] == 1 and a == 2:
                            for b in range(2):
                                ins = nc.vector.tensor_tensor(zv[:, b], zv[:, b], gv[:, 0].to_broadcast([r, h, E]), ALU.mult)
                                if b == 1:
                                    chain.step(ins)
                        else:
                            chain.step(nc.vector.tensor_tensor(zv, zv, gv.to_broadcast([r, a, h, E]), ALU.mult))
                        tile_at = (2 * i + k) if isinstance(i, int) else None
                        ct = rope[0:r, tile_at if tile_at is not None else bass.ds(i * 2 + k, 1), :]
                        if tile_at is None:
                            ct = ct.rearrange("p a c -> p (a c)")
                        bc = lambda x, w: x.unsqueeze(1).to_broadcast([r, h, w])
                        n_ops = []
                        for b in range(a):
                            v = zv[:, b]
                            va = ra[0:r, b * 4 * ROT:b * 4 * ROT + h * ROT].rearrange("p (h c) -> p h c", c=ROT)
                            vb = rb[0:r, b * 4 * ROT:b * 4 * ROT + h * ROT].rearrange("p (h c) -> p h c", c=ROT)
                            nc.vector.tensor_tensor(va, v[:, :, 0:ROT], bc(ct[:, 0:ROT], ROT), ALU.mult)
                            nc.vector.tensor_tensor(vb[:, :, 0:8], v[:, :, 8:16], bc(ct[:, 16:24], 8), ALU.mult)
                            ins = nc.vector.tensor_tensor(vb[:, :, 8:16], v[:, :, 0:8], bc(ct[:, 24:32], 8), ALU.mult)
                            if b == a - 1:
                                chain.step(ins)
                            n_ops.append((v, va, vb))
                        for b, (v, va, vb) in enumerate(n_ops):
                            ins = nc.vector.tensor_tensor(v[:, :, 0:ROT], va, vb, ALU.add)
                            if b == a - 1:
                                ins.then_inc(z_done, 1)

                loop_tiles(dve, tile, chain, per=8 if heads is not None else 0)

def dil_bias(delta):
    mult = sum(((delta >= 0) & (delta <= w) & (delta % d == 0)).astype(np.float64) for w, d in ((128, 1), (512, 4), (2048, 16)))
    return np.where(mult > 0, -np.log(np.maximum(mult, 1.0)), BIG).astype(np.float32)


def tables():
    p = np.arange(P)[:, None]
    c = np.arange(SEQ)[None, :]
    d = p + (SEQ - P) - c
    m_dil = dil_bias(d)
    m_slc = np.where(d >= 0, 0.0, BIG)
    dw = p + WIN - np.arange(WIN + P)[None, :]
    m_win = np.where((dw >= 0) & (dw < WIN), 0.0, BIG)
    t = (np.arange(TILES)[None, :, None] * P + np.arange(P)[:, None, None])
    n = np.arange(NCMP + 1)[None, None, :]
    m_cmp = np.where((n < NCMP) & (n * CMP_STRIDE + CMP_LEN - 1 <= t), 0.0, BIG).reshape(P, -1)
    masks = np.concatenate([m_dil, m_slc, m_win, m_cmp], 1).astype(np.float32)
    tt = np.tile(np.arange(DT), 8)[:, None]
    col = np.arange(PAST)[None, :]
    key = (col % P) * (PAST // P) + col // P
    s_dil = dil_bias(PAST + tt - np.concatenate([key, PAST + np.arange(DT)[None, :]], 1))
    wc = np.arange(WIN)[None, :]
    widx = np.concatenate([(wc % P) * (WIN // P) + wc // P, WIN + np.arange(DT)[None, :]], 1)
    dw = PAST + tt - (PAST - WIN + widx)
    s_win = np.where((dw >= 0) & (dw < WIN), 0.0, BIG)
    s_new = np.where(np.arange(DT)[None, :] <= tt, 0.0, BIG)
    s_zero = np.zeros((NS, NCMP + 1))
    blocks = np.tile(np.arange(PAST // SLC_BLK)[None, :], (NS, 1))
    ci = np.arange(NS)[:, None] * CMP_STRIDE
    sj = np.arange(PAST // SLC_BLK)[None, :] * SLC_BLK
    overlap = ((ci < sj + SLC_BLK) & (ci + CMP_LEN > sj) & (np.arange(NS)[:, None] < NCMP))
    row = np.arange(NS)
    same = (row[:, None] // (RA * DT) == row[None, :] // (RA * DT)) & (row[:, None] % DT == row[None, :] % DT)
    sample = np.concatenate([s_dil, s_win, s_new, s_zero, blocks, overlap, same], 1).astype(np.float32)
    return masks, sample


M_SLC, M_WIN, M_CMP = SEQ, 2 * SEQ, 2 * SEQ + WIN + P
M_ALL = M_CMP + TILES * (NCMP + 1)
S_WIN = PAST + DT
S_NEW = S_WIN + WIN + DT
S_ZERO = S_NEW + DT
S_BLK = S_ZERO + NCMP + 1
S_OVER = S_BLK + PAST // SLC_BLK
S_SAME = S_OVER + PAST // SLC_BLK
S_ALL = S_SAME + NS
NBLK = PAST // SLC_BLK
GELU_C = 0.7978845608028654


def attend(nc, t, o, scratch):
    with ExitStack() as outer:
        osb = lambda name, shape, dt=F32: outer.enter_context(nc.sbuf_tensor(name, shape, dt))
        ident = osb("a_ident", [P, P])
        w1 = osb("a_w1", [P, 2, 16, P])
        w2 = osb("a_w2", [P, 2, E])
        pe_bias = osb("a_pe_bias", [P, 2])
        q_dil_T = osb("a_q_dil_T", [P, 4, NS])
        q_nsa_T = osb("a_q_nsa_T", [P, RA, NS])
        gate_p = osb("a_gate_p", [P, TILES, 3 * HA])
        gate_s = osb("a_gate_s", [NS, DB, 3])
        compress_prompt(nc, t, o, scratch, ident, w1, w2, pe_bias, q_dil_T, q_nsa_T, gate_p, gate_s)
        attend_loop(nc, t, o, scratch, ident, w1, w2, pe_bias, q_dil_T, q_nsa_T, gate_p, gate_s)


def compress_prompt(nc, t, o, scratch, ident, w1, w2, pe_bias, q_dil_T, q_nsa_T, gate_p, gate_s):
    with ExitStack() as ctx:
        sb = lambda name, shape, dt=F32: ctx.enter_context(nc.sbuf_tensor(name, shape, dt))
        sem = lambda name: ctx.enter_context(nc.semaphore(name))
        rows16 = sb("c_rows16", [NS, 4096])
        xT = sb("c_xT", [P, 2, GA, 8, NS])
        peT = sb("c_peT", [P, 2, 16])
        qn = sb("c_qn", [NS, 2, 512])
        h = sb("c_h", [P, 2, GA * NS])
        u = sb("c_u", [P, 2, GA * NS])
        kv = sb("c_kv", [NS, 2, GA, E])
        turned = [ctx.enter_context(nc.psum_tensor(f"c_turned{k}", [P, 512], F32)) for k in range(6)]
        hidden = ctx.enter_context(nc.psum_tensor("c_hidden", [P, 2, GA, NS], F32))
        small = ctx.enter_context(nc.psum_tensor("c_small", [P, 512], F32))
        loaded, rows_in, t_filled, v = sem("c_loaded"), sem("c_rows_in"), sem("c_t_filled"), sem("c_v")
        pe_done, hid_done, tanh_in, tanh_done, kv_done, kv_copied, kv_out, gates_in = (
            sem("c_" + x) for x in ("pe_done", "hid_done", "tanh_in", "tanh_done", "kv_done", "kv_copied", "kv_out", "gates_in"))
        block = ctx.enter_context(nc.Block())

        @block.sync
        def _(sp):
            for c in range(4):
                sp.dma_start(rows16[:, c * 1024:(c + 1) * 1024].rearrange("n (r e) -> n r e", e=E),
                             o["cmp_prompt"].rearrange("b (n r) c g e -> (b n) r (c g) e", r=CMP_STRIDE)[:, :, c, :]).then_inc(rows_in, 16)
            sp.dma_start(ident[:], t["ident"]).then_inc(loaded, 16)
            for c, x in enumerate("kv"):
                sp.dma_start(w1[:, c], t["w1_cmp_" + x].rearrange("(j p) f -> p j f", p=P)).then_inc(loaded, 16)
                sp.dma_start(w2[:, c], t["w2_cmp_" + x]).then_inc(loaded, 16)
            sp.dma_start(peT[:], t["peT"]).then_inc(loaded, 16)
            sp.dma_start(qn[:, 0, :], scratch["qb"][SEQ:TOK, :]).then_inc(loaded, 16)
            for g in range(GA):
                sp.dma_start(qn[:, 1, :].rearrange("p (r g e) -> p r g e", g=GA, e=E)[:, :, g, :],
                             scratch["qa"][SEQ:TOK, g * RA * E:(g + 1) * RA * E].rearrange("p (r e) -> p r e", e=E)).then_inc(loaded, 16)
            sp.dma_start(gate_p[:], scratch["gl"][0:SEQ, :].rearrange("(a p) c -> p a c", p=P)).then_inc(gates_in, 16)
            for b in range(DB):
                sp.dma_start(gate_s[:, b, :], scratch["gl"][SEQ + b * DT:SEQ + (b + 1) * DT, :].rearrange("s (h c) -> h s c", c=3)).then_inc(gates_in, 16)
            sp.wait_ge(kv_copied, 4)
            sp.dma_start(scratch["kvc"], kv[:]).then_inc(kv_out, 16)
            sp.wait_ge(kv_out, 16)

        LOADS = 16 * 9

        @block.tensor
        def _(pe):
            pe.wait_ge(loaded, LOADS)
            for n in range(2):
                for j in range(4):
                    src = qn[:, n, j * P:(j + 1) * P]
                    last = nc.tensor.transpose(turned[4 + n][:, j * NS:(j + 1) * NS], src, ident[0:NS, 0:NS])
                last.then_inc(t_filled, 1)
            pe.wait_ge(rows_in, 64)
            for n in range(4):
                c, g = n // 2, n % 2
                for rp in range(8):
                    src = rows16[:, n * 1024 + rp * P:n * 1024 + (rp + 1) * P]
                    last = nc.tensor.transpose(turned[n][:, rp * NS:(rp + 1) * NS], src, ident[0:NS, 0:NS])
                last.then_inc(t_filled, 1)
            for c in range(2):
                for j in range(16):
                    last = nc.tensor.matmul(small[:, c:c + 1], w1[:, c, j, :], peT[:, c, j:j + 1], start=(j == 0), stop=(j == 15))
            last.then_inc(pe_done, 1)
            pe.wait_ge(v, 6)
            for c in range(2):
                for j in range(16):
                    at = j // 8
                    last = nc.tensor.matmul(hidden[:, c, :, 0:NCMP], w1[:, c, j, :], xT[:, c, :, j % 8, at:at + NCMP],
                                            start=(j == 0), stop=(j == 15))
            last.then_inc(hid_done, 1)
            pe.wait_ge(v, 13)
            for c in range(2):
                for g in range(GA):
                    hg = u[:, c, :].rearrange("p (g n) -> p g n", g=GA)[:, g, 0:NCMP]
                    last = nc.tensor.matmul(small[0:NCMP, 128 + (c * GA + g) * E:128 + (c * GA + g + 1) * E], hg, w2[:, c, :], start=True, stop=True)
            last.then_inc(kv_done, 1)

        @block.scalar
        def _(act):
            act.wait_ge(tanh_in, 1)
            uv = u[:].rearrange("p c (g n) -> p (c g) n", g=GA)[:, :, 0:NCMP]
            nc.scalar.activation(uv, uv, ACT.Tanh, scale=GELU_C).then_inc(tanh_done, 1)
            act.wait_ge(gates_in, 16 * (1 + DB))
            nc.scalar.activation(gate_p[:], gate_p[:], ACT.Exp, scale=-1.0).then_inc(tanh_done, 1)
            nc.scalar.activation(gate_s[:], gate_s[:], ACT.Exp, scale=-1.0).then_inc(tanh_done, 1)

        @block.vector
        def _(dve):
            ch = Chain(dve, v)
            nc.vector.memset(kv[:], 0.0).then_inc(kv_copied, 1)
            dve.wait_ge(t_filled, 2)
            ch.step(nc.vector.tensor_copy(q_dil_T[:].rearrange("p a n -> p (a n)"), turned[4][:, 0:4 * NS]))
            ch.step(nc.vector.tensor_copy(q_nsa_T[:].rearrange("p a n -> p (a n)"), turned[5][:, 0:4 * NS]))
            for n in range(4):
                dve.wait_ge(t_filled, 3 + n)
                ch.step(nc.vector.tensor_copy(xT[:, n // 2, n % 2].rearrange("p a n -> p (a n)"), turned[n][:, :]))
            dve.wait_ge(pe_done, 1)
            ch.step(nc.vector.tensor_copy(pe_bias[:], small[:, 0:2]))
            ch.step(nc.vector.tensor_scalar(w2[:], w2[:], 0.5, None, ALU.mult))
            dve.wait_ge(hid_done, 1)
            hv = [x[:].rearrange("p c (g n) -> p c g n", g=GA)[:, :, :, 0:NCMP] for x in (h, u)]
            for c in range(2):
                ins = nc.vector.tensor_scalar(hv[0][:, c], hidden[:, c, :, 0:NCMP], pe_bias[:, c:c + 1], None, ALU.add)
            ch.step(ins)
            hv = [x.rearrange("p c g n -> p (c g) n") for x in hv]
            ch.step(nc.vector.tensor_tensor(hv[1], hv[0], hv[0], ALU.mult))
            ch.step(nc.vector.tensor_scalar(hv[1], hv[1], 0.044715, 1.0, ALU.mult, ALU.add))
            nc.vector.tensor_tensor(hv[1], hv[1], hv[0], ALU.mult).then_inc(tanh_in, 1)
            dve.wait_ge(tanh_done, 1)
            ch.step(nc.vector.tensor_scalar(hv[1], hv[1], 1.0, None, ALU.add))
            ch.step(nc.vector.tensor_tensor(hv[1], hv[1], hv[0], ALU.mult))
            dve.wait_ge(kv_done, 1)
            dve.wait_ge(kv_copied, 1)
            nc.vector.tensor_copy(kv[0:NCMP].rearrange("p c g e -> p (c g e)"), small[0:NCMP, 128:384]).then_inc(kv_copied, 1)
            dve.wait_ge(tanh_done, 3)
            for x in (gate_p, gate_s):
                ch.step(nc.vector.tensor_scalar(x[:], x[:], 1.0, None, ALU.add))
                nc.vector.reciprocal(x[:], x[:]).then_inc(kv_copied, 1)


UNITS = ([("d", j) for j in range(8)] + [("sd", 0)] + [("l", j) for j in range(8)]
         + [("w", 0), ("w", 1), ("w", 2), ("w", 3), ("sc", 0)] + [("w", j) for j in range(4, 8)]
         + [("c", 0), ("c", 1), ("c", 2), ("sl", 0), ("c", 3), ("sw", 0)] + [("c", j) for j in range(4, 8)])
NU = len(UNITS)
BRANCH = {"d": 0, "l": 1, "w": 2, "c": 3}
NEXT = 4
EXTRAS = {s: [] for s in range(NU + 4)}
for _j in range(8):
    EXTRAS[_j].append(("kd", _j, [0]))
EXTRAS[3].append(("new", 0, [0]))
for _j in range(3):
    EXTRAS[9 + _j].append(("ksw", _j, [0]))
for _j in range(4):
    EXTRAS[12 + _j].append(("xt", _j, [0]))
for _s, _j in ((14, 0), (15, 1), (17, 2), (18, 3)):
    EXTRAS[_s].append(("hid", _j, []))
EXTRAS[20].append(("ckv", 0, []))
EXTRAS[24].append(("sel1", 0, []))
EXTRAS[26].append(("sel2", 0, []))
for _b, _s, _n in ((1, 5, 3), (2, 15, 2), (3, 23, 1), (NEXT, 28, 3)):
    for _k in range(_n):
        EXTRAS[_s + _k].append(("prep", _b, [2 * _k, 2 * _k + 1]))
SPLIT_AT = {3: 1, 13: 2, 21: 3, 26: NEXT}
PREP_CHUNKS = 6
X_USERS = ["sd", "hid", "ckv", "sel1", "sel2", "sl"]
FIRST, MID, LAST = range(3)


def key_blocks(kind, j):
    if kind in "dl":
        return 0, j + 1
    if kind == "w":
        return max(0, j - WIN // P), j + 1
    return 0, 1


def unit_chunks(n):
    kind, j = UNITS[n]
    if kind[0] == "s":
        return 2
    a, b = key_blocks(kind, j)
    return -(-(b - a) // 4)


def there(phase, n):
    return n < NU and (n >= 0 or phase != FIRST)


def stages(phase):
    return range(NU + 4 if phase == LAST else NU)


def extras(phase, s):
    return [e for e in EXTRAS[s] if s < NU and not (phase == LAST and e[:2] == ("prep", NEXT))]


def plan(phase):
    T, U = {}, {}
    for s in stages(phase):
        n = s - 2
        if there(phase, n):
            for q in range(unit_chunks(n)):
                T["tr", n, q] = len(T)
                U[n, q] = len(U)
        for name, j, qs in extras(phase, s):
            for q in qs:
                T[name, j, q] = len(T)
    return T, U


def attend_loop(nc, t, o, scratch, ident, w1, w2, pe_bias, q_dil_T, q_nsa_T, gate_p, gate_s):
    tables_ = [plan(phase) for phase in range(3)]
    T, U = [x[0] for x in tables_], [x[1] for x in tables_]
    NT, NCH = len(T[MID]), len(U[MID])
    assert NT % 2 == 0 and NCH % 4 == 0 and NU % 4 == 0
    T_SHIFT = [PREP_CHUNKS, PREP_CHUNKS + len(T[FIRST]) - NT, PREP_CHUNKS + len(T[FIRST]) - NT]
    U_SHIFT = [0, len(U[FIRST]) - NCH, len(U[FIRST]) - NCH]
    with ExitStack() as ctx:
        sb = lambda name, shape, dt=F32: ctx.enter_context(nc.sbuf_tensor(name, shape, dt))
        sem = lambda name: ctx.enter_context(nc.semaphore(name))
        masks = sb("l_masks", [P, M_ALL])
        smask = sb("l_smask", [NS, S_ALL])
        q_nat = [sb(f"l_q_nat{k}", [P, TILES, E]) for k in range(2)]
        kv_nat = [sb(f"l_kv_nat{k}", [P if k < 3 else NS, TILES if k < 3 else 1, 2, E]) for k in range(4)]
        q_split = sb("l_q_split", [P, TILES, 2 * E], F32R)
        k_split = sb("l_k_split", [P, TILES, 3 * E], F32R)
        qT = [sb(f"l_qT{k}", [P, SEQ], F32R) for k in range(2)]
        kA = [sb(f"l_kA{k}", [P, SEQ], F32R) for k in range(2)]
        kB = [sb(f"l_kB{k}", [P, SEQ], F32R) for k in range(2)]
        e_ring = sb("l_e", [P, 4, PAST + DT])
        e_gated = sb("l_e_gated", [NS, NS])
        p_ring = sb("l_p", [P, 4, 512])
        nmin = sb("l_nmin", [P, 4])
        nmin2 = sb("l_nmin2", [NS, 1])
        total = sb("l_total", [P, 4])
        rtot = sb("l_rtot", [P, 4])
        acc = [sb(f"l_acc{k}", [P, TILES, E]) for k in range(2)]
        gate_h = sb("l_gate_h", [P, TILES, 3])
        gate_b = sb("l_gate_b", [NS, 3])
        kd_k = sb("l_kd_k", [P, 8, 512])
        kd_v = sb("l_kd_v", [P, 8, 512])
        rows_nat = kd_k[0:NS].rearrange("p j n -> p (j n)")
        kd_new = sb("l_kd_new", [DT, 1024])
        ks = sb("l_ks", [P, PAGES, 256])
        kw = sb("l_kw", [P, WIN // P, 256])
        ks_new = sb("l_ks_new", [DT, 256])
        kw_new = sb("l_kw_new", [DT, 256])
        kd_T = sb("l_kd_T", [P, 4, PAST])
        rows16 = kd_T[0:NS].rearrange("p a n -> p (a n)")
        ks_T = sb("l_ks_T", [P, PAST])
        kw_T = sb("l_kw_T", [P, WIN])
        new_T = sb("l_new_T", [P, 6, DT])
        xT = sb("l_xT", [P, 2, GA, 8, NS])
        hh = sb("l_hh", [P, 2 * GA, NS])
        hu = sb("l_hu", [P, 2 * GA, NS])
        kc_T = sb("l_kc_T", [P, NCMP])
        vc = sb("l_vc", [NCMP, P])
        bd_dil = sb("l_bd_dil", [P, 4 * 80])
        bd_nsa = sb("l_bd_nsa", [P, NS])
        sel = sb("l_sel", [NS, 3, NBLK])
        selm = sb("l_selm", [NS, 2])
        oa_s = sb("l_oa_s", [P, RA * DT])
        oT_s = sb("l_oT_s", [P, 8, NS])
        pages = sb("l_pages", [1, DB * PAGES], I32)
        s_ps = [ctx.enter_context(nc.psum_tensor(f"l_s{k}", [P, 1024], F32)) for k in range(2)]
        t_ps = [ctx.enter_context(nc.psum_tensor(f"l_t{k}", [P, 512], F32)) for k in range(2)]
        o_ps = ctx.enter_context(nc.psum_tensor("l_o", [P, 512], F32))
        x_ps = ctx.enter_context(nc.psum_tensor("l_x", [P, 512], F32))

        const_in = sem("l_const_in")
        passed = sem("l_passed")
        pages_in, win_out = sem("l_pages_in"), sem("l_win_out")
        q_in = [sem(f"l_q_in{k}") for k in range(2)]
        kv_in = [sem(f"l_kv_in{k}") for k in range(4)]
        kdk_in, kdv_in, new_in, ks_in, kw_in, rows_in = (sem("l_" + x) for x in ("kdk_in", "kdv_in", "new_in", "ks_in", "kw_in", "rows_in"))
        kdk_out, kdv_out, kw_out, oT_out = (sem("l_" + x) for x in ("kdk_out", "kdv_out", "kw_out", "oT_out"))
        acc_out = [sem(f"l_acc_out{k}") for k in range(2)]
        x_filled, x_free, rows_ready = sem("l_x_filled"), sem("l_x_free"), sem("l_rows_ready")
        s_filled, s_free = sem("l_s_filled"), sem("l_s_free")
        t_filled = sem("l_t_filled")
        t_evac = [sem(f"l_t_evac{k}") for k in range(2)]
        rt_ready = sem("l_rt_ready")
        o_filled, o_free = sem("l_o_filled"), sem("l_o_free")
        masked, exped, scaled = sem("l_masked"), sem("l_exped"), sem("l_scaled")
        hi_done, lo_done = sem("l_hi_done"), sem("l_lo_done")
        dve_c, pool_c = sem("l_dve_c"), sem("l_pool_c")
        bd_zero, bd_ready = sem("l_bd_zero"), sem("l_bd_ready")
        tanh_in, tanh_done, hid_ready, ckv_ready, sel_ready = (sem("l_" + x) for x in ("tanh_in", "tanh_done", "hid_ready", "ckv_ready", "sel_ready"))

        CREDIT_O = 8
        NX = len(X_USERS)
        at_u = lambda i, n: i * NU + (n + 1)
        at_o = lambda i, n: i * NU + (n + 1 + CREDIT_O)
        prompt = [n for n in range(NU) if UNITS[n][0][0] != "s"]
        at_r = lambda i, n: i * len(prompt) + (prompt.index(n % NU) + 1 + len(prompt) * (n // NU))
        at_x = lambda i, name: i * NX + (X_USERS.index(name) + 1)
        at_t = lambda i, c: i * NT + (c + 1)
        at_evac = lambda i, c: i * (NT // 2) + (c // 2 + 2)

        def chunks_of(phase, name, j=None):
            if name == "prep" and j == 0:
                if phase == FIRST:
                    return list(range(PREP_CHUNKS))
                return [c - NT for c in chunks_of(MID, "prep", NEXT)]
            return [c + T_SHIFT[phase] for (a, b, _), c in T[phase].items() if a == name and (j is None or b == j)]

        def wait_turned(eng, i, phase, name, j=None):
            for par in range(2):
                mine = [c for c in chunks_of(phase, name, j) if c % 2 == par]
                if mine:
                    eng.wait_ge(t_evac[par], at_evac(i, max(mine)))

        def loop(eng, body, chain=None):
            body(0, FIRST)
            with eng.Fori(1, DB - 1) as i:
                if chain:
                    chain.enter(i, CHAIN_PER_PASS, 1)
                body(i, MID)
            if chain:
                chain.leave(DB - 1)
            body(DB - 1, LAST)

        block = ctx.enter_context(nc.Block())

        dil_rows = o["dil_prompt"].rearrange("b s c h e -> (b s) (c h e)").rearrange("(a p) n -> p a n", p=P)
        slc_rows = o["slc_prompt"].rearrange("b s c g e -> (b s) (c g e)").rearrange("(a p) n -> p a n", p=P)
        win_rows = scratch["kvw"][0:SEQ, :].rearrange("(a p) n -> p a n", p=P)
        q_rows = [scratch[x][0:SEQ, :].rearrange("(a p) n -> p a n", p=P) for x in ("qb", "qa")]
        o_rows = scratch["o"].rearrange("(a p) n -> p a n", p=P)
        ROWS_AT = range(9, 17)
        unit = {u: n for n, u in enumerate(UNITS)}

        @block.sync
        def _(sp):
            sp.dma_start(masks[:], t["masks"]).then_inc(const_in, 16)
            sp.dma_start(smask[:], t["smask"]).then_inc(const_in, 16)
            sp.dma_start(pages[:], t["page_table"].rearrange("(o b) n -> o (b n)", o=1)).then_inc(pages_in, 16)
            sp.dma_start(o["win_prompt"].rearrange("b s c g e -> (b s) (c g e)"), scratch["kvw"][SEQ - WIN:SEQ, :]).then_inc(win_out, 16)
            sp.wait_ge(pages_in, 16)

            sp.sem_inc(acc_out[0], 1)
            sp.sem_inc(acc_out[1], 1)

            def load_dil(i):
                sp.dma_start(q_nat[0][:], q_rows[0][:, :, bass.ds(i * E, E)]).then_inc(q_in[0], 16)
                sp.dma_start(kv_nat[0][:, :, 0, :], dil_rows[:, :, bass.ds(i * E, E)]).then_inc(kv_in[0], 16)
                sp.dma_start(kv_nat[0][:, :, 1, :], dil_rows[:, :, bass.ds(i * E + 512, E)]).then_inc(kv_in[0], 16)

            def load_q_nsa(i):
                sp.dma_start(q_nat[1][:], q_rows[1][:, :, bass.ds(i * E, E)]).then_inc(q_in[1], 16)

            def load_kv_nsa(i, k):
                g = (i // RA) * E
                for c in range(2):
                    if k == 3:
                        dst, src = kv_nat[3][:, 0, c, :], scratch["kvc"][:, c, :, :].rearrange("n g e -> n (g e)")[:, bass.ds(g, E)]
                    else:
                        dst, src = kv_nat[k][:, :, c, :], (slc_rows if k == 1 else win_rows)[:, :, bass.ds(g + c * P, E)]
                    sp.dma_start(dst, src).then_inc(kv_in[k], 16)

            def load_kd(i, c):
                src = t["state_dil"][bass.ds(i, 1), :, c, :, :].rearrange("b (p j) h e -> (b p) j (h e)", j=8)
                sp.dma_start((kd_k, kd_v)[c][:], src).then_inc((kdk_in, kdv_in)[c], 16)

            def load_new(i):
                sp.dma_start(kd_new[:], o["dil_sample"][bass.ds(i, 1), PAST:PAST + DT].rearrange("b s c h e -> (b s) (c h e)")).then_inc(new_in, 16)
                sp.dma_start(ks_new[:], o["slc_sample"][bass.ds(i, 1)].rearrange("b s c g e -> (b s) (c g e)")).then_inc(new_in, 16)
                sp.dma_start(kw_new[:], scratch["kvw"][bass.ds(i * DT + SEQ, DT), :]).then_inc(new_in, 16)

            def page(i, n):
                return sp.value_load(pages[0:1, bass.ds(i * PAGES + n, 1)], min_val=0, max_val=t["cache_slc"].shape[0] - 1)

            def load_ks(i):
                for n in range(PAGES):
                    sp.dma_start(ks[:, n, :], t["cache_slc"][bass.ds(page(i, n), 1)].rearrange("b p c g e -> (b p) (c g e)")).then_inc(ks_in, 16)

            def load_rows(i):
                for n in range(PAGES):
                    sp.dma_start(rows_nat[8 * n:8 * n + 8, :],
                                 t["cache_cmp"][bass.ds(page(i, n), 1)].rearrange("b (n r) c g e -> (b n) (r c g e)", r=CMP_STRIDE)).then_inc(rows_in, 16)

            def load_kw(i):
                sp.dma_start(kw[:], t["state_win"][bass.ds(i, 1)].rearrange("b (p j) c g e -> (b p) j (c g e)", j=WIN // P)).then_inc(kw_in, 16)

            load_dil(0)
            load_q_nsa(0)
            load_kd(0, 0)
            load_new(0)
            load_kv_nsa(0, 1)
            load_kd(0, 1)
            load_kw(0)
            load_ks(0)
            load_kv_nsa(0, 2)
            load_kv_nsa(0, 3)

            def wait(sem_, value):
                sp.wait_ge(sem_, value)
                sp.sem_inc(passed, 1)

            def store_nsa(i):
                sp.dma_start(o_rows[:, :, bass.ds((i % RA) * (GA * E) + (i // RA) * E, E)], acc[1][:]).then_inc(acc_out[1], 16)

            def body(i, phase):
                more = phase != LAST
                wait(kdk_in, i * 16 + 16)
                sp.dma_start(o["dil_sample"][bass.ds(i, 1), 0:PAST, 0, :, :].rearrange("b (p j) h e -> (b p) j (h e)", j=8), kd_k[:]).then_inc(kdk_out, 16)
                wait(kdv_in, i * 16 + 16)
                sp.dma_start(o["dil_sample"][bass.ds(i, 1), 0:PAST, 1, :, :].rearrange("b (p j) h e -> (b p) j (h e)", j=8), kd_v[:]).then_inc(kdv_out, 16)
                wait(kw_in, i * 16 + 16)
                sp.dma_start(o["win_sample"][bass.ds(i, 1), 0:WIN - DT].rearrange("b (p j) c g e -> (b p) j (c g e)", j=WIN // P), kw[2:P]).then_inc(kw_out, 16)
                wait(new_in, i * 48 + 48)
                sp.dma_start(o["win_sample"][bass.ds(i, 1), WIN - DT:WIN].rearrange("b s c g e -> (b s) (c g e)"), kw_new[:]).then_inc(kw_out, 16)
                if phase != FIRST:
                    wait(o_free, at_u(i, -1) + 1)
                    store_nsa(i - 1)
                    load_kv_nsa(i, 3)
                wait(t_filled, at_t(i, chunks_of(phase, "kd", 7)[-1]))
                wait(kdk_out, i * 16 + 16)
                load_rows(i)
                wait(o_filled, at_o(i, unit["d", 7]))
                if more:
                    load_dil(i + 1)
                wait(o_filled, at_o(i, unit["sd", 0]))
                wait(kdv_out, i * 16 + 16)
                if more:
                    load_kd(i + 1, 1)
                wait(o_free, at_u(i, unit["d", 7]) + 1)
                sp.dma_start(o_rows[:, :, bass.ds(i * E + 512, E)], acc[0][:]).then_inc(acc_out[0], 16)
                wait(rows_ready, i * 8 + 8)
                if more:
                    load_kd(i + 1, 0)
                wait(o_filled, at_o(i, unit["l", 7]))
                if more:
                    load_q_nsa(i + 1)
                    load_kv_nsa(i + 1, 1)
                wait(o_filled, at_o(i, unit["w", 7]))
                if more:
                    load_kv_nsa(i + 1, 2)
                wait(o_filled, at_o(i, unit["sl", 0]))
                if more:
                    load_ks(i + 1)
                wait(o_filled, at_o(i, unit["sw", 0]))
                wait(kw_out, i * 32 + 32)
                if more:
                    load_new(i + 1)
                    load_kw(i + 1)

            body(0, FIRST)
            with sp.Fori(1, DB - 1) as i:
                body(i, MID)
            body(DB - 1, LAST)
            sp.wait_ge(o_free, at_u(DB, -1) + 1)
            store_nsa(DB - 1)
            sp.dma_start(scratch["oT"], oT_s[:]).then_inc(oT_out, 16)
            for k in range(2):
                sp.wait_ge(acc_out[k], 16 * DB + 1)
            sp.wait_ge(oT_out, 16)
            sp.wait_ge(win_out, 16)
            sp.wait_ge(kw_out, 32 * DB)

        @block.gpsimd
        def _(pool):
            nc.gpsimd.memset(bd_dil[:], 0.0).then_inc(bd_zero, 1)
            nc.gpsimd.memset(bd_nsa[:], 0.0).then_inc(bd_zero, 1)
            pool.wait_ge(bd_zero, 2)

            ch = Chain(pool, pool_c)

            def body(i):
                ch.enter(i, 5)
                pool.wait_ge(o_free, at_u(i, -1) + 1)
                for g in range(2):
                    hp = slice(g * E, (g + 1) * E)
                    ch.step(nc.gpsimd.tensor_copy(bd_dil[hp, :].rearrange("p (a c) -> p a c", c=80)[:, :, g * DT:(g + 1) * DT],
                                                  q_dil_T[hp, :, bass.ds(i * DT, DT)]))
                    ch.step(nc.gpsimd.tensor_copy(bd_nsa[hp, g * RA * DT:(g + 1) * RA * DT].rearrange("p (a c) -> p a c", c=DT),
                                                  q_nsa_T[hp, :, bass.ds(i * DT, DT)]))
                ch.step(nc.gpsimd.tensor_copy(gate_h[:], gate_p[:, :, bass.ds(i * 3, 3)]))
                nc.gpsimd.tensor_copy(gate_b[:].unsqueeze(1), gate_s[:, bass.ds(i, 1), :]).then_inc(bd_ready, 1)

                for s in range(NU):
                    if s == unit["sd", 0] + 1:
                        pool.wait_ge(rows_in, i * 16 * PAGES + 16 * PAGES)
                        pool.sem_inc(passed, 1)
                        pool.wait_ge(s_filled, at_u(i, unit["sd", 0]))
                        pool.sem_inc(passed, 1)
                    if s in ROWS_AT:
                        m = s - ROWS_AT[0]
                        c, r = m // 2, slice(m % 2 * 8, m % 2 * 8 + 8)
                        ins = nc.gpsimd.tensor_copy(rows16[:, c * 1024:(c + 1) * 1024].rearrange("p (r e) -> p r e", e=E)[:, r, :],
                                                    rows_nat.rearrange("p (r k e) -> p r k e", k=4, e=E)[:, r, c, :])
                        ins.then_inc(rows_ready, 1)

            with pool.Fori(0, DB) as i:
                body(i)

        @block.tensor
        def _(pe):
            pe.wait_ge(const_in, 32)

            def turn_slot(i, c):
                pe.wait_ge(t_evac[c % 2], i * (NT // 2) + (c // 2 + 1))
                pe.sem_inc(passed, 1)
                return t_ps[c % 2]

            def prep(i, b, at):
                pe.wait_ge(lo_done, i * 4 + (b + 1))
                b %= NEXT
                jobs = []
                if b < 2:
                    jobs += [[(q_split[:, k, :], P) for k in range(c, c + 4)] for c in (0, 4)]
                if b < 3:
                    for x in (0, E):
                        jobs += [[(k_split[:, k, x:x + 2 * E], P) for k in range(c, c + 4)] for c in (0, 4)]
                else:
                    jobs += [[(k_split[0:NS, 0, x:x + 2 * E], NS)] for x in (0, E)]
                for q, c in at:
                    dst = turn_slot(i, c)
                    for k, (src, r) in enumerate(jobs[q]):
                        last = nc.tensor.transpose(dst[:, k * P:k * P + r], src.bitcast(F32), ident[0:r, 0:r])
                    last.then_inc(t_filled, 1)

            def body(i, phase):
                at = lambda name, j, q: T[phase][name, j, q] + T_SHIFT[phase]

                def qk(n, half=None):
                    kind, j = UNITS[n]
                    out = s_ps[n % 2]
                    if half != 1:
                        pe.wait_ge(s_free, at_u(i, n))
                    if kind[0] != "s":
                        b = BRANCH[kind]
                        a0, a1 = key_blocks(kind, j)
                        w = (a1 - a0) * P if kind != "c" else NS
                        if j == 0:
                            wait_turned(pe, i, phase, "prep", b)
                        lhs = qT[b > 0][:, j * P:(j + 1) * P]
                        for c in range(0, w, 512):
                            cw = min(512, w - c)
                            ks_ = slice(a0 * P + c, a0 * P + c + cw)
                            nc.tensor.matmul(out[:, c:c + cw], lhs, kB[b % 2][:, ks_], start=True, stop=False)
                            last = nc.tensor.matmul(out[:, c:c + cw], lhs, kA[b % 2][:, ks_], start=False, stop=True)
                        last.then_inc(s_filled, 1)
                        return
                    if kind == "sd":
                        if half == 0:
                            pe.wait_ge(bd_ready, i + 1)
                            wait_turned(pe, i, phase, "kd")
                        for a in range(4):
                            last = nc.tensor.matmul(out[0:NS, half * 512:(half + 1) * 512], bd_dil[:, a * NS:(a + 1) * NS], kd_T[:, a, half * 512:(half + 1) * 512],
                                                    start=(a == 0), stop=(a == 3))
                        if half == 1:
                            last.then_inc(s_filled, 1)
                            wait_turned(pe, i, phase, "new")
                            pe.wait_ge(x_free, at_x(i, "sd"))
                            for a in range(4):
                                last = nc.tensor.matmul(x_ps[0:NS, 0:DT], bd_dil[:, a * NS:(a + 1) * NS], new_T[:, a, :], start=(a == 0), stop=(a == 3))
                            last.then_inc(x_filled, 1)
                        return
                    if kind == "sl":
                        wait_turned(pe, i, phase, "ksw")
                    if kind == "sc":
                        pe.wait_ge(ckv_ready, i + 1)
                    src, w = {"sc": (kc_T, NCMP), "sl": (ks_T, PAST), "sw": (kw_T, WIN)}[kind]
                    for c in range(0, w, 512):
                        cw = min(512, w - c)
                        last = nc.tensor.matmul(out[0:NS, c:c + cw], bd_nsa[:], src[:, c:c + cw], start=True, stop=True)
                    if kind == "sw":
                        last = nc.tensor.matmul(out[0:NS, WIN:WIN + DT], bd_nsa[:], new_T[:, 5, :], start=True, stop=True)
                    last.then_inc(s_filled, 1)
                    if kind == "sl":
                        pe.wait_ge(x_free, at_x(i, "sl"))
                        nc.tensor.matmul(x_ps[0:NS, 0:DT], bd_nsa[:], new_T[:, 4, :], start=True, stop=True).then_inc(x_filled, 1)

                def tr(n):
                    kind, j = UNITS[n]
                    if kind[0] != "s":
                        a0, a1 = key_blocks(kind, j)
                        w = (a1 - a0) * P if kind != "c" else NS
                        pe.wait_ge(exped, at_u(i, n))
                        for c in range(0, w, 512):
                            dst = turn_slot(i, at("tr", n, c // 512))
                            for k in range(c, min(w, c + 512), P):
                                kw_ = min(P, w - k)
                                last = nc.tensor.transpose(dst[0:kw_, k - c:k - c + P], e_ring[:, n % 4, k:k + kw_], ident[:])
                            last.then_inc(t_filled, 1)
                        return
                    nth = [u for u in range(NU) if UNITS[u][0][0] == "s"].index(n)
                    w = {"sd": PAST, "sc": NCMP, "sl": PAST, "sw": WIN}[kind]
                    if kind == "sc":
                        pe.wait_ge(exped, at_u(i, n))
                    else:
                        pe.wait_ge(scaled, i * 4 + (nth + 1))
                    dst = turn_slot(i, at("tr", n, 0))
                    for k in range(0, w, P):
                        kw_ = min(P, w - k)
                        last = nc.tensor.transpose(dst[0:kw_, k // P * NS:(k // P + 1) * NS], e_ring[0:NS, n % 4, k:k + kw_], ident[0:NS, 0:NS])
                    last.then_inc(t_filled, 1)
                    dst = turn_slot(i, at("tr", n, 1))
                    if kind == "sc":
                        pe.wait_ge(scaled, i * 4 + (nth + 1))
                        pe.sem_inc(passed, 1)
                        last = nc.tensor.transpose(dst[0:NCMP, 0:NS], e_gated[:, 0:NCMP], ident[0:NS, 0:NS])
                    else:
                        last = nc.tensor.transpose(dst[0:DT, 0:NS], e_ring[0:NS, n % 4, w:w + DT], ident[0:NS, 0:NS])
                    last.then_inc(t_filled, 1)

                def probs_of(n, q):
                    c, u = (at("tr", n, q), U[phase][n, q]) if (n, q) in U[phase] else (T[MID]["tr", n + NU, q] + T_SHIFT[MID] - NT, U[MID][n + NU, q])
                    pe.wait_ge(t_evac[c % 2], at_evac(i, c))
                    return p_ring[:, (u + U_SHIFT[phase]) % 4, :]

                def pv(n, half=None):
                    kind, j = UNITS[n]
                    if half != 1:
                        pe.wait_ge(o_free, at_u(i, n))
                    out = o_ps
                    if kind[0] != "s":
                        b = BRANCH[kind]
                        a0, a1 = key_blocks(kind, j)
                        if j == 0:
                            pe.wait_ge(kv_in[b], (i if n >= 0 else i - 1) * 32 + 32)
                        for k in range(a1 - a0):
                            if k % 4 == 0:
                                probs = probs_of(n, k // 4)
                            r = P if kind != "c" else NS
                            last = nc.tensor.matmul(out[:, 0:E], probs[0:r, (k % 4) * P:(k % 4 + 1) * P], kv_nat[b][0:r, a0 + k, 1, :],
                                                    start=(k == 0), stop=(k == a1 - a0 - 1))
                        last.then_inc(o_filled, 1)
                        return
                    p0, p1 = probs_of(n, 0), probs_of(n, 1)
                    if kind == "sd":
                        pe.wait_ge(kdv_in, i * 16 + 16)
                        for a in range(2 * half, 2 * half + 2):
                            for k in range(8):
                                nc.tensor.matmul(out[:, a * 16:(a + 1) * 16], kd_v[:, k, a * P:(a + 1) * P], p0[:, k * NS + a * 16:k * NS + (a + 1) * 16],
                                                 start=(k == 0), stop=False)
                            last = nc.tensor.matmul(out[:, a * 16:(a + 1) * 16], kd_new[:, 512 + a * P:512 + (a + 1) * P], p1[0:DT, a * 16:(a + 1) * 16],
                                                    start=False, stop=True)
                        if half == 1:
                            last.then_inc(o_filled, 1)
                    elif kind == "sc":
                        pe.wait_ge(x_free, at_x(i, "sel1"))
                        pe.sem_inc(passed, 1)
                        nc.tensor.matmul(x_ps[0:NS, 0:NBLK], p0[0:NCMP, 0:NS], smask[0:NCMP, S_OVER:S_OVER + NBLK],
                                         start=True, stop=True).then_inc(x_filled, 1)
                        nc.tensor.matmul(out[:, 0:NS], vc[:], p1[0:NCMP, 0:NS], start=True, stop=True).then_inc(o_filled, 1)
                    else:
                        src, new, m = (ks, ks_new, PAGES) if kind == "sl" else (kw, kw_new, WIN // P)
                        for k in range(m):
                            nc.tensor.matmul(out[:, 0:NS], src[:, k, P:2 * P], p0[:, k * NS:(k + 1) * NS], start=(k == 0), stop=False)
                        nc.tensor.matmul(out[:, 0:NS], new[:, P:2 * P], p1[0:DT, 0:NS], start=False, stop=True).then_inc(o_filled, 1)

                def extra(name, j, qs):
                    if name == "prep":
                        prep(i, j, [(q, at(name, j, q)) for q in qs])
                    elif name == "kd":
                        if j == 0:
                            pe.wait_ge(kdk_in, i * 16 + 16)
                        dst = turn_slot(i, at(name, j, 0))
                        for a in range(4):
                            last = nc.tensor.transpose(dst[:, a * P:(a + 1) * P], kd_k[:, j, a * P:(a + 1) * P], ident[:])
                        last.then_inc(t_filled, 1)
                    elif name == "new":
                        pe.wait_ge(new_in, i * 48 + 48)
                        dst = turn_slot(i, at(name, j, 0))
                        for a in range(6):
                            src = kd_new[:, a * P:(a + 1) * P] if a < 4 else (ks_new, kw_new)[a - 4][:, 0:P]
                            last = nc.tensor.transpose(dst[:, a * DT:(a + 1) * DT], src, ident[0:DT, 0:DT])
                        last.then_inc(t_filled, 1)
                    elif name == "ksw":
                        if j < 2:
                            pe.wait_ge(ks_in, i * 16 * PAGES + 16 * PAGES)
                        else:
                            pe.wait_ge(kw_in, i * 16 + 16)
                        dst = turn_slot(i, at(name, j, 0))
                        for a in range(4):
                            src = ks[:, j * 4 + a, 0:P] if j < 2 else kw[:, a, 0:P]
                            last = nc.tensor.transpose(dst[:, a * P:(a + 1) * P], src, ident[:])
                        last.then_inc(t_filled, 1)
                    elif name == "xt":
                        if j == 0:
                            pe.wait_ge(rows_ready, i * 8 + 8)
                        dst = turn_slot(i, at(name, j, 0))
                        for rp in range(8):
                            last = nc.tensor.transpose(dst[:, rp * NS:(rp + 1) * NS], rows16[:, j * 1024 + rp * P:j * 1024 + (rp + 1) * P], ident[0:NS, 0:NS])
                        last.then_inc(t_filled, 1)
                    elif name == "hid":
                        c, half = j // 2, j % 2
                        if half == 0:
                            for g in range(GA):
                                wait_turned(pe, i, phase, "xt", c * GA + g)
                                pe.sem_inc(passed, 1)
                        if j == 0:
                            pe.wait_ge(x_free, at_x(i, "hid"))
                        out = x_ps[:, c * P:(c + 1) * P].rearrange("p (g n) -> p g n", g=GA)[:, :, 0:NCMP]
                        for k in range(8 * half, 8 * half + 8):
                            last = nc.tensor.matmul(out, w1[:, c, k, :], xT[:, c, :, k % 8, k // 8:k // 8 + NCMP], start=(k == 0), stop=(k == 15))
                        if j == 3:
                            last.then_inc(x_filled, 1)
                    elif name == "ckv":
                        pe.wait_ge(hid_ready, i + 1)
                        pe.sem_inc(passed, 1)
                        pe.wait_ge(x_free, at_x(i, "ckv"))
                        for g in range(GA):
                            nc.tensor.matmul(x_ps[g * E:(g + 1) * E, 0:NCMP], w2[:, 0, :], hu[:, g, 0:NCMP], start=True, stop=True)
                            last = nc.tensor.matmul(x_ps[0:NCMP, P + g * E:P + (g + 1) * E], hu[:, 2 + g, 0:NCMP], w2[:, 1, :], start=True, stop=True)
                        last.then_inc(x_filled, 1)
                    elif name == "sel2":
                        pe.wait_ge(sel_ready, i + 1)
                        pe.sem_inc(passed, 1)
                        pe.wait_ge(x_free, at_x(i, "sel2"))
                        pe.sem_inc(passed, 1)
                        nc.tensor.matmul(x_ps[0:NS, 0:NBLK], smask[:, S_SAME:S_SAME + NS], sel[:, 0, :], start=True, stop=True).then_inc(x_filled, 1)

                for s in stages(phase):
                    sd = s == unit["sd", 0]
                    if s < NU:
                        qk(s, 0 if sd else None)
                    if there(phase, s - 2):
                        tr(s - 2)
                    if s - 4 == unit["sd", 0]:
                        pv(s - 4, 1)
                    if there(phase, s - 3):
                        pv(s - 3, 0 if s - 3 == unit["sd", 0] else None)
                    if sd:
                        qk(s, 1)
                    for name, j, qs in extras(phase, s):
                        extra(name, j, qs)

            pe.sem_inc(o_filled, CREDIT_O)
            prep(0, 0, [(q, q) for q in range(PREP_CHUNKS)])
            loop(pe, body)

        def copy_dst(phase, name, j, q):
            if name == "tr":
                kind, jj = UNITS[j]
                dst = p_ring[:, (U[phase][j, q] + U_SHIFT[phase]) % 4, :]
                if kind[0] != "s":
                    a0, a1 = key_blocks(kind, jj)
                    w = min(4, a1 - a0 - 4 * q) * P
                    r = P if kind != "c" else NS
                elif q == 1:
                    w, r = NS, (NCMP if kind == "sc" else DT)
                else:
                    w, r = {"sd": 512, "sc": NS, "sl": 512, "sw": 4 * NS}[kind], (NCMP if kind == "sc" else P)
                return dst[0:r, 0:w], r, w
            if name == "prep":
                j %= NEXT
                if j < 2:
                    if q < 2:
                        return qT[j][:, q * 512:(q + 1) * 512], P, 512
                    q -= 2
                if j == 3:
                    return (kA, kB)[q][1][:, 0:NS], P, NS
                return (kA, kB)[q // 2][j % 2][:, (q % 2) * 512:(q % 2 + 1) * 512], P, 512
            if name == "kd":
                return kd_T[:, :, j * P:(j + 1) * P], P, 512
            if name == "new":
                return new_T[:].rearrange("p a n -> p (a n)"), P, 6 * DT
            if name == "ksw":
                return (ks_T[:, j * 512:(j + 1) * 512] if j < 2 else kw_T[:, :]), P, 512
            return xT[:, j // 2, j % 2].rearrange("p a n -> p (a n)"), P, 512

        def owner(phase, u):
            if u >= 0:
                return next((n for (n, _), v in U[phase].items() if v == u))
            return None if phase == FIRST else owner(MID, u + NCH) - NU

        def take_out(eng, i, phase, name, j, qs, copy):
            for q in qs:
                if TAKER(name, j, q) == (eng is nc.scalar):
                    take_chunk(eng, i, phase, T[phase][name, j, q] + T_SHIFT[phase], name, j, q, copy)

        def take_chunk(eng, i, phase, c, name, j, q, copy):
            par = c % 2
            eng.wait_ge(t_filled, at_t(i, c))
            if name == "tr":
                back = owner(phase, U[phase][j, q] - 4)
                if back is not None:
                    eng.wait_ge(o_filled, at_o(i, back))
            dst, r, w = copy_dst(phase, name, j, q)
            src = t_ps[par][0:r, 0:w]
            if name == "kd":
                src = src.rearrange("p (a n) -> p a n", a=4)
            copy(dst, src).then_inc(t_evac[par], 1)

        @block.scalar
        def _(act):
            copy = lambda dst, src: nc.scalar.activation(dst, src, ACT.Copy)

            def split(i, phase, b):
                if b > 0:
                    act.wait_ge(t_filled, at_t(i, chunks_of(phase, "prep", b - 1)[-1]))
                act.wait_ge(kv_in[b % NEXT], i * 32 + 32 * (1 + b // NEXT))
                b_, (r, m) = b % NEXT, ((NS, 1) if b == 3 else (P, TILES))
                if b_ < 2:
                    act.wait_ge(q_in[b_], i * 16 + 16 * (1 + b // NEXT))
                    copy(q_split[:, :, 0:E], q_nat[b_][:])
                copy(k_split[0:r, 0:m, 0:E], kv_nat[b_][0:r, 0:m, 0, :])
                copy(k_split[0:r, 0:m, 2 * E:3 * E], kv_nat[b_][0:r, 0:m, 0, :]).then_inc(hi_done, 1)

            def body(i, phase):
                def exp(n):
                    kind, j = UNITS[n]
                    if kind[0] != "s":
                        a0, a1 = key_blocks(kind, j)
                        r, w = P, ((a1 - a0) * P if kind != "c" else NS)
                    else:
                        r, w = NS, {"sd": PAST + DT, "sc": NCMP, "sl": PAST + DT, "sw": WIN + DT}[kind]
                    act.wait_ge(masked, at_u(i, n))
                    k = n % 4
                    nc.scalar.activation(e_ring[0:r, k, 0:w], e_ring[0:r, k, 0:w], ACT.Exp, bias=nmin[0:r, k:k + 1], scale=-1.0,
                                         accum_out=total[0:r, k:k + 1]).then_inc(exped, 1)

                for s in stages(phase):
                    if there(phase, s - 1):
                        exp(s - 1)
                    if there(phase, s - 2):
                        take_out(act, i, phase, "tr", s - 2, range(unit_chunks(s - 2)), copy)
                    for name, j, qs in extras(phase, s):
                        take_out(act, i, phase, name, j, qs, copy)
                        if name == "hid" and j == 3:
                            act.wait_ge(tanh_in, i + 1)
                            nc.scalar.activation(hu[:, :, 0:NCMP], hu[:, :, 0:NCMP], ACT.Tanh, scale=GELU_C).then_inc(tanh_done, 1)
                    if s in SPLIT_AT and not (phase == LAST and SPLIT_AT[s] == NEXT):
                        split(i, phase, SPLIT_AT[s])

            split(0, FIRST, 0)
            loop(act, body)

        @block.vector
        def _(dve):
            dve.sem_inc(t_evac[0], 1)
            dve.sem_inc(t_evac[1], 1)
            dve.sem_inc(s_free, 2)
            dve.sem_inc(o_free, 1)
            dve.sem_inc(x_free, 1)
            ch = Chain(dve, dve_c)
            dve.wait_ge(const_in, 32)
            copy = lambda dst, src: nc.vector.tensor_copy(dst, src)

            def split(i, b):
                dve.wait_ge(hi_done, i * 4 + (b + 1))
                b_, (r, m) = b % NEXT, ((NS, 1) if b == 3 else (P, TILES))
                if b_ < 2:
                    nc.vector.tensor_tensor(q_split[:, :, E:2 * E], q_nat[b_][:], q_split[:, :, 0:E].bitcast(F32), ALU.subtract)
                nc.vector.tensor_tensor(k_split[0:r, 0:m, E:2 * E], kv_nat[b_][0:r, 0:m, 0, :], k_split[0:r, 0:m, 0:E].bitcast(F32),
                                        ALU.subtract).then_inc(lo_done, 1)

            def body(i, phase):
                def mask(dst, src, m, acc_, last):
                    return nc.vector.tensor_tensor_reduce(out=dst, in0=src, in1=m, scale=1.0, scalar=CLAMP, op0=ALU.add, op1=ALU.min, accum_out=acc_)

                def low(n):
                    kind, j = UNITS[n]
                    k = n % 4
                    dve.wait_ge(s_filled, at_u(i, n))
                    dve.sem_inc(passed, 1)
                    sp_ = s_ps[n % 2]
                    if kind[0] != "s":
                        a0, a1 = key_blocks(kind, j)
                        w = (a1 - a0) * P if kind != "c" else NS
                        end = {"d": SEQ, "l": 2 * SEQ, "w": M_CMP, "c": M_CMP + (j + 1) * NS}[kind]
                        ins = mask(e_ring[:, k, 0:w], sp_[:, 0:w], masks[:, end - w:end], nmin[:, k:k + 1], True)
                        ins.then_inc(s_free, 1)
                        dve.wait_ge(s_free, at_u(i, n) + 2)
                        dve.sem_inc(masked, 1)
                        return
                    if kind in ("sc", "sw"):
                        w, m0 = (NCMP, S_ZERO) if kind == "sc" else (WIN + DT, S_WIN)
                        ins = mask(e_ring[0:NS, k, 0:w], sp_[0:NS, 0:w], smask[:, m0:m0 + w], nmin[0:NS, k:k + 1], True)
                        ins.then_inc(s_free, 1)
                        dve.wait_ge(s_free, at_u(i, n) + 2)
                        dve.sem_inc(masked, 1)
                        return
                    if kind == "sd":
                        ins = mask(e_ring[0:NS, k, 0:PAST], sp_[0:NS, 0:PAST], smask[:, 0:PAST], nmin[0:NS, k:k + 1], False)
                        m1 = smask[:, PAST:PAST + DT]
                    else:
                        ins = mask(e_ring[0:NS, k, 0:PAST].rearrange("p (b c) -> p b c", c=SLC_BLK), sp_[0:NS, 0:PAST].rearrange("p (b c) -> p b c", c=SLC_BLK),
                                   sel[:, 2, :].unsqueeze(2).to_broadcast([NS, NBLK, SLC_BLK]), nmin[0:NS, k:k + 1], False)
                        m1 = smask[:, S_NEW:S_NEW + DT]
                    ins.then_inc(s_free, 1)
                    dve.wait_ge(x_filled, at_x(i, kind))
                    dve.sem_inc(passed, 1)
                    mask(e_ring[0:NS, k, PAST:PAST + DT], x_ps[0:NS, 0:DT], m1, nmin2[:], True).then_inc(x_free, 1)
                    dve.wait_ge(s_free, at_u(i, n) + 2)
                    dve.wait_ge(x_free, at_x(i, kind) + 1)
                    nc.vector.tensor_tensor(nmin[0:NS, k:k + 1], nmin[0:NS, k:k + 1], nmin2[:], ALU.min).then_inc(masked, 1)

                def scale(n):
                    kind, _ = UNITS[n]
                    k = n % 4
                    dve.wait_ge(exped, at_u(i, n))
                    rt = rtot[0:NS, k:k + 1]
                    ch.step(nc.vector.reciprocal(rt, total[0:NS, k:k + 1]))
                    w = {"sd": PAST + DT, "sc": NCMP, "sl": PAST + DT, "sw": WIN + DT}[kind]
                    e = e_ring[0:NS, k, 0:w]
                    if kind == "sd":
                        nc.vector.tensor_scalar(e, e, rt, None, ALU.mult).then_inc(scaled, 1)
                    else:
                        b = {"sc": 0, "sl": 1, "sw": 2}[kind]
                        out = e_gated[:, 0:w] if kind == "sc" else e
                        nc.vector.tensor_scalar(out, e, rt, gate_b[:, b:b + 1], ALU.mult, ALU.mult).then_inc(scaled, 1)

                def ratio(n):
                    kind, j = UNITS[n]
                    k = n % 4
                    dve.wait_ge(exped, at_u(i, n))
                    if kind == "c":
                        ch.step(nc.vector.tensor_scalar(total[:, k:k + 1], total[:, k:k + 1], TINY, None, ALU.max))
                    rt = rtot[:, k:k + 1]
                    ins = nc.vector.reciprocal(rt, total[:, k:k + 1])
                    if kind in "wc":
                        ch.step(ins)
                        ins = nc.vector.tensor_tensor(rt, rt, gate_h[:, j, {"w": 2, "c": 0}[kind]:][:, 0:1], ALU.mult)
                    ins.then_inc(rt_ready, 1)

                def out(n):
                    kind, j = UNITS[n]
                    k = n % 4
                    dve.wait_ge(o_filled, at_o(i, n))
                    src = o_ps
                    if kind[0] != "s":
                        rt = rtot[:, k:k + 1]
                        dve.wait_ge(rt_ready, at_r(i, n))
                        if kind in "dl" and j == 0:
                            dve.wait_ge(acc_out[kind == "l"], i * 16 + 1)
                        if kind == "d":
                            nc.vector.tensor_scalar(acc[0][:, j, :], src[:, 0:E], rt, None, ALU.mult).then_inc(o_free, 1)
                        elif kind == "l":
                            nc.vector.tensor_scalar(acc[1][:, j, :], src[:, 0:E], rt, gate_h[:, j, 1:2], ALU.mult, ALU.mult).then_inc(o_free, 1)
                        else:
                            nc.vector.scalar_tensor_tensor(out=acc[1][:, j, :], in0=src[:, 0:E], scalar=rt, in1=acc[1][:, j, :], op0=ALU.mult, op1=ALU.add).then_inc(o_free, 1)
                        return
                    for g in range(2):
                        hp = slice(g * E, (g + 1) * E)
                        if kind == "sd":
                            ins = nc.vector.tensor_copy(oT_s[hp, 4:8, bass.ds(i * DT, DT)],
                                                        src[hp, 0:64].rearrange("p (a c) -> p a c", c=16)[:, :, g * DT:(g + 1) * DT])
                        else:
                            v = src[hp, g * 32:(g + 1) * 32]
                            if kind == "sc":
                                ins = nc.vector.tensor_copy(oa_s[hp, :], v)
                            elif kind == "sl":
                                ins = nc.vector.tensor_tensor(oa_s[hp, :], v, oa_s[hp, :], ALU.add)
                            else:
                                ins = nc.vector.tensor_tensor(oT_s[hp, 0:4, bass.ds(i * DT, DT)], v.rearrange("p (a c) -> p a c", c=DT),
                                                              oa_s[hp, :].rearrange("p (a c) -> p a c", c=DT), ALU.add)
                    ins.then_inc(o_free, 1)

                def extra(name, j):
                    if name == "hid" and j == 3:
                        dve.wait_ge(x_filled, at_x(i, name))
                        for c in range(2):
                            ins = nc.vector.tensor_scalar(hh[:, 2 * c:2 * c + 2, 0:NCMP], x_ps[:, c * P:(c + 1) * P].rearrange("p (g n) -> p g n", g=GA)[:, :, 0:NCMP],
                                                          pe_bias[:, c:c + 1], None, ALU.add)
                        ins.then_inc(x_free, 1)
                        dve.wait_ge(x_free, at_x(i, name) + 1)
                        a, b = hh[:, :, 0:NCMP], hu[:, :, 0:NCMP]
                        ch.step(nc.vector.tensor_tensor(b, a, a, ALU.mult))
                        ch.step(nc.vector.tensor_scalar(b, b, 0.044715, 1.0, ALU.mult, ALU.add))
                        nc.vector.tensor_tensor(b, b, a, ALU.mult).then_inc(tanh_in, 1)
                        dve.wait_ge(tanh_done, i + 1)
                        ch.step(nc.vector.tensor_scalar(b, b, 1.0, None, ALU.add))
                        nc.vector.tensor_tensor(b, b, a, ALU.mult).then_inc(hid_ready, 1)
                    elif name == "ckv":
                        dve.wait_ge(x_filled, at_x(i, name))
                        nc.vector.tensor_copy(kc_T[:], x_ps[:, 0:NCMP]).then_inc(x_free, 1)
                        nc.vector.tensor_copy(vc[:], x_ps[0:NCMP, P:2 * P]).then_inc(ckv_ready, 1)
                    elif name == "sel1":
                        k = unit["sc", 0] % 4
                        dve.wait_ge(x_filled, at_x(i, name))
                        nc.vector.tensor_scalar(sel[:, 0, :], x_ps[0:NS, 0:NBLK], rtot[0:NS, k:k + 1], None, ALU.mult).then_inc(x_free, 1)
                        dve.wait_ge(x_free, at_x(i, name) + 1)
                        dve.sem_inc(sel_ready, 1)
                    elif name == "sel2":
                        dve.wait_ge(x_filled, at_x(i, name))
                        nc.vector.tensor_copy(sel[:, 1, :], x_ps[0:NS, 0:NBLK]).then_inc(x_free, 1)
                        dve.wait_ge(x_free, at_x(i, name) + 1)
                        free = slice(1, NBLK - 1)
                        blk = smask[:, S_BLK:S_BLK + NBLK]
                        ch.step(nc.vector.tensor_reduce(selm[:, 0:1], sel[:, 1, free], AX, ALU.min))
                        ch.step(nc.vector.tensor_scalar(sel[:, 1, free], sel[:, 1, free], selm[:, 0:1], None, ALU.is_equal))
                        ch.step(nc.vector.tensor_tensor(sel[:, 1, free], sel[:, 1, free], blk[:, free], ALU.mult))
                        ch.step(nc.vector.tensor_reduce(selm[:, 1:2], sel[:, 1, free], AX, ALU.max))
                        ch.step(nc.vector.tensor_scalar(sel[:, 2, :], blk, selm[:, 1:2], BIG, ALU.is_equal, ALU.mult))

                for s in stages(phase):
                    sample_out = there(phase, s - 4) and UNITS[s - 4][0][0] == "s"
                    if there(phase, s - 4) and not sample_out:
                        out(s - 4)
                    sd = s == unit["sd", 0]
                    if s < NU and not sd:
                        low(s)
                    if there(phase, s - 1) and UNITS[s - 1][0][0] == "s":
                        scale(s - 1)
                    if there(phase, s - 2) and UNITS[s - 2][0][0] != "s":
                        ratio(s - 2)
                    if sample_out:
                        out(s - 4)
                    if sd:
                        low(s)
                    if there(phase, s - 2):
                        take_out(dve, i, phase, "tr", s - 2, range(unit_chunks(s - 2)), copy)
                    for name, j, qs in extras(phase, s):
                        take_out(dve, i, phase, name, j, qs, copy)
                        extra(name, j)
                    if s in SPLIT_AT and not (phase == LAST and SPLIT_AT[s] == NEXT):
                        split(i, SPLIT_AT[s])

            split(0, 0)
            for q in range(PREP_CHUNKS):
                take_chunk(dve, 0, FIRST, q, "prep", 0, q, copy)
            loop(dve, body, ch)


CHAIN_PER_PASS = 36
TAKER = lambda name, j, q: True
CHUNKS = DFF // P
PAIRS = CHUNKS // 2
CONV_W = 3
HALF = D // 2
PARTS = [(0, 512), (512, 512), (SEQ, NS)]
KEPT = (CONV_W - 1) * (1 + DB)


def finish(nc, t, o, scratch):
    with ExitStack() as outer:
        osb = lambda name, shape, dt=F32: outer.enter_context(nc.sbuf_tensor(name, shape, dt))
        ident = osb("f_ident", [P, P])
        x = osb("f_x", [P, STEPS, D])
        h_hi = osb("f_h_hi", [P, KC, TOK], F32R)
        h_lo = osb("f_h_lo", [P, KC, TOK], F32R)
        out_project(nc, t, scratch, ident, x, h_hi, h_lo)
        mix_channels(nc, t, o, ident, x, h_hi, h_lo)


def out_project(nc, t, scratch, ident, x, h_hi, h_lo):
    with ExitStack() as ctx:
        sb = lambda name, shape, dt=F32: ctx.enter_context(nc.sbuf_tensor(name, shape, dt))
        ps = lambda name, shape: ctx.enter_context(nc.psum_tensor(name, shape, F32))
        sem = lambda name: ctx.enter_context(nc.semaphore(name))
        w_hi = sb("o_w_hi", [P, KC, D], F32R)
        w_lo = sb("o_w_lo", [P, KC, D], F32R)
        rows = sb("o_rows", [P, 2, D])
        heads_s = sb("o_heads_s", [P, KC, NS])
        hn = sb("o_hn", [P, 2, D])
        o_hi = sb("o_o_hi", [P, 2, KC, P], F32R)
        o_lo = sb("o_o_lo", [P, 2, KC, P], F32R)
        gain = sb("o_gain", [P, D])
        ss = sb("o_ss", [P, 2])
        root = sb("o_root", [P, 2])
        rroot = sb("o_rroot", [P, 2])
        epst = sb("o_eps", [P, 1])
        po = ps("o_po", [P, D])
        ph = ps("o_ph", [P, D])
        py = [ps(f"o_py{k}", [P, D]) for k in range(2)]
        const_in, x_in, eps_set, vchain = sem("o_const_in"), sem("o_x_in"), sem("o_eps_set"), sem("o_vchain")
        w_in = [sem(f"o_w_in{k}") for k in range(2)]
        rows_in = [sem(f"o_rows_in{k}") for k in range(2)]
        w_hi_done, w_lo_done = sem("o_w_hi_done"), sem("o_w_lo_done")
        o_turned, o_hi_done, o_lo_done = sem("o_o_turned"), sem("o_o_hi_done"), sem("o_o_lo_done")
        y_filled, y_added = sem("o_y_filled"), sem("o_y_added")
        squared, rooted, h_ready = sem("o_squared"), sem("o_rooted"), sem("o_h_ready")
        h_turned, h_hi_done, h_lo_done = sem("o_h_turned"), sem("o_h_hi_done"), sem("o_h_lo_done")
        block = ctx.enter_context(nc.Block())

        def tile_rows(i):
            return NS if isinstance(i, int) and i == STEPS // 2 else P

        def tokens(i, k):
            if tile_rows(i) == NS:
                return slice(SEQ, TOK)
            return bass.ds(i * 2 * P + k * P, P) if not isinstance(i, int) else slice((2 * i + k) * P, (2 * i + k + 1) * P)

        def x_rows(i, k):
            r = tile_rows(i)
            if isinstance(i, int):
                return x[0:r, 2 * i + k, :]
            return x[0:r, bass.ds(i * 2 + k, 1), :].rearrange("p a n -> p (a n)")

        def loop_tiles(eng, tile):
            tile(0, 0)
            tile(0, 1)
            with eng.Fori(1, TILES // 2 - 1) as i:
                tile(i, 0)
                tile(i, 1)
            tile(TILES // 2 - 1, 0)
            tile(TILES // 2 - 1, 1)
            tile(TILES // 2, 0)

        def after(i, k, n):
            if isinstance(i, int):
                s = 2 * i + k + n
                return (s // 2, s % 2) if 0 <= s < STEPS else None
            return i + (k + n) // 2, (k + n) % 2

        chunks = lambda ap: ap.rearrange("p (c q) -> p c q", c=KC)

        @block.sync
        def _(sp):
            sp.dma_start(ident[:], t["ident"]).then_inc(const_in, 16)
            for n in range(2):
                sp.dma_start(rows[:, n, :], scratch["o"][n * P:(n + 1) * P, :]).then_inc(rows_in[n], 16)
            for c in range(KC):
                if c >= 2:
                    sp.wait_ge(w_lo_done, c - 1)
                for dst, src in w_o_rows(t, c):
                    sp.dma_start(hn[dst, c % 2, :], src).then_inc(w_in[c % 2], 16)
                if c == 1:
                    sp.dma_start(heads_s[:], scratch["oT"]).then_inc(const_in, 16)
                    sp.dma_start(gain[:], t["g_ffn"]).then_inc(const_in, 16)
                    sp.dma_start(x[:, 0:TILES, :], t["x_prompt"].rearrange("b (a p) d -> p (b a) d", p=P)).then_inc(x_in, 16)
                    sp.dma_start(x[0:NS, TILES, :], t["x_sample"].rearrange("b s d -> (b s) d")).then_inc(x_in, 16)

            def load(i, k):
                nxt = after(i, k, 2)
                if nxt is None or tile_rows(nxt[0]) == NS:
                    return
                sp.wait_ge(o_turned, i * 2 + (k + 1))
                sp.dma_start(rows[:, k, :], scratch["o"][tokens(*nxt), :]).then_inc(rows_in[k], 16)

            loop_tiles(sp, load)

        @block.gpsimd
        def _(pool):
            nc.gpsimd.memset(epst[:], EPS).then_inc(eps_set, 1)

        @block.tensor
        def _(pe):
            pe.sem_inc(h_turned, 1)
            pe.wait_ge(const_in, 48)

            def turn_o(i, k):
                if tile_rows(i) == NS:
                    return
                pe.wait_ge(rows_in[k], i * 16 + 16)
                if not (isinstance(i, int) and i == 0 and k == 0):
                    pe.wait_ge(o_lo_done, i * 2 + k)
                for c in range(KC):
                    last = nc.tensor.transpose(po[:, c * P:(c + 1) * P], rows[:, k, c * P:(c + 1) * P], ident[:])
                last.then_inc(o_turned, 1)

            def turn_h(i, k):
                r = tile_rows(i)
                pe.wait_ge(h_ready, i * 2 + (k + 1))
                pe.wait_ge(h_lo_done, i * 2 + (k + 0))
                for c in range(KC):
                    last = nc.tensor.transpose(ph[:, c * P:c * P + r], hn[0:r, k, c * P:(c + 1) * P], ident[0:r, 0:r])
                last.then_inc(h_turned, 1)

            turn_o(0, 0)
            pe.wait_ge(w_lo_done, KC)

            def tile(i, k):
                r = tile_rows(i)
                nxt, prev = after(i, k, 1), after(i, k, -1)
                if nxt is not None:
                    turn_o(*nxt)
                pe.wait_ge(o_lo_done, i * 2 + (k + 1))
                pe.wait_ge(y_added, i * 2 + (k + 1))
                for half in range(2):
                    hs = slice(half * HALF, (half + 1) * HALF)
                    for j, (a, w) in enumerate(((o_hi, w_hi), (o_hi, w_lo), (o_lo, w_hi))):
                        for c in range(KC):
                            last = nc.tensor.matmul(py[k][0:r, hs], a[:, k, c, 0:r], w[:, c, hs], start=(j == 0 and c == 0), stop=(j == 2 and c == KC - 1))
                last.then_inc(y_filled, 1)
                if prev is not None:
                    turn_h(*prev)

            loop_tiles(pe, tile)
            turn_h(TILES // 2, 0)

        @block.scalar
        def _(act):
            act.wait_ge(eps_set, 1)

            def split_o(i, k):
                r = tile_rows(i)
                if r == NS:
                    src = heads_s[:]
                    act.wait_ge(const_in, 48)
                else:
                    act.wait_ge(o_turned, i * 2 + (k + 1))
                    src = chunks(po[:])
                if not (isinstance(i, int) and i == 0):
                    act.wait_ge(y_filled, i * 2 + k - 1)
                nc.scalar.activation(o_hi[:, k, :, 0:r], src, ACT.Copy).then_inc(o_hi_done, 1)

            def split_h(i, k):
                r = tile_rows(i)
                act.wait_ge(h_turned, i * 2 + (k + 2))
                nc.scalar.activation(h_hi[:, :, tokens(i, k)], chunks(ph[:])[:, :, 0:r], ACT.Copy).then_inc(h_hi_done, 1)

            for c in range(KC):
                act.wait_ge(w_in[c % 2], 16 * sum(len(w_o_rows(t, d)) for d in range(c % 2, c + 1, 2)))
                nc.scalar.activation(w_hi[:, c, :], hn[:, c % 2, :], ACT.Copy).then_inc(w_hi_done, 1)
            split_o(0, 0)

            def tile(i, k):
                r = tile_rows(i)
                nxt, prev = after(i, k, 1), after(i, k, -1)
                if nxt is not None:
                    split_o(*nxt)
                act.wait_ge(y_added, i * 2 + (k + 3))
                if isinstance(i, int) and i == 0:
                    act.wait_ge(w_lo_done, KC)
                else:
                    act.wait_ge(h_turned, i * 2 + k)
                nc.scalar.activation(hn[0:r, k, :], x_rows(i, k), ACT.Square, accum_out=ss[0:r, k:k + 1]).then_inc(squared, 1)
                act.wait_ge(squared, i * 2 + (k + 1))
                nc.scalar.activation(root[0:r, k:k + 1], ss[0:r, k:k + 1], ACT.Sqrt, bias=epst[0:r, :], scale=1.0 / D).then_inc(rooted, 1)
                if prev is not None:
                    split_h(*prev)

            loop_tiles(act, tile)
            split_h(TILES // 2, 0)

        @block.vector
        def _(dve):
            dve.sem_inc(y_added, 2)
            dve.wait_ge(const_in, 48)
            for c in range(KC):
                dve.wait_ge(w_hi_done, c + 1)
                nc.vector.tensor_tensor(w_lo[:, c, :], hn[:, c % 2, :], w_hi[:, c, :].bitcast(F32), ALU.subtract).then_inc(w_lo_done, 1)

            def split_o(i, k):
                r = tile_rows(i)
                src = heads_s[:] if r == NS else chunks(po[:])
                dve.wait_ge(o_hi_done, i * 2 + (k + 1))
                nc.vector.tensor_tensor(o_lo[:, k, :, 0:r], src, o_hi[:, k, :, 0:r].bitcast(F32), ALU.subtract).then_inc(o_lo_done, 1)

            def split_h(i, k):
                r, tok = tile_rows(i), tokens(i, k)
                dve.wait_ge(h_hi_done, i * 2 + (k + 1))
                nc.vector.tensor_tensor(h_lo[:, :, tok], chunks(ph[:])[:, :, 0:r], h_hi[:, :, tok].bitcast(F32), ALU.subtract).then_inc(h_lo_done, 1)

            split_o(0, 0)
            dve.wait_ge(x_in, 32)

            def tile(i, k):
                r = tile_rows(i)
                nxt, prev = after(i, k, 1), after(i, k, -1)
                if nxt is not None:
                    split_o(*nxt)
                dve.wait_ge(y_filled, i * 2 + (k + 1))
                xr = x_rows(i, k)
                nc.vector.tensor_tensor(xr, py[k][0:r, :], xr, ALU.add).then_inc(y_added, 1)
                dve.wait_ge(rooted, i * 2 + (k + 1))
                rr = rroot[0:r, k:k + 1]
                nc.vector.reciprocal(rr, root[0:r, k:k + 1]).then_inc(vchain, 1)
                dve.wait_ge(vchain, i * 2 + (k + 1))
                nc.vector.scalar_tensor_tensor(out=hn[0:r, k, :], in0=xr, scalar=rr, in1=gain[0:r, :], op0=ALU.mult, op1=ALU.mult).then_inc(h_ready, 1)
                if prev is not None:
                    split_h(*prev)

            loop_tiles(dve, tile)
            split_h(TILES // 2, 0)


def w_o_rows(t, c):
    w = t["w_o"]
    if c >= RA:
        return [(slice(0, P), w[c * P:(c + 1) * P, :])]
    return [(slice(g * E, (g + 1) * E), w[(g * RA + c) * E:(g * RA + c + 1) * E, :]) for g in range(GA)]


def mix_channels(nc, t, o, ident, x, h_hi, h_lo):
    with ExitStack() as ctx:
        sb = lambda name, shape, dt=F32: ctx.enter_context(nc.sbuf_tensor(name, shape, dt))
        ps = lambda name, shape: ctx.enter_context(nc.psum_tensor(name, shape, F32))
        sem = lambda name: ctx.enter_context(nc.semaphore(name))
        raw = sb("m_raw", [P, 4 * D])
        raw_gu = raw[:, 0:2 * D].rearrange("p (m c n) -> p m c n", m=2, c=KC)
        raw_d = raw[:, 2 * D:4 * D].rearrange("p (k n) -> p k n", k=2)
        gu_hi = [sb(f"m_gu_hi{k}", [P, 2, KC, P], F32R) for k in range(2)]
        gu_lo = [sb(f"m_gu_lo{k}", [P, 2, KC, P], F32R) for k in range(2)]
        wd_hi = sb("m_wd_hi", [P, 2, D], F32R)
        wd_lo = sb("m_wd_lo", [P, 2, D], F32R)
        ext = sb("m_ext", [P, CONV_W - 1 + SEQ])
        ext_s = sb("m_ext_s", [P, DB, CONV_W - 1 + DT])
        conv = [sb(f"m_conv{k}", [P, 512]) for k in range(2)]
        gated = [sb(f"m_gated{k}", [P, 512]) for k in range(2)]
        g_hi = sb("m_g_hi", [P, 2, TOK], F32R)
        g_lo = sb("m_g_lo", [P, 2, TOK], F32R)
        past = sb("m_past", [P, CHUNKS, (CONV_W - 1) * DB])
        kept = sb("m_kept", [P, CHUNKS, KEPT])
        taps_all = sb("m_taps_all", [P, CHUNKS, 4])
        taps = sb("m_taps", [P, 2, 4])
        pa = [ps(f"m_pa{k}", [P, 512]) for k in range(2)]
        pu = [ps(f"m_pu{k}", [P, 512]) for k in range(2)]
        pd = [ps(f"m_pd{k}", [P, 512]) for k in range(3)]
        psm = ps("m_psm", [P, 512])
        rows_s = sb("m_rows_s", [NS, 2 * P])
        (taps_in, state_in, state_turned, past_done, gu_in, wd_in, gu_hi_done, gu_lo_done, wd_hi_done, wd_lo_done, filled, copied,
         convolved, silu_done, g_made, g_hi_done, g_lo_done, d_filled, d_added, taps_ready, vchain, zeroed, kept_turned, kept_rows, y_out,
         s_filled, s_copied, passed) = (
            sem("m_" + n) for n in ("taps_in state_in state_turned past_done gu_in wd_in gu_hi_done gu_lo_done wd_hi_done wd_lo_done filled "
                                    "copied convolved silu_done g_made g_hi_done g_lo_done d_filled d_added taps_ready vchain zeroed kept_turned kept_rows y_out "
                                    "s_filled s_copied passed").split())
        UNITS_D = 2 * STEPS
        NP = 6
        block = ctx.enter_context(nc.Block())

        DOWN = [*range(0, 8), 16, 17, *range(8, 16)]
        DOWN_AFTER = {0: range(0, 10), 2: range(10, 18)}

        def banks(q, w):
            if q % 3 == 2:
                return psm[:, 2 * P:2 * P + NS], psm[:, 2 * P + NS:2 * P + 2 * NS]
            return pa[q % 3][:, 0:w], pu[q % 3][:, 0:w]

        def chunk_in(i, k):
            return bass.ds(i * 2 + k, 1) if not isinstance(i, int) else slice(2 * i + k, 2 * i + k + 1)

        def loop_pairs(eng, body):
            body(0, True, False)
            with eng.Fori(1, PAIRS - 1) as i:
                body(i, False, False)
            body(PAIRS - 1, False, True)

        @block.sync
        def _(sp):
            sp.dma_start(taps_all[:], t["taps"]).then_inc(taps_in, 16)
            sp.dma_start(raw[0:(CONV_W - 1) * DB, 0:DFF], t["state_conv"].rearrange("b w f -> (b w) f")).then_inc(state_in, 16)

            def load_gu(i, k):
                for m, name in enumerate(("w_gate", "w_up")):
                    n0 = i * 2 * P + k * P
                    cols = bass.ds(n0, P) if not isinstance(i, int) else slice(n0, n0 + P)
                    sp.dma_start(raw_gu[:, m], t[name][:, cols].rearrange("(c p) n -> p c n", p=P)).then_inc(gu_in, 16)

            def load_wd(i):
                at = i * 2 * P
                rows = bass.ds(at, 2 * P) if not isinstance(i, int) else slice(at, at + 2 * P)
                sp.dma_start(raw_d, t["w_down"][rows, :].rearrange("(k p) n -> p k n", p=P)).then_inc(wd_in, 16)

            sp.wait_ge(state_turned, 1)
            load_gu(0, 0)
            load_wd(0)

            def body(i, more):
                sp.wait_ge(gu_lo_done, i * 2 + 1)
                load_gu(i, 1)
                if more:
                    sp.wait_ge(gu_lo_done, i * 2 + 2)
                    load_gu(i + 1, 0)
                    sp.wait_ge(wd_lo_done, i + 1)
                    load_wd(i + 1)

            with sp.Fori(0, PAIRS - 1) as i:
                body(i, True)
            body(PAIRS - 1, False)
            for n in range(STEPS):
                sp.wait_ge(d_added, 3 + (PAIRS - 1) * UNITS_D + DOWN.index(2 * n + 1) + 1)
                if n < TILES:
                    sp.dma_start(o["y_prompt"][0, n * P:(n + 1) * P, :], x[:, n, :]).then_inc(y_out, 16)
                else:
                    sp.dma_start(o["y_sample"].rearrange("b s d -> (b s) d"), x[0:NS, n, :]).then_inc(y_out, 16)
            sp.wait_ge(kept_rows, 6)
            sp.dma_start(o["conv_prompt"].rearrange("b w f -> (b w) f"), raw[0:CONV_W - 1, 0:DFF]).then_inc(y_out, 16)
            sp.dma_start(o["conv_sample"].rearrange("b w f -> (b w) f"), raw[CONV_W - 1:KEPT, 0:DFF]).then_inc(y_out, 16)
            sp.wait_ge(y_out, 16 * (STEPS + 2))

        @block.gpsimd
        def _(pool):
            nc.gpsimd.memset(ext[:, 0:CONV_W - 1], 0.0).then_inc(zeroed, 1)
            pool.wait_ge(taps_in, 16)
            nc.gpsimd.tensor_copy(taps[:], taps_all[:, 0:2, :]).then_inc(taps_ready, 1)
            with pool.Fori(1, PAIRS) as i:
                pool.wait_ge(g_made, i * NP)
                nc.gpsimd.tensor_copy(taps[:], taps_all[:, bass.ds(i * 2, 2), :]).then_inc(taps_ready, 1)

        @block.tensor
        def _(pe):
            pe.wait_ge(state_in, 16)
            for c in range(CHUNKS):
                last = nc.tensor.transpose(pd[0][:, c * 16:(c + 1) * 16], raw[0:16, c * P:(c + 1) * P], ident[0:16, 0:16])
            last.then_inc(state_turned, 1)
            pe.wait_ge(past_done, 1)

            products = ((gu_hi, h_hi), (gu_hi, h_lo), (gu_lo, h_hi))

            def part(i, q):
                k, (t0, w) = q // 3, PARTS[q % 3]
                if q % 3 == 0:
                    pe.wait_ge(gu_lo_done, i * 2 + (k + 1))
                if q >= 3 or not isinstance(i, int) or i > 0:
                    pe.wait_ge(g_made, i * NP + (q - 2))
                for m, bank in enumerate((pa, pu)):
                    for j, (ws, hs) in enumerate(products):
                        for c in range(KC):
                            last = nc.tensor.matmul(bank[q % 3][:, 0:w], ws[k][:, m, c, :], hs[:, c, t0:t0 + w], start=(j == 0 and c == 0), stop=(j == 2 and c == KC - 1))
                last.then_inc(filled, 1)

            def part_s(i, k):
                if k > 0 or not isinstance(i, int) or i > 0:
                    pe.wait_ge(g_made, i * NP + 3 * k)
                for j, (ws, hs) in enumerate(products):
                    for c in range(KC):
                        last = nc.tensor.matmul(psm[0:NS, 0:2 * P].rearrange("p (m n) -> p m n", m=2), hs[:, c, SEQ:TOK], ws[k][:, :, c, :],
                                                start=(j == 0 and c == 0), stop=(j == 2 and c == KC - 1))
                last.then_inc(s_filled, 1)

            def turn_s(i, k):
                pe.wait_ge(s_copied, i * 2 + (k + 1))
                pe.sem_inc(passed, 1)
                for m in range(2):
                    last = nc.tensor.transpose(psm[:, 2 * P + m * NS:2 * P + (m + 1) * NS], rows_s[:, m * P:(m + 1) * P], ident[0:NS, 0:NS])
                last.then_inc(filled, 1)

            def down(i, units):
                for d in units:
                    tile, half = DOWN[d] // 2, DOWN[d] % 2
                    r = P if tile < TILES else NS
                    tok, hs = slice(tile * P, tile * P + r), slice(half * HALF, (half + 1) * HALF)
                    if d == 0:
                        pe.wait_ge(wd_lo_done, i + 1)
                    if d in (0, 8, 10):
                        pe.wait_ge(g_lo_done, i * NP + {0: 4, 8: 6, 10: 5}[d])
                    pe.wait_ge(d_added, i * UNITS_D + (d + 1))
                    for n in range(6):
                        k, j = n // 3, n % 3
                        a, w = ((g_hi, wd_hi), (g_hi, wd_lo), (g_lo, wd_hi))[j]
                        last = nc.tensor.matmul(pd[d % 3][0:r, :], a[:, k, tok], w[:, k, hs], start=(n == 0), stop=(n == 5))
                    last.then_inc(d_filled, 1)

            def body(i, first, last):
                part(i, 0)
                if not first:
                    down(i - 1, DOWN_AFTER[0])
                part_s(i, 0)
                part(i, 1)
                turn_s(i, 0)
                if not first:
                    down(i - 1, DOWN_AFTER[2])
                part(i, 3)
                part_s(i, 1)
                part(i, 4)
                turn_s(i, 1)

            loop_pairs(pe, body)
            down(PAIRS - 1, range(UNITS_D))
            for n in range(6):
                if n < 4:
                    bank = (pa + pu)[n]
                else:
                    bank = pa[n - 4]
                    pe.wait_ge(kept_rows, n - 3)
                for c in range(4 * n, min(4 * n + 4, CHUNKS)):
                    last = nc.tensor.transpose(bank[0:KEPT, (c % 4) * P:(c % 4 + 1) * P], kept[:, c, :], ident[:])
                last.then_inc(kept_turned, 1)

        @block.scalar
        def _(act):
            act.wait_ge(past_done, 1)
            act.wait_ge(zeroed, 1)

            def split_gu(i, k):
                act.wait_ge(gu_in, i * 64 + (k + 1) * 32)
                nc.scalar.activation(gu_hi[k][:], raw_gu, ACT.Copy).then_inc(gu_hi_done, 1)

            def split_g(i, q):
                k, (t0, w) = q // 3, PARTS[q % 3]
                act.wait_ge(g_made, i * NP + (q + 1))
                nc.scalar.activation(g_hi[:, k, t0:t0 + w], gated[q % 2][:, 0:w], ACT.Copy).then_inc(g_hi_done, 1)

            split_gu(0, 0)

            def body(i, first, last):
                for q in range(NP):
                    k, (t0, w) = q // 3, PARTS[q % 3]
                    a, c = banks(q, w)[0], conv[q % 2][:, 0:w]
                    if q == 0:
                        act.wait_ge(taps_ready, i + 1)
                    if q % 3 == 1:
                        act.wait_ge(s_filled, i * 2 + (k + 1))
                        nc.scalar.activation(rows_s[:], psm[0:NS, 0:2 * P], ACT.Copy).then_inc(s_copied, 1)
                    act.wait_ge(filled, i * NP + (q + 1))
                    nc.scalar.activation(c, a, ACT.Identity, bias=taps[:, k, 3:4], scale=taps[:, k, 2:3])
                    if q % 3 < 2:
                        ins = nc.scalar.activation(ext[:, CONV_W - 1 + t0:CONV_W - 1 + t0 + w], a, ACT.Copy)
                    else:
                        nc.scalar.activation(ext_s[:, :, 0:CONV_W - 1], past[:, chunk_in(i, k), :].rearrange("p a (b w) -> p (a b) w", w=CONV_W - 1), ACT.Copy)
                        ins = nc.scalar.activation(ext_s[:, :, CONV_W - 1:], a.rearrange("p (b s) -> p b s", s=DT), ACT.Copy)
                    ins.then_inc(copied, 1)
                    if q % 3 == 1:
                        nc.scalar.activation(kept[:, chunk_in(i, k), 0:CONV_W - 1], a[:, w - CONV_W + 1:w].unsqueeze(1), ACT.Copy)
                    if q % 3 == 2:
                        nc.scalar.activation(kept[:, chunk_in(i, k), CONV_W - 1:KEPT].rearrange("p a (b w) -> p (a b) w", w=CONV_W - 1),
                                             a.rearrange("p (b s) -> p b s", s=DT)[:, :, DT - CONV_W + 1:], ACT.Copy)
                    act.wait_ge(convolved, i * NP + (q + 1))
                    nc.scalar.activation(c, c, ACT.Silu).then_inc(silu_done, 1)
                    if q == 0:
                        if not first:
                            split_g(i - 1, NP - 1)
                        split_gu(i, 1)
                    else:
                        if not first and q <= 2:
                            act.wait_ge(d_filled, (i - 1) * UNITS_D + (8, UNITS_D)[q - 1])
                        split_g(i, q - 1)
                    if q == 3 and not last:
                        split_gu(i + 1, 0)
                    if q == 4:
                        act.wait_ge(wd_in, i * 16 + 16)
                        nc.scalar.activation(wd_hi[:], raw_d, ACT.Copy).then_inc(wd_hi_done, 1)

            loop_pairs(act, body)
            split_g(PAIRS - 1, NP - 1)

        @block.vector
        def _(dve):
            dve.sem_inc(d_added, 3)
            dve.wait_ge(state_turned, 1)
            nc.vector.tensor_copy(past[:].rearrange("p c n -> p (c n)"), pd[0][:, 0:CHUNKS * 16]).then_inc(past_done, 1)

            def split_gu(i, k):
                dve.wait_ge(gu_hi_done, i * 2 + (k + 1))
                nc.vector.tensor_tensor(gu_lo[k][:], raw_gu, gu_hi[k][:].bitcast(F32), ALU.subtract).then_inc(gu_lo_done, 1)

            def split_g(i, q):
                k, (t0, w) = q // 3, PARTS[q % 3]
                dve.wait_ge(g_hi_done, i * NP + (q + 1))
                nc.vector.tensor_tensor(g_lo[:, k, t0:t0 + w], gated[q % 2][:, 0:w], g_hi[:, k, t0:t0 + w].bitcast(F32), ALU.subtract).then_inc(g_lo_done, 1)

            def add(i, units):
                for d in units:
                    tile, half = DOWN[d] // 2, DOWN[d] % 2
                    r = P if tile < TILES else NS
                    xs = x[0:r, tile, half * HALF:(half + 1) * HALF]
                    dve.wait_ge(d_filled, i * UNITS_D + (d + 1))
                    nc.vector.tensor_tensor(xs, pd[d % 3][0:r, :], xs, ALU.add).then_inc(d_added, 1)

            split_gu(0, 0)

            def body(i, first, last):
                for q in range(NP):
                    k, (t0, w) = q // 3, PARTS[q % 3]
                    c, u = conv[q % 2][:, 0:w], banks(q, w)[1]
                    dve.wait_ge(copied, i * NP + (q + 1))
                    if q % 3 < 2:
                        taps_at = [ext[:, t0 + n:t0 + n + w] for n in range(2)]
                        cv = c
                    else:
                        taps_at = [ext_s[:, :, n:n + DT] for n in range(2)]
                        cv = c.rearrange("p (b s) -> p b s", s=DT)
                    nc.vector.scalar_tensor_tensor(out=cv, in0=taps_at[1], scalar=taps[:, k, 1:2], in1=cv, op0=ALU.mult, op1=ALU.add).then_inc(vchain, 1)
                    dve.wait_ge(vchain, i * NP + (q + 1))
                    nc.vector.scalar_tensor_tensor(out=cv, in0=taps_at[0], scalar=taps[:, k, 0:1], in1=cv, op0=ALU.mult, op1=ALU.add).then_inc(convolved, 1)
                    if not first:
                        add(i - 1, {0: range(0, 2), 1: range(10, 11), 2: range(12, 13)}.get(q, ()))
                    dve.wait_ge(silu_done, i * NP + (q + 1))
                    nc.vector.tensor_tensor(gated[q % 2][:, 0:w], c, u, ALU.mult).then_inc(g_made, 1)
                    if not first and q == 0:
                        split_g(i - 1, NP - 1)
                    if not first:
                        add(i - 1, {0: range(2, 10), 1: range(11, 12), 2: range(13, 18)}.get(q, ()))
                    if q > 0:
                        split_g(i, q - 1)
                    if q == 0:
                        split_gu(i, 1)
                    if q == 3 and not last:
                        split_gu(i + 1, 0)
                    if q == 4:
                        dve.wait_ge(wd_hi_done, i + 1)
                        nc.vector.tensor_tensor(wd_lo[:], raw_d, wd_hi[:].bitcast(F32), ALU.subtract).then_inc(wd_lo_done, 1)

            loop_pairs(dve, body)
            split_g(PAIRS - 1, NP - 1)
            add(PAIRS - 1, range(UNITS_D))
            for n in range(6):
                w = (min(4 * n + 4, CHUNKS) - 4 * n) * P
                bank = (pa + pu)[n] if n < 4 else pa[n - 4]
                dve.wait_ge(kept_turned, n + 1)
                nc.vector.tensor_copy(raw[0:KEPT, 4 * n * P:4 * n * P + w], bank[0:KEPT, 0:w]).then_inc(kept_rows, 1)


def rope_table():
    half = ROT // 2
    inv = np.float32(500000.0) ** (np.float32(-2.0) * np.arange(half, dtype=np.float32) / np.float32(ROT))
    pos = np.concatenate([np.arange(SEQ), np.tile(PAST + np.arange(DT), DB)]).astype(np.float32)
    ang = (pos[:, None] * inv.astype(np.float32)[None, :]).astype(np.float64)
    c, s = np.cos(ang), np.sin(ang)
    return np.concatenate([c, c, -s, s], 1).astype(np.float32)


OUTS = {
    "y_prompt": (1, SEQ, D), "y_sample": (DB, DT, D),
    "cmp_prompt": (1, SEQ, 2, GA, E), "cmp_sample": (DB, DT, 2, GA, E),
    "slc_prompt": (1, SEQ, 2, GA, E), "slc_sample": (DB, DT, 2, GA, E),
    "win_prompt": (1, WIN, 2, GA, E), "win_sample": (DB, WIN, 2, GA, E),
    "dil_prompt": (1, SEQ, 2, HB, E), "dil_sample": (DB, PAST + DT, 2, HB, E),
    "conv_prompt": (1, CONV_W - 1, DFF), "conv_sample": (DB, CONV_W - 1, DFF),
}
SCRATCH = {"qa": (TOK, HA * E), "qb": (TOK, HB * E), "kvw": (TOK, 2 * GA * E), "gl": (TOK, 3 * HA), "kvc": (NS, 2, GA, E),
           "o": (SEQ, D), "oT": (P, KC, NS)}


def build(nc, t, o):
    scratch = {n: nc.dram_tensor("scratch_" + n, s, F32, kind="Internal").ap() for n, s in SCRATCH.items()}
    project(nc, t, o, scratch)
    attend(nc, t, o, scratch)
    finish(nc, t, o, scratch)


def kernel(**inputs):
    import concourse.bacc as bacc
    from concourse.bass_utils import run_bass_kernel_spmd

    x = {n: np.asarray(a) for n, a in inputs.items()}
    masks, smask = tables()
    across = lambda a, n: np.broadcast_to(a, (n,) + a.shape)
    gains = np.stack([x[n] for n in ("gq_a", "gk_cmp", "gk_slc", "gk_win", "gq_b", "gk_b")])
    data = {n: x[n] for n in ("x_prompt", "x_sample", "cache_cmp", "cache_slc", "state_win", "state_dil", "state_conv", "page_table",
                              "w_in", "w1_cmp_k", "w2_cmp_k", "w1_cmp_v", "w2_cmp_v", "w_o", "w_gate", "w_up", "w_down")}
    data.update(
        ident=np.eye(P, dtype=np.float32), rope=rope_table(), masks=masks, smask=smask,
        g_attn=x["g_attn"].reshape(KC, P).T, gains=across(gains, P), g_ffn=across(x["g_ffn"], P),
        peT=np.stack([x["pe_cmp_" + n].reshape(CMP_LEN * E // P, P).T for n in "kv"], 1),
        taps=np.concatenate([x["conv_w"], x["conv_b"][None]], 0).reshape(CONV_W + 1, CHUNKS, P).transpose(2, 1, 0))
    data = {n: np.ascontiguousarray(a) for n, a in data.items()}
    nc = bacc.Bacc("TRN2", target_bir_lowering=False, num_devices=1)
    t = {n: nc.dram_tensor("in_" + n, a.shape, mybir.dt.from_np(a.dtype), kind="ExternalInput").ap() for n, a in data.items()}
    o = {n: nc.dram_tensor("out_" + n, s, F32, kind="ExternalOutput").ap() for n, s in OUTS.items()}
    build(nc, t, o)
    r = run_bass_kernel_spmd(nc, [{"in_" + n: a for n, a in data.items()}], core_ids=[0])
    return tuple(r.results[0]["out_" + n] for n in OUTS)
```

```python
from contextlib import ExitStack

import numpy as np

import concourse.bass as bass
from concourse import mybir

F32 = mybir.dt.float32
F32R = mybir.dt.float32r
I32 = mybir.dt.int32
ALU = mybir.AluOpType
ACT = mybir.ActivationFunctionType
AX = mybir.AxisListType.X

P = 128
D = 1024
SEQ = 1024
DB = 8
DT = 8
PAST = 1024
NS = DB * DT
E = 64
HA = 8
HB = 8
GA = 2
RA = HA // GA
ROT = 16
EPS = 1e-6
DFF = 2816
IN_DIM = 2840
PAGE = 128
PAGES = PAST // PAGE
WIN = 512
CMP_STRIDE = 16
CMP_LEN = 32
SLC_BLK = 64
NCMP = PAST // CMP_STRIDE - 1
KC = D // P
TILES = SEQ // P
TOK = SEQ + NS
BIG = 1.0e30
CLAMP = 1.0e20
TINY = 1.0e-30


class Chain:

    def __init__(self, eng, sem):
        self.eng, self.sem, self.n, self.i, self.per = eng, sem, 0, None, 0

    def value(self):
        return self.n if self.i is None else self.i * self.per + self.n

    def step(self, ins):
        self.n += 1
        ins.then_inc(self.sem, 1)
        self.eng.wait_ge(self.sem, self.value())

    def enter(self, i, per, first=0):
        self.n -= first * per
        self.i, self.per, self.start = i, per, self.n

    def leave(self, trips):
        if self.n - self.start != self.per:
            raise ValueError(f"chain steps in a trip: {self.n - self.start}, not {self.per}")
        self.n = self.start + trips * self.per
        self.i = None


GROUPS = [
    ("qa", 0, 512, (2, 4), (0, 1)),
    ("cmp_slc", 512, 512, (2, 2), (1, 3)),
    ("win_gate", 1024, 280, (1, 2), (3, 4)),
    ("qb", 1304, 512, (2, 4), (4, 5)),
    ("kb", 1816, 512, (2, 4), (5, 6)),
    ("vb", 2328, 512, None, None),
]
NG = len(GROUPS)
FIRST_SPLITS = {4: (0, 1), 5: (2, 3), 6: (4, 5), 7: (6, 7)}
STEPS = TILES + 1


def project(nc, t, o, scratch, const):
    with ExitStack() as ctx:
        sb = lambda name, shape, dt=F32: ctx.enter_context(nc.sbuf_tensor(name, shape, dt))
        ps = lambda name, shape: ctx.enter_context(nc.psum_tensor(name, shape, F32))
        sem = lambda name: ctx.enter_context(nc.semaphore(name))

        ident = const.ident
        xin = sb("p_x", [P, 2, D])
        xsq = sb("p_xsq", [P, D])
        xss = sb("p_xss", [P, 2])
        xrt = sb("p_xrt", [P, 2])
        xrr = sb("p_xrr", [P, 2])
        xnT = sb("p_xnT", [P, KC, TOK])
        g_in = sb("p_gin", [P, KC])
        gains = sb("p_gains", [P, 6, E])
        rope = sb("p_rope", [P, STEPS, 2 * ROT])
        epst = sb("p_eps", [P, 1])
        raw = sb("p_raw", [P, KC, 512])
        w_hi = sb("p_whi", [P, 2, KC, 512], F32R)
        w_lo = sb("p_wlo", [P, 2, KC, 512], F32R)
        x_hi = sb("p_xhi", [P, 2, KC, P], F32R)
        x_lo = sb("p_xlo", [P, 2, KC, P], F32R)
        z = sb("p_z", [P, 2, 512])
        zsq = sb("p_zsq", [P, 2, 512])
        zss = sb("p_zss", [P, 2, 8])
        zrt = sb("p_zrt", [P, 2, 8])
        zrr = sb("p_zrr", [P, 2, 8])
        ra = sb("p_ra", [P, 8 * ROT])
        rb = sb("p_rb", [P, 8 * ROT])
        pt = [ps(f"p_pt{k}", [P, D]) for k in range(2)]
        pz = [ps(f"p_pz{k}", [P, 512]) for k in range(2)]

        const_in = sem("p_const_in")
        later_in = sem("p_later_in")
        x_in = [sem(f"p_x_in{k}") for k in range(2)]
        x_square = sem("p_x_square")
        x_root = sem("p_x_root")
        x_normed = sem("p_x_normed")
        x_turned = sem("p_x_turned")
        x_stored = sem("p_x_stored")
        eps_set = sem("p_eps_set")
        raw_in = sem("p_raw_in")
        w_hi_done = sem("p_w_hi_done")
        w_lo_done = sem("p_w_lo_done")
        x_hi_done = sem("p_x_hi_done")
        x_lo_done = sem("p_x_lo_done")
        z_summed = sem("p_z_summed")
        z_copied = sem("p_z_copied")
        z_squared = sem("p_z_squared")
        z_reduced = sem("p_z_reduced")
        z_root = sem("p_z_root")
        z_done = sem("p_z_done")
        z_out = [sem(f"p_z_out{k}") for k in range(2)]
        vchain = sem("p_vchain")

        SAMPLE = TILES // 2

        def rows(i):
            return NS if isinstance(i, int) and i == SAMPLE else P

        def tokens(i, k):
            if isinstance(i, int):
                return slice((2 * i + k) * P, (2 * i + k) * P + rows(i))
            return bass.ds(i * (2 * P) + k * P, P)

        def loop_tiles(eng, body, chain=None, per=0):
            with eng.Fori(0, 3) as i:
                if chain:
                    chain.enter(i, per)
                body(i, 0)
                body(i, 1)
            if chain:
                chain.leave(3)
            body(3, 0)
            body(3, 1)
            body(SAMPLE, 0)

        def normed(G, i, k):
            return sum(g[3] is not None for g in GROUPS[:G]) * STEPS + i * 2 + k + 1

        def stores(G):
            return 1 if GROUPS[G][3] is not None and GROUPS[G][0] in ("qa", "qb", "kb") or GROUPS[G][0] == "vb" else 2

        def stored_before(G, i, k):
            slot = (G + k) % 2
            before = sum(16 * stores(g) * (5 if (slot - g) % 2 == 0 else 4) for g in range(G))
            return i * (16 * stores(G)) + (before + 1)

        block = ctx.enter_context(nc.Block())

        @block.sync
        def _(sp):
            sp.sem_inc(z_out[0], 1)
            sp.sem_inc(z_out[1], 1)
            sp.dma_start(ident[:], t["ident"]).then_inc(const_in, 16)
            sp.dma_start(g_in[:], t["g_attn"]).then_inc(const_in, 16)
            sp.dma_start(gains[:], t["gains"]).then_inc(const_in, 16)
            sp.dma_start(rope[:, 0:TILES, :], t["rope"][0:SEQ, :].rearrange("(a p) c -> p a c", p=P)).then_inc(const_in, 16)
            sp.dma_start(rope[0:NS, TILES, :], t["rope"][SEQ:TOK, :]).then_inc(const_in, 16)
            for n in range(STEPS):
                r = P if n < TILES else NS
                src = t["x_prompt"][0, n * P:(n + 1) * P, :] if n < TILES else t["x_sample"].rearrange("b t d -> (b t) d")
                if n >= 2:
                    sp.wait_ge(x_turned, n - 1)
                sp.dma_start(xin[0:r, n % 2, :], src).then_inc(x_in[n % 2], 16)
                if n == 1:
                    sp.dma_start(raw[:], t["w_in"][:, 0:512].rearrange("(c p) n -> p c n", p=P)).then_inc(raw_in, 16)
            for G, (name, c0, wd, heads, _) in enumerate(GROUPS):
                if G + 1 < NG:
                    sp.wait_ge(w_lo_done, KC + 4 * G)
                    c1, w1 = GROUPS[G + 1][1:3]
                    sp.dma_start(raw[:, :, 0:w1], t["w_in"][:, c1:c1 + w1].rearrange("(c p) n -> p c n", p=P)).then_inc(raw_in, 16)

                if G == 0:
                    for dst, src in const.loads:
                        sp.dma_start(dst, src).then_inc(later_in, 16)

                def store_tile(i, k, G=G, name=name, heads=heads):
                    slot = (G + k) % 2
                    r = rows(i)
                    last = r == NS
                    if heads is not None:
                        sp.wait_ge(z_done, normed(G, i, k))
                    else:
                        sp.wait_ge(z_copied, i * 2 + (k + G * STEPS + 3))
                    tok = slice(0, NS) if last else tokens(i, k)
                    src = z[0:r, slot, :]
                    if name in ("qa", "qb"):
                        sp.dma_start(scratch[name][tokens(i, k), :], src).then_inc(z_out[slot], 16)
                    elif name == "win_gate":
                        sp.dma_start(scratch["kvw"][tokens(i, k), :], src[:, 0:256]).then_inc(z_out[slot], 16)
                        sp.dma_start(scratch["gl"][tokens(i, k), :], src[:, 256:280]).then_inc(z_out[slot], 16)
                    elif name == "cmp_slc":
                        for j, x in enumerate(("cmp", "slc")):
                            dst = o[x + ("_sample" if last else "_prompt")].rearrange("b s c g e -> (b s) (c g e)")
                            sp.dma_start(dst[tok, :], src[:, 256 * j:256 * j + 256]).then_inc(z_out[slot], 16)
                    else:
                        c = 0 if name == "kb" else 1
                        if last:
                            sp.dma_start(o["dil_sample"][:, PAST:PAST + DT, c, :, :].rearrange("b s h e -> b s (h e)"),
                                         src).then_inc(z_out[slot], 16)
                        else:
                            sp.dma_start(o["dil_prompt"][0, tok, c, :, :].rearrange("s h e -> s (h e)"), src).then_inc(z_out[slot], 16)

                loop_tiles(sp, store_tile)
            sp.wait_ge(later_in, 16 * len(const.loads))
            for k in range(2):
                sp.wait_ge(z_out[k], 1 + sum(16 * stores(g) * (5 if (k - g) % 2 == 0 else 4) for g in range(NG)))

        @block.gpsimd
        def _(pool):
            nc.gpsimd.memset(epst[:], EPS).then_inc(eps_set, 1)

        @block.scalar
        def _(act):
            act.sem_inc(z_copied, 2)
            act.wait_ge(eps_set, 1)
            for n in range(STEPS):
                r, s = (P if n < TILES else NS), slice(n % 2, n % 2 + 1)
                act.wait_ge(x_in[n % 2], 16 * (n // 2 + 1))
                if n >= 2:
                    act.wait_ge(x_normed, n - 1)
                if n >= 1:
                    act.wait_ge(x_square, n)
                nc.scalar.activation(xsq[0:r, :], xin[0:r, n % 2, :], ACT.Square, accum_out=xss[0:r, s]).then_inc(x_square, 1)
                act.wait_ge(x_square, n + 1)
                nc.scalar.activation(xrt[0:r, s], xss[0:r, s], ACT.Sqrt, bias=epst[0:r, :], scale=1.0 / D).then_inc(x_root, 1)
                for c in FIRST_SPLITS.get(n, ()):
                    act.wait_ge(raw_in, 16)
                    nc.scalar.activation(w_hi[:, 0, c, :], raw[:, c, :], ACT.Copy).then_inc(w_hi_done, 1)

            def split_x(slot, i, k):
                r = rows(i)
                nc.scalar.activation(x_hi[:, slot, :, 0:r], xnT[:, :, tokens(i, k)], ACT.Copy).then_inc(x_hi_done, 1)

            act.wait_ge(x_stored, STEPS)
            split_x(0, 0, 0)
            split_x(1, 0, 1)
            for G, (name, c0, wd, heads, _) in enumerate(GROUPS):
                def tile(i, k, G=G, heads=heads, wd=wd):
                    slot = (G + k) % 2
                    r = rows(i)
                    act.wait_ge(z_summed, i * 2 + (k + G * STEPS + 1))
                    act.wait_ge(z_out[slot], stored_before(G, i, k))
                    nc.scalar.activation(z[0:r, slot, 0:wd], pz[slot][0:r, 0:wd], ACT.Copy).then_inc(z_copied, 1)
                    if r == NS:
                        i2, k2, more = 0, 1, G + 1 < NG
                    elif isinstance(i, int) and k == 1:
                        i2, k2, more = 0, 0, G + 1 < NG
                    else:
                        i2, k2, more = i + 1, k, True
                    if more:
                        split_x(slot, i2, k2)
                    if heads is not None:
                        a, h = heads
                        act.wait_ge(z_copied, i * 2 + (k + G * STEPS + 3))
                        nc.scalar.activation(zsq[0:r, slot, 0:a * h * E].rearrange("p (a h e) -> p a h e", h=h, e=E),
                                             z[0:r, slot, 0:a * 256].rearrange("p (a h e) -> p a h e", h=4, e=E)[:, :, 0:h, :],
                                             ACT.Square).then_inc(z_squared, 1)
                    if G + 1 < NG and k == 1:
                        w = GROUPS[G + 1][2]
                        act.wait_ge(raw_in, 16 * (G + 2))
                        cs = bass.ds(i * 2, 2)
                        nc.scalar.activation(w_hi[:, (G + 1) % 2, cs, 0:w], raw[:, cs, 0:w], ACT.Copy).then_inc(w_hi_done, 1)
                    if heads is not None:
                        a, h = heads
                        act.wait_ge(z_reduced, normed(G, i, k))
                        nc.scalar.activation(zrt[0:r, slot, 0:a * h], zss[0:r, slot, 0:a * h], ACT.Sqrt,
                                             bias=epst[0:r, :], scale=1.0 / E).then_inc(z_root, 1)

                loop_tiles(act, tile)

        @block.tensor
        def _(pe):
            pe.wait_ge(const_in, 80)
            for n in range(STEPS):
                r = P if n < TILES else NS
                pe.wait_ge(x_normed, n + 1)
                if n >= 2:
                    pe.wait_ge(x_stored, n - 1)
                for c in range(KC):
                    last = nc.tensor.transpose(pt[n % 2][:, c * P:c * P + r], xin[0:r, n % 2, c * P:(c + 1) * P], ident[0:r, 0:r])
                last.then_inc(x_turned, 1)
            for G, (name, c0, wd, heads, _) in enumerate(GROUPS):
                pe.wait_ge(w_lo_done, KC + 4 * G)

                def tile(i, k, G=G, wd=wd):
                    slot = (G + k) % 2
                    r = rows(i)
                    pe.wait_ge(x_lo_done, i * 2 + (k + G * STEPS + 1))
                    pe.wait_ge(z_copied, i * 2 + (k + G * STEPS + 1))
                    for j, (xs, ws) in enumerate(((x_hi, w_hi), (x_hi, w_lo), (x_lo, w_hi))):
                        for c in range(KC):
                            last = nc.tensor.matmul(pz[slot][0:r, 0:wd], xs[:, slot, c, 0:r], ws[:, G % 2, c, 0:wd],
                                                    start=(j == 0 and c == 0), stop=(j == 2 and c == KC - 1))
                    last.then_inc(z_summed, 1)

                loop_tiles(pe, tile)

        @block.vector
        def _(dve):
            chain = Chain(dve, vchain)
            dve.wait_ge(const_in, 80)
            for g in (0, 4):
                chain.step(nc.vector.tensor_scalar(gains[:, g, :], gains[:, g, :], -(E ** -0.5), None, ALU.mult))
            def norm(n):
                r, s = (P if n < TILES else NS), slice(n % 2, n % 2 + 1)
                dve.wait_ge(x_root, n + 1)
                chain.step(nc.vector.reciprocal(xrr[0:r, s], xrt[0:r, s]))
                nc.vector.tensor_scalar(xin[0:r, n % 2, :], xin[0:r, n % 2, :], xrr[0:r, s], None, ALU.mult).then_inc(x_normed, 1)

            norm(0)
            for n in range(STEPS):
                r = P if n < TILES else NS
                if n + 1 < STEPS:
                    norm(n + 1)
                for c in FIRST_SPLITS.get(n, ()):
                    dve.wait_ge(w_hi_done, c + 1)
                    nc.vector.tensor_tensor(w_lo[:, 0, c, :], raw[:, c, :], w_hi[:, 0, c, :].bitcast(F32), ALU.subtract).then_inc(w_lo_done, 1)
                dve.wait_ge(x_turned, n + 1)
                nc.vector.tensor_tensor(xnT[:, :, n * P:n * P + r], pt[n % 2][:, :].rearrange("p (c q) -> p c q", c=KC)[:, :, 0:r],
                                        g_in[:, :].unsqueeze(2).to_broadcast([P, KC, r]), ALU.mult).then_inc(x_stored, 1)

            def split_x(slot, i, k, n):
                r = rows(i)
                dve.wait_ge(x_hi_done, n)
                nc.vector.tensor_tensor(x_lo[:, slot, :, 0:r], xnT[:, :, tokens(i, k)], x_hi[:, slot, :, 0:r].bitcast(F32),
                                        ALU.subtract).then_inc(x_lo_done, 1)

            dve.wait_ge(x_stored, STEPS)
            split_x(0, 0, 0, 1)
            split_x(1, 0, 1, 2)
            for G, (name, c0, wd, heads, grow) in enumerate(GROUPS):
                def tile(i, k, G=G, heads=heads, wd=wd, grow=grow):
                    slot = (G + k) % 2
                    r = rows(i)
                    if r == NS:
                        i2, k2, more = 0, 1, G + 1 < NG
                    elif isinstance(i, int) and k == 1:
                        i2, k2, more = 0, 0, G + 1 < NG
                    else:
                        i2, k2, more = i + 1, k, True
                    if more:
                        split_x(slot, i2, k2, i * 2 + (k + G * STEPS + 3))
                    if heads is not None:
                        a, h = heads
                        zs3 = zss[0:r, slot, 0:a * h]
                        dve.wait_ge(z_squared, normed(G, i, k))
                        nc.vector.reduce_sum(zs3, zsq[0:r, slot, 0:a * h * E].rearrange("p (h e) -> p h e", e=E), AX).then_inc(z_reduced, 1)
                    if G + 1 < NG and k == 1:
                        w = GROUPS[G + 1][2]
                        cs = bass.ds(i * 2, 2)
                        dve.wait_ge(w_hi_done, i + (KC + 4 * G + 1))
                        nc.vector.tensor_tensor(w_lo[:, (G + 1) % 2, cs, 0:w], raw[:, cs, 0:w], w_hi[:, (G + 1) % 2, cs, 0:w].bitcast(F32),
                                                ALU.subtract).then_inc(w_lo_done, 1)
                    if heads is not None:
                        zv = z[0:r, slot, 0:a * 256].rearrange("p (a h e) -> p a h e", h=4, e=E)[:, :, 0:h, :]
                        dve.wait_ge(z_root, normed(G, i, k))
                        chain.step(nc.vector.reciprocal(zrr[0:r, slot, 0:a * h], zrt[0:r, slot, 0:a * h]))
                        rr = zrr[0:r, slot, 0:a * h].rearrange("p (a h) -> p a h", a=a).unsqueeze(3)
                        chain.step(nc.vector.tensor_tensor(zv, zv, rr.to_broadcast([r, a, h, E]), ALU.mult))
                        gv = gains[0:r, grow[0]:grow[1], :].unsqueeze(2)
                        if grow[1] - grow[0] == 1 and a == 2:
                            for b in range(2):
                                ins = nc.vector.tensor_tensor(zv[:, b], zv[:, b], gv[:, 0].to_broadcast([r, h, E]), ALU.mult)
                                if b == 1:
                                    chain.step(ins)
                        else:
                            chain.step(nc.vector.tensor_tensor(zv, zv, gv.to_broadcast([r, a, h, E]), ALU.mult))
                        tile_at = (2 * i + k) if isinstance(i, int) else None
                        ct = rope[0:r, tile_at if tile_at is not None else bass.ds(i * 2 + k, 1), :]
                        if tile_at is None:
                            ct = ct.rearrange("p a c -> p (a c)")
                        bc = lambda x, w: x.unsqueeze(1).to_broadcast([r, h, w])
                        n_ops = []
                        for b in range(a):
                            v = zv[:, b]
                            va = ra[0:r, b * 4 * ROT:b * 4 * ROT + h * ROT].rearrange("p (h c) -> p h c", c=ROT)
                            vb = rb[0:r, b * 4 * ROT:b * 4 * ROT + h * ROT].rearrange("p (h c) -> p h c", c=ROT)
                            nc.vector.tensor_tensor(va, v[:, :, 0:ROT], bc(ct[:, 0:ROT], ROT), ALU.mult)
                            nc.vector.tensor_tensor(vb[:, :, 0:8], v[:, :, 8:16], bc(ct[:, 16:24], 8), ALU.mult)
                            ins = nc.vector.tensor_tensor(vb[:, :, 8:16], v[:, :, 0:8], bc(ct[:, 24:32], 8), ALU.mult)
                            if b == a - 1:
                                chain.step(ins)
                            n_ops.append((v, va, vb))
                        for b, (v, va, vb) in enumerate(n_ops):
                            ins = nc.vector.tensor_tensor(v[:, :, 0:ROT], va, vb, ALU.add)
                            if b == a - 1:
                                ins.then_inc(z_done, 1)

                loop_tiles(dve, tile, chain, per=8 if heads is not None else 0)

def dil_bias(delta):
    mult = sum(((delta >= 0) & (delta <= w) & (delta % d == 0)).astype(np.float64) for w, d in ((128, 1), (512, 4), (2048, 16)))
    return np.where(mult > 0, -np.log(np.maximum(mult, 1.0)), BIG).astype(np.float32)


def tables():
    p = np.arange(P)[:, None]
    c = np.arange(SEQ)[None, :]
    d = p + (SEQ - P) - c
    m_dil = dil_bias(d)
    m_slc = np.where(d >= 0, 0.0, BIG)
    dw = p + WIN - np.arange(WIN + P)[None, :]
    m_win = np.where((dw >= 0) & (dw < WIN), 0.0, BIG)
    t = (np.arange(TILES)[None, :, None] * P + np.arange(P)[:, None, None])
    n = np.arange(NCMP + 1)[None, None, :]
    m_cmp = np.where((n < NCMP) & (n * CMP_STRIDE + CMP_LEN - 1 <= t), 0.0, BIG).reshape(P, -1)
    masks = np.concatenate([m_dil, m_slc, m_win, m_cmp], 1).astype(np.float32)
    tt = np.tile(np.arange(DT), 8)[:, None]
    col = np.arange(PAST)[None, :]
    key = (col % P) * (PAST // P) + col // P
    s_dil = dil_bias(PAST + tt - np.concatenate([key, PAST + np.arange(DT)[None, :]], 1))
    wc = np.arange(WIN)[None, :]
    widx = np.concatenate([(wc % P) * (WIN // P) + wc // P, WIN + np.arange(DT)[None, :]], 1)
    dw = PAST + tt - (PAST - WIN + widx)
    s_win = np.where((dw >= 0) & (dw < WIN), 0.0, BIG)
    s_new = np.where(np.arange(DT)[None, :] <= tt, 0.0, BIG)
    s_zero = np.zeros((NS, NCMP + 1))
    blocks = np.tile(np.arange(PAST // SLC_BLK)[None, :], (NS, 1))
    ci = np.arange(NS)[:, None] * CMP_STRIDE
    sj = np.arange(PAST // SLC_BLK)[None, :] * SLC_BLK
    overlap = ((ci < sj + SLC_BLK) & (ci + CMP_LEN > sj) & (np.arange(NS)[:, None] < NCMP))
    row = np.arange(NS)
    same = (row[:, None] // (RA * DT) == row[None, :] // (RA * DT)) & (row[:, None] % DT == row[None, :] % DT)
    sample = np.concatenate([s_dil, s_win, s_new, s_zero, blocks, overlap, same], 1).astype(np.float32)
    return masks, sample


M_SLC, M_WIN, M_CMP = SEQ, 2 * SEQ, 2 * SEQ + WIN + P
M_ALL = M_CMP + TILES * (NCMP + 1)
S_WIN = PAST + DT
S_NEW = S_WIN + WIN + DT
S_ZERO = S_NEW + DT
S_BLK = S_ZERO + NCMP + 1
S_OVER = S_BLK + PAST // SLC_BLK
S_SAME = S_OVER + PAST // SLC_BLK
S_ALL = S_SAME + NS
NBLK = PAST // SLC_BLK
GELU_C = 0.7978845608028654


class Bag:
    pass


def shared_constants(nc, t, ctx):
    sb = lambda name, shape: ctx.enter_context(nc.sbuf_tensor(name, shape, F32))
    k = Bag()
    k.ident = sb("k_ident", [P, P])
    k.w1 = sb("k_w1", [P, 2, 16, P])
    k.w2 = sb("k_w2", [P, 2, E])
    k.peT = sb("k_peT", [P, 2, 16])
    k.masks = sb("k_masks", [P, M_ALL])
    k.smask = sb("k_smask", [NS, S_ALL])
    k.loads = [(k.peT[:], t["peT"]), (k.smask[:], t["smask"]), (k.masks[:], t["masks"])]
    for c, x in enumerate("kv"):
        k.loads += [(k.w1[:, c], t["w1_cmp_" + x].rearrange("(j p) f -> p j f", p=P)), (k.w2[:, c], t["w2_cmp_" + x])]
    return k


def attend(nc, t, o, scratch, const):
    with ExitStack() as ctx:
        sb = lambda name, shape, dt=F32: ctx.enter_context(nc.sbuf_tensor(name, shape, dt))
        sem = lambda name: ctx.enter_context(nc.semaphore(name))
        b = Bag()
        b.pe_bias = sb("a_pe_bias", [P, 2])
        b.q_dil_T = sb("a_q_dil_T", [P, 4, NS])
        b.q_nsa_T = sb("a_q_nsa_T", [P, RA, NS])
        b.gate_p = sb("a_gate_p", [P, TILES, 3 * HA])
        b.gate_s = sb("a_gate_s", [NS, DB, 3])
        b.q_nat = [sb(f"l_q_nat{k}", [P, TILES, E]) for k in range(2)]
        b.kv_nat = [sb(f"l_kv_nat{k}", [P if k < 3 else NS, TILES if k < 3 else 1, 2, E]) for k in range(4)]
        b.p_ring = sb("l_p", [P, 4, 512])
        b.kd_k = sb("l_kd_k", [P, 8, 512])
        b.kd_v = sb("l_kd_v", [P, 8, 512])
        b.kd_new = sb("l_kd_new", [DT, 1024])
        b.ks = sb("l_ks", [P, PAGES, 256])
        b.kw = sb("l_kw", [P, WIN // P, 256])
        b.ks_new = sb("l_ks_new", [DT, 256])
        b.kw_new = sb("l_kw_new", [DT, 256])
        b.kd_T = sb("l_kd_T", [P, 4, PAST])
        b.xT = sb("l_xT", [P, 2, GA, 8, NS])
        b.hh = sb("l_hh", [P, 2 * GA, NS])
        b.hu = sb("l_hu", [P, 2 * GA, NS])
        b.pages = sb("l_pages", [1, DB * PAGES], I32)
        b.q_in = [sem(f"l_q_in{k}") for k in range(2)]
        b.kv_in = [sem(f"l_kv_in{k}") for k in range(4)]
        b.pages_in = sem("l_pages_in")
        b.kdk_in = sem("l_kdk_in")
        b.kdv_in = sem("l_kdv_in")
        b.new_in = sem("l_new_in")
        b.ks_in = sem("l_ks_in")
        b.kw_in = sem("l_kw_in")
        b.rows_in = sem("l_rows_in")
        compress_prompt(nc, t, o, scratch, const, b)
        attend_loop(nc, t, o, scratch, const, b)


def loader(sp, t, o, scratch, b):
    rows_nat = b.kd_k[0:NS].rearrange("p j n -> p (j n)")
    dil_rows = o["dil_prompt"].rearrange("b s c h e -> (b s) (c h e)").rearrange("(a p) n -> p a n", p=P)
    slc_rows = o["slc_prompt"].rearrange("b s c g e -> (b s) (c g e)").rearrange("(a p) n -> p a n", p=P)
    win_rows = scratch["kvw"][0:SEQ, :].rearrange("(a p) n -> p a n", p=P)
    q_rows = [scratch[x][0:SEQ, :].rearrange("(a p) n -> p a n", p=P) for x in ("qb", "qa")]

    def load_dil(i):
        sp.dma_start(b.q_nat[0][:], q_rows[0][:, :, bass.ds(i * E, E)]).then_inc(b.q_in[0], 16)
        sp.dma_start(b.kv_nat[0][:, :, 0, :], dil_rows[:, :, bass.ds(i * E, E)]).then_inc(b.kv_in[0], 16)
        sp.dma_start(b.kv_nat[0][:, :, 1, :], dil_rows[:, :, bass.ds(i * E + 512, E)]).then_inc(b.kv_in[0], 16)

    def load_q_nsa(i):
        sp.dma_start(b.q_nat[1][:], q_rows[1][:, :, bass.ds(i * E, E)]).then_inc(b.q_in[1], 16)

    def load_kv_nsa(i, k):
        g = (i // RA) * E
        for c in range(2):
            if k == 3:
                dst, src = b.kv_nat[3][:, 0, c, :], scratch["kvc"][:, c, :, :].rearrange("n g e -> n (g e)")[:, bass.ds(g, E)]
            else:
                dst, src = b.kv_nat[k][:, :, c, :], (slc_rows if k == 1 else win_rows)[:, :, bass.ds(g + c * P, E)]
            sp.dma_start(dst, src).then_inc(b.kv_in[k], 16)

    def load_kd(i, c):
        src = t["state_dil"][bass.ds(i, 1), :, c, :, :].rearrange("b (p j) h e -> (b p) j (h e)", j=8)
        sp.dma_start((b.kd_k, b.kd_v)[c][:], src).then_inc((b.kdk_in, b.kdv_in)[c], 16)

    def load_new(i):
        sp.dma_start(b.kd_new[:], o["dil_sample"][bass.ds(i, 1), PAST:PAST + DT].rearrange("b s c h e -> (b s) (c h e)")).then_inc(b.new_in, 16)
        sp.dma_start(b.ks_new[:], o["slc_sample"][bass.ds(i, 1)].rearrange("b s c g e -> (b s) (c g e)")).then_inc(b.new_in, 16)
        sp.dma_start(b.kw_new[:], scratch["kvw"][bass.ds(i * DT + SEQ, DT), :]).then_inc(b.new_in, 16)

    def page(i, n):
        return sp.value_load(b.pages[0:1, bass.ds(i * PAGES + n, 1)], min_val=0, max_val=t["cache_slc"].shape[0] - 1)

    def load_ks(i):
        for n in range(PAGES):
            sp.dma_start(b.ks[:, n, :], t["cache_slc"][bass.ds(page(i, n), 1)].rearrange("b p c g e -> (b p) (c g e)")).then_inc(b.ks_in, 16)

    def load_rows(i):
        for n in range(PAGES):
            sp.dma_start(rows_nat[8 * n:8 * n + 8, :],
                         t["cache_cmp"][bass.ds(page(i, n), 1)].rearrange("b (n r) c g e -> (b n) (r c g e)", r=CMP_STRIDE)).then_inc(b.rows_in, 16)

    def load_kw(i):
        sp.dma_start(b.kw[:], t["state_win"][bass.ds(i, 1)].rearrange("b (p j) c g e -> (b p) j (c g e)", j=WIN // P)).then_inc(b.kw_in, 16)

    at = Bag()
    at.load_dil = load_dil
    at.load_q_nsa = load_q_nsa
    at.load_kv_nsa = load_kv_nsa
    at.load_kd = load_kd
    at.load_new = load_new
    at.load_ks = load_ks
    at.load_rows = load_rows
    at.load_kw = load_kw
    return at

def compress_prompt(nc, t, o, scratch, const, b):
    ident, w1, w2, peT = const.ident, const.w1, const.w2, const.peT
    pe_bias, q_dil_T, q_nsa_T, gate_p, gate_s, xT = b.pe_bias, b.q_dil_T, b.q_nsa_T, b.gate_p, b.gate_s, b.xT
    rows16 = b.kd_T[0:NS].rearrange("p a n -> p (a n)")
    qn = b.p_ring[0:NS, 0:2, :]
    h, u = (x[:].rearrange("p (c g) n -> p c (g n)", c=2) for x in (b.hh, b.hu))
    with ExitStack() as ctx:
        sb = lambda name, shape, dt=F32: ctx.enter_context(nc.sbuf_tensor(name, shape, dt))
        sem = lambda name: ctx.enter_context(nc.semaphore(name))
        kv = sb("c_kv", [NS, 2, GA, E])
        turned = [ctx.enter_context(nc.psum_tensor(f"c_turned{k}", [P, 512], F32)) for k in range(6)]
        hidden = ctx.enter_context(nc.psum_tensor("c_hidden", [P, 2, GA, NS], F32))
        small = ctx.enter_context(nc.psum_tensor("c_small", [P, 512], F32))
        loaded, rows_in, t_filled, v = sem("c_loaded"), sem("c_rows_in"), sem("c_t_filled"), sem("c_v")
        pe_done, hid_done, tanh_in, tanh_done, kv_done, kv_copied, kv_out, gates_in = (
            sem("c_" + x) for x in ("pe_done", "hid_done", "tanh_in", "tanh_done", "kv_done", "kv_copied", "kv_out", "gates_in"))
        gates_up = sem("c_gates_up")
        block = ctx.enter_context(nc.Block())

        @block.sync
        def _(sp):
            for c in range(4):
                sp.dma_start(rows16[:, c * 1024:(c + 1) * 1024].rearrange("n (r e) -> n r e", e=E),
                             o["cmp_prompt"].rearrange("b (n r) c g e -> (b n) r (c g) e", r=CMP_STRIDE)[:, :, c, :]).then_inc(rows_in, 16)
            sp.dma_start(qn[:, 0, :], scratch["qb"][SEQ:TOK, :]).then_inc(loaded, 16)
            for g in range(GA):
                sp.dma_start(qn[:, 1, :].rearrange("p (r g e) -> p r g e", g=GA, e=E)[:, :, g, :],
                             scratch["qa"][SEQ:TOK, g * RA * E:(g + 1) * RA * E].rearrange("p (r e) -> p r e", e=E)).then_inc(loaded, 16)
            sp.dma_start(gate_p[:], scratch["gl"][0:SEQ, :].rearrange("(a p) c -> p a c", p=P)).then_inc(gates_in, 16)
            for n in range(DB):
                sp.dma_start(gate_s[:, n, :], scratch["gl"][SEQ + n * DT:SEQ + (n + 1) * DT, :].rearrange("s (h c) -> h s c", c=3)).then_inc(gates_in, 16)
            sp.dma_start(b.pages[:], t["page_table"].rearrange("(o b) n -> o (b n)", o=1)).then_inc(b.pages_in, 16)
            at = loader(sp, t, o, scratch, b)
            at.load_dil(0)
            at.load_kd(0, 0)
            at.load_new(0)
            at.load_q_nsa(0)
            at.load_kv_nsa(0, 1)
            at.load_kd(0, 1)
            at.load_kw(0)
            at.load_kv_nsa(0, 2)
            sp.wait_ge(b.pages_in, 16)
            at.load_ks(0)

        LOADS = 16 * 3

        @block.tensor
        def _(pe):
            for c in range(2):
                for j in range(16):
                    last = nc.tensor.matmul(small[:, c:c + 1], w1[:, c, j, :], peT[:, c, j:j + 1], start=(j == 0), stop=(j == 15))
            last.then_inc(pe_done, 1)
            pe.wait_ge(loaded, LOADS)
            for n in range(2):
                for j in range(4):
                    src = qn[:, n, j * P:(j + 1) * P]
                    last = nc.tensor.transpose(turned[4 + n][:, j * NS:(j + 1) * NS], src, ident[0:NS, 0:NS])
                last.then_inc(t_filled, 1)
            pe.wait_ge(rows_in, 64)
            for n in range(4):
                c, g = n // 2, n % 2
                for rp in range(8):
                    src = rows16[:, n * 1024 + rp * P:n * 1024 + (rp + 1) * P]
                    last = nc.tensor.transpose(turned[n][:, rp * NS:(rp + 1) * NS], src, ident[0:NS, 0:NS])
                last.then_inc(t_filled, 1)
            pe.wait_ge(v, 6)
            for c in range(2):
                for j in range(16):
                    at = j // 8
                    last = nc.tensor.matmul(hidden[:, c, :, 0:NCMP], w1[:, c, j, :], xT[:, c, :, j % 8, at:at + NCMP],
                                            start=(j == 0), stop=(j == 15))
            last.then_inc(hid_done, 1)
            pe.wait_ge(v, 15)
            for c in range(2):
                for g in range(GA):
                    hg = u[:, c, :].rearrange("p (g n) -> p g n", g=GA)[:, g, 0:NCMP]
                    last = nc.tensor.matmul(small[0:NCMP, 128 + (c * GA + g) * E:128 + (c * GA + g + 1) * E], hg, w2[:, c, :], start=True, stop=True)
            last.then_inc(kv_done, 1)

        @block.scalar
        def _(act):
            act.wait_ge(gates_in, 16 * (1 + DB))
            nc.scalar.activation(gate_p[:], gate_p[:], ACT.Exp, scale=-1.0).then_inc(gates_up, 1)
            nc.scalar.activation(gate_s[:], gate_s[:], ACT.Exp, scale=-1.0).then_inc(gates_up, 1)
            act.wait_ge(tanh_in, 1)
            uv = b.hu[:, :, 0:NCMP]
            nc.scalar.activation(uv, uv, ACT.Tanh, scale=GELU_C).then_inc(tanh_done, 1)
            act.wait_ge(kv_copied, 2)
            act.dma_start(scratch["kvc"], kv[:]).then_inc(kv_out, 16)
            act.wait_ge(kv_out, 16)

        @block.vector
        def _(dve):
            ch = Chain(dve, v)
            nc.vector.memset(kv[:], 0.0).then_inc(kv_copied, 1)
            dve.wait_ge(t_filled, 2)
            ch.step(nc.vector.tensor_copy(q_dil_T[:].rearrange("p a n -> p (a n)"), turned[4][:, 0:4 * NS]))
            ch.step(nc.vector.tensor_copy(q_nsa_T[:].rearrange("p a n -> p (a n)"), turned[5][:, 0:4 * NS]))
            for n in range(4):
                dve.wait_ge(t_filled, 3 + n)
                ch.step(nc.vector.tensor_copy(xT[:, n // 2, n % 2].rearrange("p a n -> p (a n)"), turned[n][:, :]))
            dve.wait_ge(pe_done, 1)
            ch.step(nc.vector.tensor_copy(pe_bias[:], small[:, 0:2]))
            dve.wait_ge(gates_up, 2)
            for x in (gate_p, gate_s):
                ch.step(nc.vector.tensor_scalar(x[:], x[:], 1.0, None, ALU.add))
                nc.vector.reciprocal(x[:], x[:])
            ch.step(nc.vector.tensor_scalar(w2[:], w2[:], 0.5, None, ALU.mult))
            dve.wait_ge(hid_done, 1)
            hv = [x[:].rearrange("p c (g n) -> p c g n", g=GA)[:, :, :, 0:NCMP] for x in (h, u)]
            for c in range(2):
                ins = nc.vector.tensor_scalar(hv[0][:, c], hidden[:, c, :, 0:NCMP], pe_bias[:, c:c + 1], None, ALU.add)
            ch.step(ins)
            hv = [x.rearrange("p c g n -> p (c g) n") for x in hv]
            ch.step(nc.vector.tensor_tensor(hv[1], hv[0], hv[0], ALU.mult))
            ch.step(nc.vector.tensor_scalar(hv[1], hv[1], 0.044715, 1.0, ALU.mult, ALU.add))
            nc.vector.tensor_tensor(hv[1], hv[1], hv[0], ALU.mult).then_inc(tanh_in, 1)
            dve.wait_ge(tanh_done, 1)
            ch.step(nc.vector.tensor_scalar(hv[1], hv[1], 1.0, None, ALU.add))
            ch.step(nc.vector.tensor_tensor(hv[1], hv[1], hv[0], ALU.mult))
            dve.wait_ge(kv_done, 1)
            dve.wait_ge(kv_copied, 1)
            nc.vector.tensor_copy(kv[0:NCMP].rearrange("p c g e -> p (c g e)"), small[0:NCMP, 128:384]).then_inc(kv_copied, 1)


UNITS = ([("d", j) for j in range(8)] + [("sd", 0)] + [("l", j) for j in range(8)]
         + [("w", 0), ("w", 1), ("w", 2), ("w", 3), ("sc", 0)] + [("w", j) for j in range(4, 8)]
         + [("c", 0), ("c", 1), ("c", 2), ("sl", 0), ("c", 3), ("sw", 0)] + [("c", j) for j in range(4, 8)])
NU = len(UNITS)
BRANCH = {"d": 0, "l": 1, "w": 2, "c": 3}
NEXT = 4
EXTRAS = {s: [] for s in range(NU + 4)}
for _j in range(8):
    EXTRAS[_j].append(("kd", _j, [0]))
EXTRAS[3].append(("new", 0, [0]))
for _j in range(3):
    EXTRAS[9 + _j].append(("ksw", _j, [0]))
for _j in range(4):
    EXTRAS[12 + _j].append(("xt", _j, [0]))
for _s, _j in ((14, 0), (15, 1), (17, 2), (18, 3)):
    EXTRAS[_s].append(("hid", _j, []))
EXTRAS[19].append(("tanh", 0, []))
EXTRAS[20].append(("ckv", 0, []))
EXTRAS[24].append(("sel1", 0, []))
EXTRAS[26].append(("sel2", 0, []))
for _b, _s, _n in ((1, 5, 3), (2, 15, 2), (3, 23, 1), (NEXT, 28, 3)):
    for _k in range(_n):
        EXTRAS[_s + _k].append(("prep", _b, [2 * _k, 2 * _k + 1]))
SPLIT_AT = {3: 1, 13: 2, 21: 3, 26: NEXT}
PREP_CHUNKS = 6
X_USERS = ["sd", "hid", "ckv", "sel1", "sel2", "sl"]
FIRST, MID, LAST = range(3)


def key_blocks(kind, j):
    if kind in "dl":
        return 0, j + 1
    if kind == "w":
        return max(0, j - WIN // P), j + 1
    return 0, 1


def unit_chunks(n):
    kind, j = UNITS[n]
    if kind[0] == "s":
        return 2
    a, b = key_blocks(kind, j)
    return -(-(b - a) // 4)


def there(phase, n):
    return n < NU and (n >= 0 or phase != FIRST)


def stages(phase):
    return range(NU + 4 if phase == LAST else NU)


def extras(phase, s):
    return [e for e in EXTRAS[s] if s < NU and not (phase == LAST and e[:2] == ("prep", NEXT))]


def plan(phase):
    T, U = {}, {}
    for s in stages(phase):
        n = s - 2
        if there(phase, n):
            for q in range(unit_chunks(n)):
                T["tr", n, q] = len(T)
                U[n, q] = len(U)
        for name, j, qs in extras(phase, s):
            for q in qs:
                T[name, j, q] = len(T)
    return T, U


def attend_loop(nc, t, o, scratch, const, b):
    ident, w1, w2, masks, smask = const.ident, const.w1, const.w2, const.masks, const.smask
    pe_bias, q_dil_T, q_nsa_T, gate_p, gate_s = b.pe_bias, b.q_dil_T, b.q_nsa_T, b.gate_p, b.gate_s
    q_nat, kv_nat, p_ring, kd_k, kd_v, kd_new, ks, kw = b.q_nat, b.kv_nat, b.p_ring, b.kd_k, b.kd_v, b.kd_new, b.ks, b.kw
    ks_new, kw_new, kd_T, xT, hh, hu = b.ks_new, b.kw_new, b.kd_T, b.xT, b.hh, b.hu
    q_in, kv_in, kdk_in, kdv_in, new_in, ks_in, kw_in, rows_in = b.q_in, b.kv_in, b.kdk_in, b.kdv_in, b.new_in, b.ks_in, b.kw_in, b.rows_in
    tables_ = [plan(phase) for phase in range(3)]
    T, U = [x[0] for x in tables_], [x[1] for x in tables_]
    NT, NCH = len(T[MID]), len(U[MID])
    assert NT % 2 == 0 and NCH % 4 == 0 and NU % 4 == 0
    T_SHIFT = [PREP_CHUNKS, PREP_CHUNKS + len(T[FIRST]) - NT, PREP_CHUNKS + len(T[FIRST]) - NT]
    U_SHIFT = [0, len(U[FIRST]) - NCH, len(U[FIRST]) - NCH]
    with ExitStack() as ctx:
        sb = lambda name, shape, dt=F32: ctx.enter_context(nc.sbuf_tensor(name, shape, dt))
        sem = lambda name: ctx.enter_context(nc.semaphore(name))
        ident_r = sb("l_ident_r", [P, P], F32R)
        ident_made = sem("l_ident_made")
        q_split = sb("l_q_split", [P, TILES, 2 * E], F32R)
        k_split = sb("l_k_split", [P, TILES, 3 * E], F32R)
        qT = [sb(f"l_qT{k}", [P, SEQ], F32R) for k in range(2)]
        kA = [sb(f"l_kA{k}", [P, SEQ], F32R) for k in range(2)]
        kB = [sb(f"l_kB{k}", [P, SEQ], F32R) for k in range(2)]
        e_ring = sb("l_e", [P, 4, PAST + DT])
        e_gated = sb("l_e_gated", [NS, NS])
        nmin = sb("l_nmin", [P, 4])
        nmin2 = sb("l_nmin2", [NS, 1])
        total = sb("l_total", [P, 4])
        rtot = sb("l_rtot", [P, 4])
        acc = [sb(f"l_acc{k}", [P, TILES, E]) for k in range(2)]
        gate_h = sb("l_gate_h", [P, TILES, 3])
        gate_b = sb("l_gate_b", [NS, 3])
        rows_nat = kd_k[0:NS].rearrange("p j n -> p (j n)")
        rows16 = kd_T[0:NS].rearrange("p a n -> p (a n)")
        ks_T = sb("l_ks_T", [P, PAST])
        kw_T = sb("l_kw_T", [P, WIN])
        new_T = sb("l_new_T", [P, 6, DT])
        kc_T = sb("l_kc_T", [P, NCMP])
        vc = sb("l_vc", [NCMP, P])
        bd_dil = sb("l_bd_dil", [P, 4 * 80])
        bd_nsa = sb("l_bd_nsa", [P, NS])
        sel = sb("l_sel", [NS, 3, NBLK])
        selm = sb("l_selm", [NS, 2])
        oa_s = sb("l_oa_s", [P, RA * DT])
        oT_s = sb("l_oT_s", [P, 8, NS])
        s_ps = [ctx.enter_context(nc.psum_tensor(f"l_s{k}", [P, 1024], F32)) for k in range(2)]
        t_ps = [ctx.enter_context(nc.psum_tensor(f"l_t{k}", [P, 512], F32)) for k in range(2)]
        o_ps = ctx.enter_context(nc.psum_tensor("l_o", [P, 512], F32))
        x_ps = ctx.enter_context(nc.psum_tensor("l_x", [P, 512], F32))

        passed = sem("l_passed")
        win_out = sem("l_win_out")
        kdk_out, kdv_out, kw_out, oT_out = (sem("l_" + x) for x in ("kdk_out", "kdv_out", "kw_out", "oT_out"))
        acc_out = [sem(f"l_acc_out{k}") for k in range(2)]
        x_filled, x_free, rows_ready = sem("l_x_filled"), sem("l_x_free"), sem("l_rows_ready")
        s_filled, s_free = sem("l_s_filled"), sem("l_s_free")
        t_filled = sem("l_t_filled")
        t_evac = [sem(f"l_t_evac{k}") for k in range(2)]
        rt_ready = sem("l_rt_ready")
        o_filled, o_free = sem("l_o_filled"), sem("l_o_free")
        masked, exped, scaled = sem("l_masked"), sem("l_exped"), sem("l_scaled")
        hi_done, lo_done = sem("l_hi_done"), sem("l_lo_done")
        dve_c, pool_c = sem("l_dve_c"), sem("l_pool_c")
        bd_zero, bd_ready = sem("l_bd_zero"), sem("l_bd_ready")
        tanh_in, tanh_done, hid_ready, ckv_ready, sel_ready = (sem("l_" + x) for x in ("tanh_in", "tanh_done", "hid_ready", "ckv_ready", "sel_ready"))

        CREDIT_O = 8
        NX = len(X_USERS)
        at_u = lambda i, n: i * NU + (n + 1)
        at_o = lambda i, n: i * NU + (n + 1 + CREDIT_O)
        prompt = [n for n in range(NU) if UNITS[n][0][0] != "s"]
        at_r = lambda i, n: i * len(prompt) + (prompt.index(n % NU) + 1 + len(prompt) * (n // NU))
        at_x = lambda i, name: i * NX + (X_USERS.index(name) + 1)
        at_t = lambda i, c: i * NT + (c + 1)
        at_evac = lambda i, c: i * (NT // 2) + (c // 2 + 2)

        def chunks_of(phase, name, j=None):
            if name == "prep" and j == 0:
                if phase == FIRST:
                    return list(range(PREP_CHUNKS))
                return [c - NT for c in chunks_of(MID, "prep", NEXT)]
            return [c + T_SHIFT[phase] for (a, b, _), c in T[phase].items() if a == name and (j is None or b == j)]

        def wait_turned(eng, i, phase, name, j=None):
            for par in range(2):
                mine = [c for c in chunks_of(phase, name, j) if c % 2 == par]
                if mine:
                    eng.wait_ge(t_evac[par], at_evac(i, max(mine)))

        def loop(eng, body, chain=None):
            body(0, FIRST)
            with eng.Fori(1, DB - 1) as i:
                if chain:
                    chain.enter(i, CHAIN_PER_PASS, 1)
                body(i, MID)
            if chain:
                chain.leave(DB - 1)
            body(DB - 1, LAST)

        block = ctx.enter_context(nc.Block())

        o_rows = scratch["o"].rearrange("(a p) n -> p a n", p=P)
        unit = {u: n for n, u in enumerate(UNITS)}
        ROWS_AT = unit["sd", 0] + 1

        @block.sync
        def _(sp):
            sp.dma_start(o["win_prompt"].rearrange("b s c g e -> (b s) (c g e)"), scratch["kvw"][SEQ - WIN:SEQ, :]).then_inc(win_out, 16)

            sp.sem_inc(acc_out[0], 1)
            sp.sem_inc(acc_out[1], 1)

            at = loader(sp, t, o, scratch, b)
            at.load_kv_nsa(0, 3)

            def wait(sem_, value):
                sp.wait_ge(sem_, value)
                sp.sem_inc(passed, 1)

            def store_nsa(i):
                sp.dma_start(o_rows[:, :, bass.ds((i % RA) * (GA * E) + (i // RA) * E, E)], acc[1][:]).then_inc(acc_out[1], 16)

            def body(i, phase):
                more = phase != LAST
                wait(kdk_in, i * 16 + 16)
                sp.dma_start(o["dil_sample"][bass.ds(i, 1), 0:PAST, 0, :, :].rearrange("b (p j) h e -> (b p) j (h e)", j=8), kd_k[:]).then_inc(kdk_out, 16)
                wait(kdv_in, i * 16 + 16)
                sp.dma_start(o["dil_sample"][bass.ds(i, 1), 0:PAST, 1, :, :].rearrange("b (p j) h e -> (b p) j (h e)", j=8), kd_v[:]).then_inc(kdv_out, 16)
                wait(kw_in, i * 16 + 16)
                sp.dma_start(o["win_sample"][bass.ds(i, 1), 0:WIN - DT].rearrange("b (p j) c g e -> (b p) j (c g e)", j=WIN // P), kw[2:P]).then_inc(kw_out, 16)
                wait(new_in, i * 48 + 48)
                sp.dma_start(o["win_sample"][bass.ds(i, 1), WIN - DT:WIN].rearrange("b s c g e -> (b s) (c g e)"), kw_new[:]).then_inc(kw_out, 16)
                if phase != FIRST:
                    wait(o_free, at_u(i, -1) + 1)
                    store_nsa(i - 1)
                    at.load_kv_nsa(i, 3)
                wait(t_filled, at_t(i, chunks_of(phase, "kd", 7)[-1]))
                wait(kdk_out, i * 16 + 16)
                at.load_rows(i)
                wait(o_filled, at_o(i, unit["d", 7]))
                if more:
                    at.load_dil(i + 1)
                wait(o_filled, at_o(i, unit["sd", 0]))
                wait(kdv_out, i * 16 + 16)
                if more:
                    at.load_kd(i + 1, 1)
                wait(o_free, at_u(i, unit["d", 7]) + 1)
                sp.dma_start(o_rows[:, :, bass.ds(i * E + 512, E)], acc[0][:]).then_inc(acc_out[0], 16)
                wait(rows_ready, i * 8 + 8)
                if more:
                    at.load_kd(i + 1, 0)
                wait(o_filled, at_o(i, unit["l", 7]))
                if more:
                    at.load_q_nsa(i + 1)
                    at.load_kv_nsa(i + 1, 1)
                wait(o_filled, at_o(i, unit["w", 7]))
                if more:
                    at.load_kv_nsa(i + 1, 2)
                wait(o_filled, at_o(i, unit["sl", 0]))
                if more:
                    at.load_ks(i + 1)
                wait(o_filled, at_o(i, unit["sw", 0]))
                wait(kw_out, i * 32 + 32)
                if more:
                    at.load_new(i + 1)
                    at.load_kw(i + 1)

            body(0, FIRST)
            with sp.Fori(1, DB - 1) as i:
                body(i, MID)
            body(DB - 1, LAST)
            sp.wait_ge(o_free, at_u(DB, -1) + 1)
            store_nsa(DB - 1)
            sp.dma_start(scratch["oT"], oT_s[:]).then_inc(oT_out, 16)
            for k in range(2):
                sp.wait_ge(acc_out[k], 16 * DB + 1)
            sp.wait_ge(oT_out, 16)
            sp.wait_ge(win_out, 16)
            sp.wait_ge(kw_out, 32 * DB)

        @block.gpsimd
        def _(pool):
            nc.gpsimd.memset(bd_dil[:], 0.0).then_inc(bd_zero, 1)
            nc.gpsimd.memset(bd_nsa[:], 0.0).then_inc(bd_zero, 1)
            pool.wait_ge(bd_zero, 2)

            ch = Chain(pool, pool_c)

            def split(i, b):
                pool.wait_ge(hi_done, i * 4 + (b + 1))
                pool.sem_inc(passed, 1)
                b_, (r, m) = b % NEXT, ((NS, 1) if b == 3 else (P, TILES))
                if b_ < 2:
                    nc.gpsimd.tensor_tensor(q_split[:, :, E:2 * E], q_nat[b_][:], q_split[:, :, 0:E].bitcast(F32), ALU.subtract)
                nc.gpsimd.tensor_tensor(k_split[0:r, 0:m, E:2 * E], kv_nat[b_][0:r, 0:m, 0, :], k_split[0:r, 0:m, 0:E].bitcast(F32),
                                        ALU.subtract).then_inc(lo_done, 1)
                pool.wait_ge(lo_done, i * 4 + (b + 1))
                pool.sem_inc(passed, 1)

            def body(i, more):
                pool.wait_ge(o_free, at_u(i, -1) + 1)
                for g in range(2):
                    hp = slice(g * E, (g + 1) * E)
                    ch.step(nc.gpsimd.tensor_copy(bd_dil[hp, :].rearrange("p (a c) -> p a c", c=80)[:, :, g * DT:(g + 1) * DT],
                                                  q_dil_T[hp, :, bass.ds(i * DT, DT)]))
                    ch.step(nc.gpsimd.tensor_copy(bd_nsa[hp, g * RA * DT:(g + 1) * RA * DT].rearrange("p (a c) -> p a c", c=DT),
                                                  q_nsa_T[hp, :, bass.ds(i * DT, DT)]))
                ch.step(nc.gpsimd.tensor_copy(gate_h[:], gate_p[:, :, bass.ds(i * 3, 3)]))
                nc.gpsimd.tensor_copy(gate_b[:].unsqueeze(1), gate_s[:, bass.ds(i, 1), :]).then_inc(bd_ready, 1)

                for s in range(NU):
                    if s in SPLIT_AT and (more or SPLIT_AT[s] != NEXT):
                        split(i, SPLIT_AT[s])
                    if s == unit["sd", 0] + 1:
                        pool.wait_ge(rows_in, i * 16 * PAGES + 16 * PAGES)
                        pool.sem_inc(passed, 1)
                        pool.wait_ge(s_filled, at_u(i, unit["sd", 0]))
                        pool.sem_inc(passed, 1)
                    if s == 18:
                        pool.wait_ge(x_free, at_x(i, "hid") + 1)
                        pool.sem_inc(passed, 1)
                        x, y = hh[:, :, 0:NCMP], hu[:, :, 0:NCMP]
                        ch.step(nc.gpsimd.tensor_tensor(y, x, x, ALU.mult))
                        pool.sem_inc(passed, 1)
                        ch.step(nc.gpsimd.tensor_scalar(y, y, 0.044715, 1.0, ALU.mult, ALU.add))
                        nc.gpsimd.tensor_tensor(y, y, x, ALU.mult).then_inc(tanh_in, 1)
                        pool.wait_ge(tanh_done, i + 1)
                        pool.sem_inc(passed, 1)
                        ch.step(nc.gpsimd.tensor_scalar(y, y, 1.0, None, ALU.add))
                        nc.gpsimd.tensor_tensor(y, y, x, ALU.mult).then_inc(hid_ready, 1)
                    for m in range(8 if s == ROWS_AT else 0):
                        c, r = m // 2, slice(m % 2 * 8, m % 2 * 8 + 8)
                        ins = nc.gpsimd.tensor_copy(rows16[:, c * 1024:(c + 1) * 1024].rearrange("p (r e) -> p r e", e=E)[:, r, :],
                                                    rows_nat.rearrange("p (r k e) -> p r k e", k=4, e=E)[:, r, c, :])
                        ins.then_inc(rows_ready, 1)

            split(0, 0)
            with pool.Fori(0, DB - 1) as i:
                ch.enter(i, 5 + 3)
                body(i, True)
            ch.leave(DB - 1)
            body(DB - 1, False)

        @block.tensor
        def _(pe):

            def turn_slot(i, c):
                pe.wait_ge(t_evac[c % 2], i * (NT // 2) + (c // 2 + 1))
                pe.sem_inc(passed, 1)
                return t_ps[c % 2]

            def prep(i, b, at):
                pe.wait_ge(lo_done, i * 4 + (b + 1))
                b %= NEXT
                jobs = []
                if b < 2:
                    jobs += [[(q_split[:, k, :], P) for k in range(c, c + 4)] for c in (0, 4)]
                if b < 3:
                    for x in (0, E):
                        jobs += [[(k_split[:, k, x:x + 2 * E], P) for k in range(c, c + 4)] for c in (0, 4)]
                else:
                    jobs += [[(k_split[0:NS, 0, x:x + 2 * E], NS)] for x in (0, E)]
                for q, c in at:
                    dst = turn_slot(i, c)
                    for k, (src, r) in enumerate(jobs[q]):
                        last = nc.tensor.transpose(dst[:, k * P:k * P + r].bitcast(F32R), src, ident_r[0:r, 0:r])
                    last.then_inc(t_filled, 1)

            def body(i, phase):
                at = lambda name, j, q: T[phase][name, j, q] + T_SHIFT[phase]

                def qk(n, half=None):
                    kind, j = UNITS[n]
                    out = s_ps[n % 2]
                    if half != 1:
                        pe.wait_ge(s_free, at_u(i, n))
                    if kind[0] != "s":
                        b = BRANCH[kind]
                        a0, a1 = key_blocks(kind, j)
                        w = (a1 - a0) * P if kind != "c" else NS
                        if j == 0:
                            wait_turned(pe, i, phase, "prep", b)
                        lhs = qT[b > 0][:, j * P:(j + 1) * P]
                        for c in range(0, w, 512):
                            cw = min(512, w - c)
                            ks_ = slice(a0 * P + c, a0 * P + c + cw)
                            nc.tensor.matmul(out[:, c:c + cw], lhs, kB[b % 2][:, ks_], start=True, stop=False)
                            last = nc.tensor.matmul(out[:, c:c + cw], lhs, kA[b % 2][:, ks_], start=False, stop=True)
                        last.then_inc(s_filled, 1)
                        return
                    if kind == "sd":
                        if half == 0:
                            pe.wait_ge(bd_ready, i + 1)
                            wait_turned(pe, i, phase, "kd")
                        for a in range(4):
                            last = nc.tensor.matmul(out[0:NS, half * 512:(half + 1) * 512], bd_dil[:, a * NS:(a + 1) * NS], kd_T[:, a, half * 512:(half + 1) * 512],
                                                    start=(a == 0), stop=(a == 3))
                        if half == 1:
                            last.then_inc(s_filled, 1)
                            wait_turned(pe, i, phase, "new")
                            pe.wait_ge(x_free, at_x(i, "sd"))
                            for a in range(4):
                                last = nc.tensor.matmul(x_ps[0:NS, 0:DT], bd_dil[:, a * NS:(a + 1) * NS], new_T[:, a, :], start=(a == 0), stop=(a == 3))
                            last.then_inc(x_filled, 1)
                        return
                    if kind == "sl":
                        wait_turned(pe, i, phase, "ksw")
                    if kind == "sc":
                        pe.wait_ge(ckv_ready, i + 1)
                    src, w = {"sc": (kc_T, NCMP), "sl": (ks_T, PAST), "sw": (kw_T, WIN)}[kind]
                    for c in range(0, w, 512):
                        cw = min(512, w - c)
                        last = nc.tensor.matmul(out[0:NS, c:c + cw], bd_nsa[:], src[:, c:c + cw], start=True, stop=True)
                    if kind == "sw":
                        last = nc.tensor.matmul(out[0:NS, WIN:WIN + DT], bd_nsa[:], new_T[:, 5, :], start=True, stop=True)
                    last.then_inc(s_filled, 1)
                    if kind == "sl":
                        pe.wait_ge(x_free, at_x(i, "sl"))
                        nc.tensor.matmul(x_ps[0:NS, 0:DT], bd_nsa[:], new_T[:, 4, :], start=True, stop=True).then_inc(x_filled, 1)

                def tr(n):
                    kind, j = UNITS[n]
                    if kind[0] != "s":
                        a0, a1 = key_blocks(kind, j)
                        w = (a1 - a0) * P if kind != "c" else NS
                        pe.wait_ge(exped, at_u(i, n))
                        for c in range(0, w, 512):
                            dst = turn_slot(i, at("tr", n, c // 512))
                            for k in range(c, min(w, c + 512), P):
                                kw_ = min(P, w - k)
                                last = nc.tensor.transpose(dst[0:kw_, k - c:k - c + P], e_ring[:, n % 4, k:k + kw_], ident[:])
                            last.then_inc(t_filled, 1)
                        return
                    nth = [u for u in range(NU) if UNITS[u][0][0] == "s"].index(n)
                    w = {"sd": PAST, "sc": NCMP, "sl": PAST, "sw": WIN}[kind]
                    if kind == "sc":
                        pe.wait_ge(exped, at_u(i, n))
                    else:
                        pe.wait_ge(scaled, i * 4 + (nth + 1))
                    dst = turn_slot(i, at("tr", n, 0))
                    for k in range(0, w, P):
                        kw_ = min(P, w - k)
                        last = nc.tensor.transpose(dst[0:kw_, k // P * NS:(k // P + 1) * NS], e_ring[0:NS, n % 4, k:k + kw_], ident[0:NS, 0:NS])
                    last.then_inc(t_filled, 1)
                    dst = turn_slot(i, at("tr", n, 1))
                    if kind == "sc":
                        pe.wait_ge(scaled, i * 4 + (nth + 1))
                        pe.sem_inc(passed, 1)
                        last = nc.tensor.transpose(dst[0:NCMP, 0:NS], e_gated[:, 0:NCMP], ident[0:NS, 0:NS])
                    else:
                        last = nc.tensor.transpose(dst[0:DT, 0:NS], e_ring[0:NS, n % 4, w:w + DT], ident[0:NS, 0:NS])
                    last.then_inc(t_filled, 1)

                def probs_of(n, q):
                    c, u = (at("tr", n, q), U[phase][n, q]) if (n, q) in U[phase] else (T[MID]["tr", n + NU, q] + T_SHIFT[MID] - NT, U[MID][n + NU, q])
                    pe.wait_ge(t_evac[c % 2], at_evac(i, c))
                    return p_ring[:, (u + U_SHIFT[phase]) % 4, :]

                def pv(n, half=None):
                    kind, j = UNITS[n]
                    if half != 1:
                        pe.wait_ge(o_free, at_u(i, n))
                    out = o_ps
                    if kind[0] != "s":
                        b = BRANCH[kind]
                        a0, a1 = key_blocks(kind, j)
                        if j == 0:
                            pe.wait_ge(kv_in[b], (i if n >= 0 else i - 1) * 32 + 32)
                        for k in range(a1 - a0):
                            if k % 4 == 0:
                                probs = probs_of(n, k // 4)
                            r = P if kind != "c" else NS
                            last = nc.tensor.matmul(out[:, 0:E], probs[0:r, (k % 4) * P:(k % 4 + 1) * P], kv_nat[b][0:r, a0 + k, 1, :],
                                                    start=(k == 0), stop=(k == a1 - a0 - 1))
                        last.then_inc(o_filled, 1)
                        return
                    p0, p1 = probs_of(n, 0), probs_of(n, 1)
                    if kind == "sd":
                        pe.wait_ge(kdv_in, i * 16 + 16)
                        for a in range(2 * half, 2 * half + 2):
                            for k in range(8):
                                nc.tensor.matmul(out[:, a * 16:(a + 1) * 16], kd_v[:, k, a * P:(a + 1) * P], p0[:, k * NS + a * 16:k * NS + (a + 1) * 16],
                                                 start=(k == 0), stop=False)
                            last = nc.tensor.matmul(out[:, a * 16:(a + 1) * 16], kd_new[:, 512 + a * P:512 + (a + 1) * P], p1[0:DT, a * 16:(a + 1) * 16],
                                                    start=False, stop=True)
                        if half == 1:
                            last.then_inc(o_filled, 1)
                    elif kind == "sc":
                        pe.wait_ge(x_free, at_x(i, "sel1"))
                        pe.sem_inc(passed, 1)
                        nc.tensor.matmul(x_ps[0:NS, 0:NBLK], p0[0:NCMP, 0:NS], smask[0:NCMP, S_OVER:S_OVER + NBLK],
                                         start=True, stop=True).then_inc(x_filled, 1)
                        nc.tensor.matmul(out[:, 0:NS], vc[:], p1[0:NCMP, 0:NS], start=True, stop=True).then_inc(o_filled, 1)
                    else:
                        src, new, m = (ks, ks_new, PAGES) if kind == "sl" else (kw, kw_new, WIN // P)
                        for k in range(m):
                            nc.tensor.matmul(out[:, 0:NS], src[:, k, P:2 * P], p0[:, k * NS:(k + 1) * NS], start=(k == 0), stop=False)
                        nc.tensor.matmul(out[:, 0:NS], new[:, P:2 * P], p1[0:DT, 0:NS], start=False, stop=True).then_inc(o_filled, 1)

                def extra(name, j, qs):
                    if name == "prep":
                        prep(i, j, [(q, at(name, j, q)) for q in qs])
                    elif name == "kd":
                        if j == 0:
                            pe.wait_ge(kdk_in, i * 16 + 16)
                        dst = turn_slot(i, at(name, j, 0))
                        for a in range(4):
                            last = nc.tensor.transpose(dst[:, a * P:(a + 1) * P], kd_k[:, j, a * P:(a + 1) * P], ident[:])
                        last.then_inc(t_filled, 1)
                    elif name == "new":
                        pe.wait_ge(new_in, i * 48 + 48)
                        dst = turn_slot(i, at(name, j, 0))
                        for a in range(6):
                            src = kd_new[:, a * P:(a + 1) * P] if a < 4 else (ks_new, kw_new)[a - 4][:, 0:P]
                            last = nc.tensor.transpose(dst[:, a * DT:(a + 1) * DT], src, ident[0:DT, 0:DT])
                        last.then_inc(t_filled, 1)
                    elif name == "ksw":
                        if j < 2:
                            pe.wait_ge(ks_in, i * 16 * PAGES + 16 * PAGES)
                        else:
                            pe.wait_ge(kw_in, i * 16 + 16)
                        dst = turn_slot(i, at(name, j, 0))
                        for a in range(4):
                            src = ks[:, j * 4 + a, 0:P] if j < 2 else kw[:, a, 0:P]
                            last = nc.tensor.transpose(dst[:, a * P:(a + 1) * P], src, ident[:])
                        last.then_inc(t_filled, 1)
                    elif name == "xt":
                        if j == 0:
                            pe.wait_ge(rows_ready, i * 8 + 8)
                        dst = turn_slot(i, at(name, j, 0))
                        for rp in range(8):
                            last = nc.tensor.transpose(dst[:, rp * NS:(rp + 1) * NS], rows16[:, j * 1024 + rp * P:j * 1024 + (rp + 1) * P], ident[0:NS, 0:NS])
                        last.then_inc(t_filled, 1)
                    elif name == "hid":
                        c, half = j // 2, j % 2
                        if half == 0:
                            for g in range(GA):
                                wait_turned(pe, i, phase, "xt", c * GA + g)
                                pe.sem_inc(passed, 1)
                        if j == 0:
                            pe.wait_ge(x_free, at_x(i, "hid"))
                        out = x_ps[:, c * P:(c + 1) * P].rearrange("p (g n) -> p g n", g=GA)[:, :, 0:NCMP]
                        for k in range(8 * half, 8 * half + 8):
                            last = nc.tensor.matmul(out, w1[:, c, k, :], xT[:, c, :, k % 8, k // 8:k // 8 + NCMP], start=(k == 0), stop=(k == 15))
                        if j == 3:
                            last.then_inc(x_filled, 1)
                    elif name == "ckv":
                        pe.wait_ge(hid_ready, i + 1)
                        pe.sem_inc(passed, 1)
                        pe.wait_ge(x_free, at_x(i, "ckv"))
                        for g in range(GA):
                            nc.tensor.matmul(x_ps[g * E:(g + 1) * E, 0:NCMP], w2[:, 0, :], hu[:, g, 0:NCMP], start=True, stop=True)
                            last = nc.tensor.matmul(x_ps[0:NCMP, P + g * E:P + (g + 1) * E], hu[:, 2 + g, 0:NCMP], w2[:, 1, :], start=True, stop=True)
                        last.then_inc(x_filled, 1)
                    elif name == "sel2":
                        pe.wait_ge(sel_ready, i + 1)
                        pe.sem_inc(passed, 1)
                        pe.wait_ge(x_free, at_x(i, "sel2"))
                        pe.sem_inc(passed, 1)
                        nc.tensor.matmul(x_ps[0:NS, 0:NBLK], smask[:, S_SAME:S_SAME + NS], sel[:, 0, :], start=True, stop=True).then_inc(x_filled, 1)

                for s in stages(phase):
                    sd = s == unit["sd", 0]
                    if s < NU:
                        qk(s, 0 if sd else None)
                    if there(phase, s - 2):
                        tr(s - 2)
                    if s - 4 == unit["sd", 0]:
                        pv(s - 4, 1)
                    if there(phase, s - 3):
                        pv(s - 3, 0 if s - 3 == unit["sd", 0] else None)
                    if sd:
                        qk(s, 1)
                    for name, j, qs in extras(phase, s):
                        extra(name, j, qs)

            pe.sem_inc(o_filled, CREDIT_O)
            pe.wait_ge(ident_made, 1)
            prep(0, 0, [(q, q) for q in range(PREP_CHUNKS)])
            loop(pe, body)

        def copy_dst(phase, name, j, q):
            if name == "tr":
                kind, jj = UNITS[j]
                dst = p_ring[:, (U[phase][j, q] + U_SHIFT[phase]) % 4, :]
                if kind[0] != "s":
                    a0, a1 = key_blocks(kind, jj)
                    w = min(4, a1 - a0 - 4 * q) * P
                    r = P if kind != "c" else NS
                elif q == 1:
                    w, r = NS, (NCMP if kind == "sc" else DT)
                else:
                    w, r = {"sd": 512, "sc": NS, "sl": 512, "sw": 4 * NS}[kind], (NCMP if kind == "sc" else P)
                return dst[0:r, 0:w], r, w
            if name == "prep":
                j %= NEXT
                if j < 2:
                    if q < 2:
                        return qT[j][:, q * 512:(q + 1) * 512], P, 512
                    q -= 2
                if j == 3:
                    return (kA, kB)[q][1][:, 0:NS], P, NS
                return (kA, kB)[q // 2][j % 2][:, (q % 2) * 512:(q % 2 + 1) * 512], P, 512
            if name == "kd":
                return kd_T[:, :, j * P:(j + 1) * P], P, 512
            if name == "new":
                return new_T[:].rearrange("p a n -> p (a n)"), P, 6 * DT
            if name == "ksw":
                return (ks_T[:, j * 512:(j + 1) * 512] if j < 2 else kw_T[:, :]), P, 512
            return xT[:, j // 2, j % 2].rearrange("p a n -> p (a n)"), P, 512

        def owner(phase, u):
            if u >= 0:
                return next((n for (n, _), v in U[phase].items() if v == u))
            return None if phase == FIRST else owner(MID, u + NCH) - NU

        def take_out(eng, i, phase, name, j, qs, copy):
            for q in qs:
                if TAKER(name, j, q) == (eng is nc.scalar):
                    take_chunk(eng, i, phase, T[phase][name, j, q] + T_SHIFT[phase], name, j, q, copy)

        def take_chunk(eng, i, phase, c, name, j, q, copy):
            par = c % 2
            eng.wait_ge(t_filled, at_t(i, c))
            if name == "tr":
                back = owner(phase, U[phase][j, q] - 4)
                if back is not None:
                    eng.wait_ge(o_filled, at_o(i, back))
            dst, r, w = copy_dst(phase, name, j, q)
            src = t_ps[par][0:r, 0:w]
            if name == "kd":
                src = src.rearrange("p (a n) -> p a n", a=4)
            copy(dst, src).then_inc(t_evac[par], 1)

        @block.scalar
        def _(act):
            copy = lambda dst, src: nc.scalar.activation(dst, src, ACT.Copy)

            def split(i, phase, b):
                if b > 0:
                    act.wait_ge(t_filled, at_t(i, chunks_of(phase, "prep", b - 1)[-1]))
                act.wait_ge(kv_in[b % NEXT], i * 32 + 32 * (1 + b // NEXT))
                b_, (r, m) = b % NEXT, ((NS, 1) if b == 3 else (P, TILES))
                if b_ < 2:
                    act.wait_ge(q_in[b_], i * 16 + 16 * (1 + b // NEXT))
                    copy(q_split[:, :, 0:E], q_nat[b_][:])
                copy(k_split[0:r, 0:m, 0:E], kv_nat[b_][0:r, 0:m, 0, :])
                copy(k_split[0:r, 0:m, 2 * E:3 * E], kv_nat[b_][0:r, 0:m, 0, :]).then_inc(hi_done, 1)

            def body(i, phase):
                def exp(n):
                    kind, j = UNITS[n]
                    if kind[0] != "s":
                        a0, a1 = key_blocks(kind, j)
                        r, w = P, ((a1 - a0) * P if kind != "c" else NS)
                    else:
                        r, w = NS, {"sd": PAST + DT, "sc": NCMP, "sl": PAST + DT, "sw": WIN + DT}[kind]
                    act.wait_ge(masked, at_u(i, n))
                    k = n % 4
                    nc.scalar.activation(e_ring[0:r, k, 0:w], e_ring[0:r, k, 0:w], ACT.Exp, bias=nmin[0:r, k:k + 1], scale=-1.0,
                                         accum_out=total[0:r, k:k + 1]).then_inc(exped, 1)

                for s in stages(phase):
                    if there(phase, s - 1):
                        exp(s - 1)
                    if there(phase, s - 2):
                        take_out(act, i, phase, "tr", s - 2, range(unit_chunks(s - 2)), copy)
                    for name, j, qs in extras(phase, s):
                        take_out(act, i, phase, name, j, qs, copy)
                        if name == "tanh":
                            act.wait_ge(tanh_in, i + 1)
                            nc.scalar.activation(hu[:, :, 0:NCMP], hu[:, :, 0:NCMP], ACT.Tanh, scale=GELU_C).then_inc(tanh_done, 1)
                    if s in SPLIT_AT and not (phase == LAST and SPLIT_AT[s] == NEXT):
                        split(i, phase, SPLIT_AT[s])

            nc.scalar.activation(ident_r[:], ident[:], ACT.Copy).then_inc(ident_made, 1)
            split(0, FIRST, 0)
            loop(act, body)

        @block.vector
        def _(dve):
            dve.sem_inc(t_evac[0], 1)
            dve.sem_inc(t_evac[1], 1)
            dve.sem_inc(s_free, 2)
            dve.sem_inc(o_free, 1)
            dve.sem_inc(x_free, 1)
            ch = Chain(dve, dve_c)
            copy = lambda dst, src: nc.vector.tensor_copy(dst, src)

            def body(i, phase):
                def mask(dst, src, m, acc_, last):
                    return nc.vector.tensor_tensor_reduce(out=dst, in0=src, in1=m, scale=1.0, scalar=CLAMP, op0=ALU.add, op1=ALU.min, accum_out=acc_)

                def low(n):
                    kind, j = UNITS[n]
                    k = n % 4
                    dve.wait_ge(s_filled, at_u(i, n))
                    dve.sem_inc(passed, 1)
                    sp_ = s_ps[n % 2]
                    if kind[0] != "s":
                        a0, a1 = key_blocks(kind, j)
                        w = (a1 - a0) * P if kind != "c" else NS
                        end = {"d": SEQ, "l": 2 * SEQ, "w": M_CMP, "c": M_CMP + (j + 1) * NS}[kind]
                        ins = mask(e_ring[:, k, 0:w], sp_[:, 0:w], masks[:, end - w:end], nmin[:, k:k + 1], True)
                        ins.then_inc(s_free, 1)
                        dve.wait_ge(s_free, at_u(i, n) + 2)
                        dve.sem_inc(masked, 1)
                        return
                    if kind in ("sc", "sw"):
                        w, m0 = (NCMP, S_ZERO) if kind == "sc" else (WIN + DT, S_WIN)
                        ins = mask(e_ring[0:NS, k, 0:w], sp_[0:NS, 0:w], smask[:, m0:m0 + w], nmin[0:NS, k:k + 1], True)
                        ins.then_inc(s_free, 1)
                        dve.wait_ge(s_free, at_u(i, n) + 2)
                        dve.sem_inc(masked, 1)
                        return
                    if kind == "sd":
                        ins = mask(e_ring[0:NS, k, 0:PAST], sp_[0:NS, 0:PAST], smask[:, 0:PAST], nmin[0:NS, k:k + 1], False)
                        m1 = smask[:, PAST:PAST + DT]
                    else:
                        ins = mask(e_ring[0:NS, k, 0:PAST].rearrange("p (b c) -> p b c", c=SLC_BLK), sp_[0:NS, 0:PAST].rearrange("p (b c) -> p b c", c=SLC_BLK),
                                   sel[:, 2, :].unsqueeze(2).to_broadcast([NS, NBLK, SLC_BLK]), nmin[0:NS, k:k + 1], False)
                        m1 = smask[:, S_NEW:S_NEW + DT]
                    ins.then_inc(s_free, 1)
                    dve.wait_ge(x_filled, at_x(i, kind))
                    dve.sem_inc(passed, 1)
                    mask(e_ring[0:NS, k, PAST:PAST + DT], x_ps[0:NS, 0:DT], m1, nmin2[:], True).then_inc(x_free, 1)
                    dve.wait_ge(s_free, at_u(i, n) + 2)
                    dve.wait_ge(x_free, at_x(i, kind) + 1)
                    nc.vector.tensor_tensor(nmin[0:NS, k:k + 1], nmin[0:NS, k:k + 1], nmin2[:], ALU.min).then_inc(masked, 1)

                def scale(n):
                    kind, _ = UNITS[n]
                    k = n % 4
                    dve.wait_ge(exped, at_u(i, n))
                    rt = rtot[0:NS, k:k + 1]
                    ch.step(nc.vector.reciprocal(rt, total[0:NS, k:k + 1]))
                    w = {"sd": PAST + DT, "sc": NCMP, "sl": PAST + DT, "sw": WIN + DT}[kind]
                    e = e_ring[0:NS, k, 0:w]
                    if kind == "sd":
                        nc.vector.tensor_scalar(e, e, rt, None, ALU.mult).then_inc(scaled, 1)
                    else:
                        b = {"sc": 0, "sl": 1, "sw": 2}[kind]
                        out = e_gated[:, 0:w] if kind == "sc" else e
                        nc.vector.tensor_scalar(out, e, rt, gate_b[:, b:b + 1], ALU.mult, ALU.mult).then_inc(scaled, 1)

                def ratio(n):
                    kind, j = UNITS[n]
                    k = n % 4
                    dve.wait_ge(exped, at_u(i, n))
                    if kind == "c":
                        ch.step(nc.vector.tensor_scalar(total[:, k:k + 1], total[:, k:k + 1], TINY, None, ALU.max))
                    rt = rtot[:, k:k + 1]
                    ins = nc.vector.reciprocal(rt, total[:, k:k + 1])
                    if kind in "wc":
                        ch.step(ins)
                        ins = nc.vector.tensor_tensor(rt, rt, gate_h[:, j, {"w": 2, "c": 0}[kind]:][:, 0:1], ALU.mult)
                    ins.then_inc(rt_ready, 1)

                def out(n):
                    kind, j = UNITS[n]
                    k = n % 4
                    dve.wait_ge(o_filled, at_o(i, n))
                    src = o_ps
                    if kind[0] != "s":
                        rt = rtot[:, k:k + 1]
                        dve.wait_ge(rt_ready, at_r(i, n))
                        if kind in "dl" and j == 0:
                            dve.wait_ge(acc_out[kind == "l"], i * 16 + 1)
                        if kind == "d":
                            nc.vector.tensor_scalar(acc[0][:, j, :], src[:, 0:E], rt, None, ALU.mult).then_inc(o_free, 1)
                        elif kind == "l":
                            nc.vector.tensor_scalar(acc[1][:, j, :], src[:, 0:E], rt, gate_h[:, j, 1:2], ALU.mult, ALU.mult).then_inc(o_free, 1)
                        else:
                            nc.vector.scalar_tensor_tensor(out=acc[1][:, j, :], in0=src[:, 0:E], scalar=rt, in1=acc[1][:, j, :], op0=ALU.mult, op1=ALU.add).then_inc(o_free, 1)
                        return
                    for g in range(2):
                        hp = slice(g * E, (g + 1) * E)
                        if kind == "sd":
                            ins = nc.vector.tensor_copy(oT_s[hp, 4:8, bass.ds(i * DT, DT)],
                                                        src[hp, 0:64].rearrange("p (a c) -> p a c", c=16)[:, :, g * DT:(g + 1) * DT])
                        else:
                            v = src[hp, g * 32:(g + 1) * 32]
                            if kind == "sc":
                                ins = nc.vector.tensor_copy(oa_s[hp, :], v)
                            elif kind == "sl":
                                ins = nc.vector.tensor_tensor(oa_s[hp, :], v, oa_s[hp, :], ALU.add)
                            else:
                                ins = nc.vector.tensor_tensor(oT_s[hp, 0:4, bass.ds(i * DT, DT)], v.rearrange("p (a c) -> p a c", c=DT),
                                                              oa_s[hp, :].rearrange("p (a c) -> p a c", c=DT), ALU.add)
                    ins.then_inc(o_free, 1)

                def extra(name, j):
                    if name == "hid" and j == 3:
                        dve.wait_ge(x_filled, at_x(i, name))
                        for c in range(2):
                            ins = nc.vector.tensor_scalar(hh[:, 2 * c:2 * c + 2, 0:NCMP], x_ps[:, c * P:(c + 1) * P].rearrange("p (g n) -> p g n", g=GA)[:, :, 0:NCMP],
                                                          pe_bias[:, c:c + 1], None, ALU.add)
                        ins.then_inc(x_free, 1)
                    elif name == "ckv":
                        dve.wait_ge(x_filled, at_x(i, name))
                        nc.vector.tensor_copy(kc_T[:], x_ps[:, 0:NCMP]).then_inc(x_free, 1)
                        nc.vector.tensor_copy(vc[:], x_ps[0:NCMP, P:2 * P]).then_inc(ckv_ready, 1)
                    elif name == "sel1":
                        k = unit["sc", 0] % 4
                        dve.wait_ge(x_filled, at_x(i, name))
                        nc.vector.tensor_scalar(sel[:, 0, :], x_ps[0:NS, 0:NBLK], rtot[0:NS, k:k + 1], None, ALU.mult).then_inc(x_free, 1)
                        dve.wait_ge(x_free, at_x(i, name) + 1)
                        dve.sem_inc(sel_ready, 1)
                    elif name == "sel2":
                        dve.wait_ge(x_filled, at_x(i, name))
                        nc.vector.tensor_copy(sel[:, 1, :], x_ps[0:NS, 0:NBLK]).then_inc(x_free, 1)
                        dve.wait_ge(x_free, at_x(i, name) + 1)
                        free = slice(1, NBLK - 1)
                        blk = smask[:, S_BLK:S_BLK + NBLK]
                        ch.step(nc.vector.tensor_reduce(selm[:, 0:1], sel[:, 1, free], AX, ALU.min))
                        ch.step(nc.vector.tensor_scalar(sel[:, 1, free], sel[:, 1, free], selm[:, 0:1], None, ALU.is_equal))
                        ch.step(nc.vector.tensor_tensor(sel[:, 1, free], sel[:, 1, free], blk[:, free], ALU.mult))
                        ch.step(nc.vector.tensor_reduce(selm[:, 1:2], sel[:, 1, free], AX, ALU.max))
                        ch.step(nc.vector.tensor_scalar(sel[:, 2, :], blk, selm[:, 1:2], BIG, ALU.is_equal, ALU.mult))

                for s in stages(phase):
                    sample_out = there(phase, s - 4) and UNITS[s - 4][0][0] == "s"
                    if there(phase, s - 4) and not sample_out:
                        out(s - 4)
                    sd = s == unit["sd", 0]
                    if s < NU and not sd:
                        low(s)
                    if there(phase, s - 1) and UNITS[s - 1][0][0] == "s":
                        scale(s - 1)
                    if there(phase, s - 2) and UNITS[s - 2][0][0] != "s":
                        ratio(s - 2)
                    if sample_out:
                        out(s - 4)
                    if sd:
                        low(s)
                    if there(phase, s - 2):
                        take_out(dve, i, phase, "tr", s - 2, range(unit_chunks(s - 2)), copy)
                    for name, j, qs in extras(phase, s):
                        take_out(dve, i, phase, name, j, qs, copy)
                        extra(name, j)
            for q in range(PREP_CHUNKS):
                take_chunk(dve, 0, FIRST, q, "prep", 0, q, copy)
            loop(dve, body, ch)


CHAIN_PER_PASS = 33
TAKER = lambda name, j, q: name != "prep" or q % 2 == 0
CHUNKS = DFF // P
PAIRS = CHUNKS // 2
CONV_W = 3
HALF = D // 2
PARTS = [(0, 512), (512, 512), (SEQ, NS)]
KEPT = (CONV_W - 1) * (1 + DB)


def finish(nc, t, o, scratch):
    with ExitStack() as outer:
        osb = lambda name, shape, dt=F32: outer.enter_context(nc.sbuf_tensor(name, shape, dt))
        ident = osb("f_ident", [P, P])
        x = osb("f_x", [P, STEPS, D])
        h_hi = osb("f_h_hi", [P, KC, TOK], F32R)
        h_lo = osb("f_h_lo", [P, KC, TOK], F32R)
        out_project(nc, t, scratch, ident, x, h_hi, h_lo)
        mix_channels(nc, t, o, ident, x, h_hi, h_lo)


def out_project(nc, t, scratch, ident, x, h_hi, h_lo):
    with ExitStack() as ctx:
        sb = lambda name, shape, dt=F32: ctx.enter_context(nc.sbuf_tensor(name, shape, dt))
        ps = lambda name, shape: ctx.enter_context(nc.psum_tensor(name, shape, F32))
        sem = lambda name: ctx.enter_context(nc.semaphore(name))
        w_hi = sb("o_w_hi", [P, KC, D], F32R)
        w_lo = sb("o_w_lo", [P, KC, D], F32R)
        w_raw = x
        rows = sb("o_rows", [P, 2, D])
        heads_s = sb("o_heads_s", [P, KC, NS])
        hn = sb("o_hn", [P, 2, D])
        o_hi = sb("o_o_hi", [P, 2, KC, P], F32R)
        o_lo = sb("o_o_lo", [P, 2, KC, P], F32R)
        gain = sb("o_gain", [P, D])
        ss = sb("o_ss", [P, 2])
        root = sb("o_root", [P, 2])
        rroot = sb("o_rroot", [P, 2])
        epst = sb("o_eps", [P, 1])
        po = ps("o_po", [P, D])
        ph = ps("o_ph", [P, D])
        py = [ps(f"o_py{k}", [P, D]) for k in range(2)]
        const_in, eps_set, vchain = sem("o_const_in"), sem("o_eps_set"), sem("o_vchain")
        x_in = [sem(f"o_x_in{k}") for k in range(2)]
        w_in = [sem(f"o_w_in{c}") for c in range(KC)]
        heads_in = sem("o_heads_in")
        rows_in = [sem(f"o_rows_in{k}") for k in range(2)]
        w_hi_done, w_lo_done = sem("o_w_hi_done"), sem("o_w_lo_done")
        o_turned, o_hi_done, o_lo_done = sem("o_o_turned"), sem("o_o_hi_done"), sem("o_o_lo_done")
        y_filled, y_added = sem("o_y_filled"), sem("o_y_added")
        squared, rooted, h_ready = sem("o_squared"), sem("o_rooted"), sem("o_h_ready")
        h_turned, h_hi_done, h_lo_done = sem("o_h_turned"), sem("o_h_hi_done"), sem("o_h_lo_done")
        block = ctx.enter_context(nc.Block())

        def tile_rows(i):
            return NS if isinstance(i, int) and i == STEPS // 2 else P

        def tokens(i, k):
            if tile_rows(i) == NS:
                return slice(SEQ, TOK)
            return bass.ds(i * 2 * P + k * P, P) if not isinstance(i, int) else slice((2 * i + k) * P, (2 * i + k + 1) * P)

        def x_rows(i, k):
            r = tile_rows(i)
            if isinstance(i, int):
                return x[0:r, 2 * i + k, :]
            return x[0:r, bass.ds(i * 2 + k, 1), :].rearrange("p a n -> p (a n)")

        def loop_tiles(eng, tile):
            tile(0, 0)
            tile(0, 1)
            with eng.Fori(1, TILES // 2 - 1) as i:
                tile(i, 0)
                tile(i, 1)
            tile(TILES // 2 - 1, 0)
            tile(TILES // 2 - 1, 1)
            tile(TILES // 2, 0)

        def after(i, k, n):
            if isinstance(i, int):
                s = 2 * i + k + n
                return (s // 2, s % 2) if 0 <= s < STEPS else None
            return i + (k + n) // 2, (k + n) % 2

        chunks = lambda ap: ap.rearrange("p (c q) -> p c q", c=KC)

        @block.sync
        def _(sp):
            sp.dma_start(ident[:], t["ident"]).then_inc(const_in, 16)
            for n in range(2):
                sp.dma_start(rows[:, n, :], scratch["o"][n * P:(n + 1) * P, :]).then_inc(rows_in[n], 16)
            for c in range(KC):
                for dst, src in w_o_rows(t, c):
                    sp.dma_start(w_raw[dst, c, :], src).then_inc(w_in[c], 16)
            sp.dma_start(gain[:], t["g_ffn"]).then_inc(const_in, 16)
            sp.dma_start(heads_s[:], scratch["oT"]).then_inc(heads_in, 16)
            for n in range(STEPS):
                if n >= 2:
                    sp.wait_ge(x_in[n % 2], 16 * (n // 2))
                if n < TILES:
                    sp.wait_ge(w_lo_done, n + 1)
                    sp.dma_start(x[:, n, :], t["x_prompt"][0, n * P:(n + 1) * P, :]).then_inc(x_in[n % 2], 16)
                else:
                    sp.dma_start(x[0:NS, n, :], t["x_sample"].rearrange("b s d -> (b s) d")).then_inc(x_in[n % 2], 16)

            def load(i, k):
                nxt = after(i, k, 2)
                if nxt is None or tile_rows(nxt[0]) == NS:
                    return
                sp.wait_ge(o_turned, i * 2 + (k + 1))
                sp.dma_start(rows[:, k, :], scratch["o"][tokens(*nxt), :]).then_inc(rows_in[k], 16)

            loop_tiles(sp, load)

        @block.gpsimd
        def _(pool):
            nc.gpsimd.memset(epst[:], EPS).then_inc(eps_set, 1)

        @block.tensor
        def _(pe):
            pe.sem_inc(h_turned, 1)
            pe.wait_ge(const_in, 16)

            def turn_o(i, k):
                if tile_rows(i) == NS:
                    return
                pe.wait_ge(rows_in[k], i * 16 + 16)
                if not (isinstance(i, int) and i == 0 and k == 0):
                    pe.wait_ge(o_lo_done, i * 2 + k)
                for c in range(KC):
                    last = nc.tensor.transpose(po[:, c * P:(c + 1) * P], rows[:, k, c * P:(c + 1) * P], ident[:])
                last.then_inc(o_turned, 1)

            def turn_h(i, k):
                r = tile_rows(i)
                pe.wait_ge(h_ready, i * 2 + (k + 1))
                pe.wait_ge(h_lo_done, i * 2 + (k + 0))
                for c in range(KC):
                    last = nc.tensor.transpose(ph[:, c * P:c * P + r], hn[0:r, k, c * P:(c + 1) * P], ident[0:r, 0:r])
                last.then_inc(h_turned, 1)

            turn_o(0, 0)
            pe.wait_ge(w_lo_done, KC)

            def tile(i, k):
                r = tile_rows(i)
                nxt, prev = after(i, k, 1), after(i, k, -1)
                if nxt is not None:
                    turn_o(*nxt)
                pe.wait_ge(o_lo_done, i * 2 + (k + 1))
                pe.wait_ge(y_added, i * 2 + (k + 1))
                for half in range(2):
                    hs = slice(half * HALF, (half + 1) * HALF)
                    for j, (a, w) in enumerate(((o_hi, w_hi), (o_hi, w_lo), (o_lo, w_hi))):
                        for c in range(KC):
                            last = nc.tensor.matmul(py[k][0:r, hs], a[:, k, c, 0:r], w[:, c, hs], start=(j == 0 and c == 0), stop=(j == 2 and c == KC - 1))
                last.then_inc(y_filled, 1)
                if prev is not None:
                    turn_h(*prev)

            loop_tiles(pe, tile)
            turn_h(TILES // 2, 0)

        @block.scalar
        def _(act):
            act.wait_ge(eps_set, 1)

            def split_o(i, k):
                r = tile_rows(i)
                if r == NS:
                    src = heads_s[:]
                    act.wait_ge(heads_in, 16)
                else:
                    act.wait_ge(o_turned, i * 2 + (k + 1))
                    src = chunks(po[:])
                if not (isinstance(i, int) and i == 0):
                    act.wait_ge(y_filled, i * 2 + k - 1)
                nc.scalar.activation(o_hi[:, k, :, 0:r], src, ACT.Copy).then_inc(o_hi_done, 1)

            def split_h(i, k):
                r = tile_rows(i)
                act.wait_ge(h_turned, i * 2 + (k + 2))
                nc.scalar.activation(h_hi[:, :, tokens(i, k)], chunks(ph[:])[:, :, 0:r], ACT.Copy).then_inc(h_hi_done, 1)

            for c in range(KC):
                act.wait_ge(w_in[c], 16 * len(w_o_rows(t, c)))
                nc.scalar.activation(w_hi[:, c, :], w_raw[:, c, :], ACT.Copy).then_inc(w_hi_done, 1)
            split_o(0, 0)

            def tile(i, k):
                r = tile_rows(i)
                nxt, prev = after(i, k, 1), after(i, k, -1)
                if nxt is not None:
                    split_o(*nxt)
                act.wait_ge(y_added, i * 2 + (k + 3))
                if not (isinstance(i, int) and i == 0):
                    act.wait_ge(h_turned, i * 2 + k)
                nc.scalar.activation(hn[0:r, k, :], x_rows(i, k), ACT.Square, accum_out=ss[0:r, k:k + 1]).then_inc(squared, 1)
                act.wait_ge(squared, i * 2 + (k + 1))
                nc.scalar.activation(root[0:r, k:k + 1], ss[0:r, k:k + 1], ACT.Sqrt, bias=epst[0:r, :], scale=1.0 / D).then_inc(rooted, 1)
                if prev is not None:
                    split_h(*prev)

            loop_tiles(act, tile)
            split_h(TILES // 2, 0)

        @block.vector
        def _(dve):
            dve.sem_inc(y_added, 2)
            for c in range(KC):
                dve.wait_ge(w_hi_done, c + 1)
                nc.vector.tensor_tensor(w_lo[:, c, :], w_raw[:, c, :], w_hi[:, c, :].bitcast(F32), ALU.subtract).then_inc(w_lo_done, 1)

            def split_o(i, k):
                r = tile_rows(i)
                src = heads_s[:] if r == NS else chunks(po[:])
                dve.wait_ge(o_hi_done, i * 2 + (k + 1))
                nc.vector.tensor_tensor(o_lo[:, k, :, 0:r], src, o_hi[:, k, :, 0:r].bitcast(F32), ALU.subtract).then_inc(o_lo_done, 1)

            def split_h(i, k):
                r, tok = tile_rows(i), tokens(i, k)
                dve.wait_ge(h_hi_done, i * 2 + (k + 1))
                nc.vector.tensor_tensor(h_lo[:, :, tok], chunks(ph[:])[:, :, 0:r], h_hi[:, :, tok].bitcast(F32), ALU.subtract).then_inc(h_lo_done, 1)

            split_o(0, 0)
            dve.wait_ge(const_in, 32)

            def tile(i, k):
                r = tile_rows(i)
                nxt, prev = after(i, k, 1), after(i, k, -1)
                if nxt is not None:
                    split_o(*nxt)
                dve.wait_ge(x_in[k], i * 16 + 16)
                dve.wait_ge(y_filled, i * 2 + (k + 1))
                xr = x_rows(i, k)
                nc.vector.tensor_tensor(xr, py[k][0:r, :], xr, ALU.add).then_inc(y_added, 1)
                dve.wait_ge(rooted, i * 2 + (k + 1))
                rr = rroot[0:r, k:k + 1]
                nc.vector.reciprocal(rr, root[0:r, k:k + 1]).then_inc(vchain, 1)
                dve.wait_ge(vchain, i * 2 + (k + 1))
                nc.vector.scalar_tensor_tensor(out=hn[0:r, k, :], in0=xr, scalar=rr, in1=gain[0:r, :], op0=ALU.mult, op1=ALU.mult).then_inc(h_ready, 1)
                if prev is not None:
                    split_h(*prev)

            loop_tiles(dve, tile)
            split_h(TILES // 2, 0)


def w_o_rows(t, c):
    w = t["w_o"]
    if c >= RA:
        return [(slice(0, P), w[c * P:(c + 1) * P, :])]
    return [(slice(g * E, (g + 1) * E), w[(g * RA + c) * E:(g * RA + c + 1) * E, :]) for g in range(GA)]


def mix_channels(nc, t, o, ident, x, h_hi, h_lo):
    with ExitStack() as ctx:
        sb = lambda name, shape, dt=F32: ctx.enter_context(nc.sbuf_tensor(name, shape, dt))
        ps = lambda name, shape: ctx.enter_context(nc.psum_tensor(name, shape, F32))
        sem = lambda name: ctx.enter_context(nc.semaphore(name))
        raw = sb("m_raw", [P, 4 * D])
        raw_gu = raw[:, 0:2 * D].rearrange("p (m c n) -> p m c n", m=2, c=KC)
        raw_d = raw[:, 2 * D:4 * D].rearrange("p (k n) -> p k n", k=2)
        gu_hi = [sb(f"m_gu_hi{k}", [P, 2, KC, P], F32R) for k in range(2)]
        gu_lo = [sb(f"m_gu_lo{k}", [P, 2, KC, P], F32R) for k in range(2)]
        wd_hi = sb("m_wd_hi", [P, 2, D], F32R)
        wd_lo = sb("m_wd_lo", [P, 2, D], F32R)
        ext = sb("m_ext", [P, CONV_W - 1 + SEQ])
        ext_s = sb("m_ext_s", [P, DB, CONV_W - 1 + DT])
        conv = [sb(f"m_conv{k}", [P, 512]) for k in range(2)]
        gated = [sb(f"m_gated{k}", [P, 512]) for k in range(2)]
        g_hi = sb("m_g_hi", [P, 2, TOK], F32R)
        g_lo = sb("m_g_lo", [P, 2, TOK], F32R)
        past = sb("m_past", [P, CHUNKS, (CONV_W - 1) * DB])
        kept = sb("m_kept", [P, CHUNKS, KEPT])
        taps_all = sb("m_taps_all", [P, CHUNKS, 4])
        taps = sb("m_taps", [P, 2, 4])
        pa = [ps(f"m_pa{k}", [P, 512]) for k in range(2)]
        pu = [ps(f"m_pu{k}", [P, 512]) for k in range(2)]
        pd = [ps(f"m_pd{k}", [P, 512]) for k in range(3)]
        psm = ps("m_psm", [P, 512])
        rows_s = sb("m_rows_s", [NS, 2 * P])
        (taps_in, state_in, state_turned, past_done, gu_in, wd_in, gu_hi_done, gu_lo_done, wd_hi_done, wd_lo_done, filled, copied,
         convolved, silu_done, g_made, g_hi_done, g_lo_done, d_filled, d_added, taps_ready, vchain, zeroed, kept_turned, kept_rows, y_out,
         s_filled, s_copied, passed) = (
            sem("m_" + n) for n in ("taps_in state_in state_turned past_done gu_in wd_in gu_hi_done gu_lo_done wd_hi_done wd_lo_done filled "
                                    "copied convolved silu_done g_made g_hi_done g_lo_done d_filled d_added taps_ready vchain zeroed kept_turned kept_rows y_out "
                                    "s_filled s_copied passed").split())
        UNITS_D = 2 * STEPS
        NP = 6
        block = ctx.enter_context(nc.Block())

        DOWN = [*range(0, 8), 16, 17, *range(8, 16)]
        DOWN_AFTER = {0: range(0, 10), 2: range(10, 18)}

        def banks(q, w):
            if q % 3 == 2:
                return psm[:, 2 * P:2 * P + NS], psm[:, 2 * P + NS:2 * P + 2 * NS]
            return pa[q % 3][:, 0:w], pu[q % 3][:, 0:w]

        def chunk_in(i, k):
            return bass.ds(i * 2 + k, 1) if not isinstance(i, int) else slice(2 * i + k, 2 * i + k + 1)

        def loop_pairs(eng, body):
            body(0, True, False)
            with eng.Fori(1, PAIRS - 1) as i:
                body(i, False, False)
            body(PAIRS - 1, False, True)

        def state_rows():
            r = (CONV_W - 1) * DB
            return [raw[0:r, 2 * D:4 * D], gated[0][0:r, :], gated[1][0:r, 0:DFF - 2 * D - 512]]

        @block.sync
        def _(sp):
            sp.dma_start(taps_all[:], t["taps"]).then_inc(taps_in, 16)

            def load_gu(i, k):
                for m, name in enumerate(("w_gate", "w_up")):
                    n0 = i * 2 * P + k * P
                    cols = bass.ds(n0, P) if not isinstance(i, int) else slice(n0, n0 + P)
                    sp.dma_start(raw_gu[:, m], t[name][:, cols].rearrange("(c p) n -> p c n", p=P)).then_inc(gu_in, 16)

            def load_wd(i):
                at = i * 2 * P
                rows = bass.ds(at, 2 * P) if not isinstance(i, int) else slice(at, at + 2 * P)
                sp.dma_start(raw_d, t["w_down"][rows, :].rearrange("(k p) n -> p k n", p=P)).then_inc(wd_in, 16)

            load_gu(0, 0)
            at = 0
            for dst in state_rows():
                w = dst.shape[-1]
                sp.dma_start(dst, t["state_conv"].rearrange("b w f -> (b w) f")[:, at:at + w]).then_inc(state_in, 16)
                at += w
            sp.wait_ge(state_turned, 1)
            load_wd(0)

            def body(i, more):
                sp.wait_ge(gu_lo_done, i * 2 + 1)
                load_gu(i, 1)
                if more:
                    sp.wait_ge(gu_lo_done, i * 2 + 2)
                    load_gu(i + 1, 0)
                    sp.wait_ge(wd_lo_done, i + 1)
                    load_wd(i + 1)

            with sp.Fori(0, PAIRS - 1) as i:
                body(i, True)
            body(PAIRS - 1, False)
            for n in range(STEPS):
                sp.wait_ge(d_added, 3 + (PAIRS - 1) * UNITS_D + DOWN.index(2 * n + 1) + 1)
                if n < TILES:
                    sp.dma_start(o["y_prompt"][0, n * P:(n + 1) * P, :], x[:, n, :]).then_inc(y_out, 16)
                else:
                    sp.dma_start(o["y_sample"].rearrange("b s d -> (b s) d"), x[0:NS, n, :]).then_inc(y_out, 16)
            sp.wait_ge(kept_rows, 6)
            sp.dma_start(o["conv_prompt"].rearrange("b w f -> (b w) f"), raw[0:CONV_W - 1, 0:DFF]).then_inc(y_out, 16)
            sp.dma_start(o["conv_sample"].rearrange("b w f -> (b w) f"), raw[CONV_W - 1:KEPT, 0:DFF]).then_inc(y_out, 16)
            sp.wait_ge(y_out, 16 * (STEPS + 2))

        @block.gpsimd
        def _(pool):
            nc.gpsimd.memset(ext[:, 0:CONV_W - 1], 0.0).then_inc(zeroed, 1)
            pool.wait_ge(taps_in, 16)
            nc.gpsimd.tensor_copy(taps[:], taps_all[:, 0:2, :]).then_inc(taps_ready, 1)
            with pool.Fori(1, PAIRS) as i:
                pool.wait_ge(g_made, i * NP)
                nc.gpsimd.tensor_copy(taps[:], taps_all[:, bass.ds(i * 2, 2), :]).then_inc(taps_ready, 1)

        @block.tensor
        def _(pe):
            pe.wait_ge(state_in, 48)
            c = 0
            for rows_ in state_rows():
                for k in range(rows_.shape[-1] // P):
                    last = nc.tensor.transpose(pd[0][:, c * 16:(c + 1) * 16], rows_[:, k * P:(k + 1) * P], ident[0:16, 0:16])
                    c += 1
            last.then_inc(state_turned, 1)

            products = ((gu_hi, h_hi), (gu_hi, h_lo), (gu_lo, h_hi))

            def part(i, q):
                k, (t0, w) = q // 3, PARTS[q % 3]
                if q % 3 == 0:
                    pe.wait_ge(gu_lo_done, i * 2 + (k + 1))
                if q >= 3 or not isinstance(i, int) or i > 0:
                    pe.wait_ge(g_made, i * NP + (q - 2))
                for m, bank in enumerate((pa, pu)):
                    for j, (ws, hs) in enumerate(products):
                        for c in range(KC):
                            last = nc.tensor.matmul(bank[q % 3][:, 0:w], ws[k][:, m, c, :], hs[:, c, t0:t0 + w], start=(j == 0 and c == 0), stop=(j == 2 and c == KC - 1))
                last.then_inc(filled, 1)

            def part_s(i, k):
                if k > 0 or not isinstance(i, int) or i > 0:
                    pe.wait_ge(g_made, i * NP + 3 * k)
                for j, (ws, hs) in enumerate(products):
                    for c in range(KC):
                        last = nc.tensor.matmul(psm[0:NS, 0:2 * P].rearrange("p (m n) -> p m n", m=2), hs[:, c, SEQ:TOK], ws[k][:, :, c, :],
                                                start=(j == 0 and c == 0), stop=(j == 2 and c == KC - 1))
                last.then_inc(s_filled, 1)

            def turn_s(i, k):
                pe.wait_ge(s_copied, i * 2 + (k + 1))
                pe.sem_inc(passed, 1)
                for m in range(2):
                    last = nc.tensor.transpose(psm[:, 2 * P + m * NS:2 * P + (m + 1) * NS], rows_s[:, m * P:(m + 1) * P], ident[0:NS, 0:NS])
                last.then_inc(filled, 1)

            def down(i, units):
                for d in units:
                    tile, half = DOWN[d] // 2, DOWN[d] % 2
                    r = P if tile < TILES else NS
                    tok, hs = slice(tile * P, tile * P + r), slice(half * HALF, (half + 1) * HALF)
                    if d == 0:
                        pe.wait_ge(wd_lo_done, i + 1)
                    if d in (0, 8, 10):
                        pe.wait_ge(g_lo_done, i * NP + {0: 4, 8: 6, 10: 5}[d])
                    pe.wait_ge(d_added, i * UNITS_D + (d + 1))
                    for n in range(6):
                        k, j = n // 3, n % 3
                        a, w = ((g_hi, wd_hi), (g_hi, wd_lo), (g_lo, wd_hi))[j]
                        last = nc.tensor.matmul(pd[d % 3][0:r, :], a[:, k, tok], w[:, k, hs], start=(n == 0), stop=(n == 5))
                    last.then_inc(d_filled, 1)

            def body(i, first, last):
                part(i, 0)
                if not first:
                    down(i - 1, DOWN_AFTER[0])
                part_s(i, 0)
                part(i, 1)
                turn_s(i, 0)
                if not first:
                    down(i - 1, DOWN_AFTER[2])
                part(i, 3)
                part_s(i, 1)
                part(i, 4)
                turn_s(i, 1)

            loop_pairs(pe, body)
            down(PAIRS - 1, range(UNITS_D))
            for n in range(6):
                if n < 4:
                    bank = (pa + pu)[n]
                else:
                    bank = pa[n - 4]
                    pe.wait_ge(kept_rows, n - 3)
                for c in range(4 * n, min(4 * n + 4, CHUNKS)):
                    last = nc.tensor.transpose(bank[0:KEPT, (c % 4) * P:(c % 4 + 1) * P], kept[:, c, :], ident[:])
                last.then_inc(kept_turned, 1)

        @block.scalar
        def _(act):
            act.wait_ge(zeroed, 1)

            def split_gu(i, k):
                act.wait_ge(gu_in, i * 64 + (k + 1) * 32)
                nc.scalar.activation(gu_hi[k][:], raw_gu, ACT.Copy).then_inc(gu_hi_done, 1)

            def split_g(i, q):
                k, (t0, w) = q // 3, PARTS[q % 3]
                act.wait_ge(g_made, i * NP + (q + 1))
                nc.scalar.activation(g_hi[:, k, t0:t0 + w], gated[q % 2][:, 0:w], ACT.Copy).then_inc(g_hi_done, 1)

            split_gu(0, 0)
            act.wait_ge(past_done, 1)

            def body(i, first, last):
                for q in range(NP):
                    k, (t0, w) = q // 3, PARTS[q % 3]
                    a, c = banks(q, w)[0], conv[q % 2][:, 0:w]
                    if q == 0:
                        act.wait_ge(taps_ready, i + 1)
                    if q % 3 == 1:
                        act.wait_ge(s_filled, i * 2 + (k + 1))
                        nc.scalar.activation(rows_s[:], psm[0:NS, 0:2 * P], ACT.Copy).then_inc(s_copied, 1)
                    act.wait_ge(filled, i * NP + (q + 1))
                    nc.scalar.activation(c, a, ACT.Identity, bias=taps[:, k, 3:4], scale=taps[:, k, 2:3])
                    if q % 3 < 2:
                        ins = nc.scalar.activation(ext[:, CONV_W - 1 + t0:CONV_W - 1 + t0 + w], a, ACT.Copy)
                    else:
                        nc.scalar.activation(ext_s[:, :, 0:CONV_W - 1], past[:, chunk_in(i, k), :].rearrange("p a (b w) -> p (a b) w", w=CONV_W - 1), ACT.Copy)
                        ins = nc.scalar.activation(ext_s[:, :, CONV_W - 1:], a.rearrange("p (b s) -> p b s", s=DT), ACT.Copy)
                    ins.then_inc(copied, 1)
                    if q % 3 == 1:
                        nc.scalar.activation(kept[:, chunk_in(i, k), 0:CONV_W - 1], a[:, w - CONV_W + 1:w].unsqueeze(1), ACT.Copy)
                    if q % 3 == 2:
                        nc.scalar.activation(kept[:, chunk_in(i, k), CONV_W - 1:KEPT].rearrange("p a (b w) -> p (a b) w", w=CONV_W - 1),
                                             a.rearrange("p (b s) -> p b s", s=DT)[:, :, DT - CONV_W + 1:], ACT.Copy)
                    act.wait_ge(convolved, i * NP + (q + 1))
                    nc.scalar.activation(c, c, ACT.Silu).then_inc(silu_done, 1)
                    if q == 0:
                        if not first:
                            split_g(i - 1, NP - 1)
                        split_gu(i, 1)
                    else:
                        if not first and q <= 2:
                            act.wait_ge(d_filled, (i - 1) * UNITS_D + (8, UNITS_D)[q - 1])
                        split_g(i, q - 1)
                    if q == 3 and not last:
                        split_gu(i + 1, 0)
                    if q == 4:
                        act.wait_ge(wd_in, i * 16 + 16)
                        nc.scalar.activation(wd_hi[:], raw_d, ACT.Copy).then_inc(wd_hi_done, 1)

            loop_pairs(act, body)
            split_g(PAIRS - 1, NP - 1)

        @block.vector
        def _(dve):
            dve.sem_inc(d_added, 3)
            dve.wait_ge(state_turned, 1)
            nc.vector.tensor_copy(past[:].rearrange("p c n -> p (c n)"), pd[0][:, 0:CHUNKS * 16]).then_inc(past_done, 1)

            def split_gu(i, k):
                dve.wait_ge(gu_hi_done, i * 2 + (k + 1))
                nc.vector.tensor_tensor(gu_lo[k][:], raw_gu, gu_hi[k][:].bitcast(F32), ALU.subtract).then_inc(gu_lo_done, 1)

            def split_g(i, q):
                k, (t0, w) = q // 3, PARTS[q % 3]
                dve.wait_ge(g_hi_done, i * NP + (q + 1))
                nc.vector.tensor_tensor(g_lo[:, k, t0:t0 + w], gated[q % 2][:, 0:w], g_hi[:, k, t0:t0 + w].bitcast(F32), ALU.subtract).then_inc(g_lo_done, 1)

            def add(i, units):
                for d in units:
                    tile, half = DOWN[d] // 2, DOWN[d] % 2
                    r = P if tile < TILES else NS
                    xs = x[0:r, tile, half * HALF:(half + 1) * HALF]
                    dve.wait_ge(d_filled, i * UNITS_D + (d + 1))
                    nc.vector.tensor_tensor(xs, pd[d % 3][0:r, :], xs, ALU.add).then_inc(d_added, 1)

            split_gu(0, 0)

            def body(i, first, last):
                for q in range(NP):
                    k, (t0, w) = q // 3, PARTS[q % 3]
                    c, u = conv[q % 2][:, 0:w], banks(q, w)[1]
                    dve.wait_ge(copied, i * NP + (q + 1))
                    if q % 3 < 2:
                        taps_at = [ext[:, t0 + n:t0 + n + w] for n in range(2)]
                        cv = c
                    else:
                        taps_at = [ext_s[:, :, n:n + DT] for n in range(2)]
                        cv = c.rearrange("p (b s) -> p b s", s=DT)
                    nc.vector.scalar_tensor_tensor(out=cv, in0=taps_at[1], scalar=taps[:, k, 1:2], in1=cv, op0=ALU.mult, op1=ALU.add).then_inc(vchain, 1)
                    dve.wait_ge(vchain, i * NP + (q + 1))
                    nc.vector.scalar_tensor_tensor(out=cv, in0=taps_at[0], scalar=taps[:, k, 0:1], in1=cv, op0=ALU.mult, op1=ALU.add).then_inc(convolved, 1)
                    if not first:
                        add(i - 1, {0: range(0, 2), 1: range(10, 11), 2: range(12, 13)}.get(q, ()))
                    dve.wait_ge(silu_done, i * NP + (q + 1))
                    nc.vector.tensor_tensor(gated[q % 2][:, 0:w], c, u, ALU.mult).then_inc(g_made, 1)
                    if not first and q == 0:
                        split_g(i - 1, NP - 1)
                    if not first:
                        add(i - 1, {0: range(2, 10), 1: range(11, 12), 2: range(13, 18)}.get(q, ()))
                    if q > 0:
                        split_g(i, q - 1)
                    if q == 0:
                        split_gu(i, 1)
                    if q == 3 and not last:
                        split_gu(i + 1, 0)
                    if q == 4:
                        dve.wait_ge(wd_hi_done, i + 1)
                        nc.vector.tensor_tensor(wd_lo[:], raw_d, wd_hi[:].bitcast(F32), ALU.subtract).then_inc(wd_lo_done, 1)

            loop_pairs(dve, body)
            split_g(PAIRS - 1, NP - 1)
            add(PAIRS - 1, range(UNITS_D))
            for n in range(6):
                w = (min(4 * n + 4, CHUNKS) - 4 * n) * P
                bank = (pa + pu)[n] if n < 4 else pa[n - 4]
                dve.wait_ge(kept_turned, n + 1)
                nc.vector.tensor_copy(raw[0:KEPT, 4 * n * P:4 * n * P + w], bank[0:KEPT, 0:w]).then_inc(kept_rows, 1)


def rope_table():
    half = ROT // 2
    inv = np.float32(500000.0) ** (np.float32(-2.0) * np.arange(half, dtype=np.float32) / np.float32(ROT))
    pos = np.concatenate([np.arange(SEQ), np.tile(PAST + np.arange(DT), DB)]).astype(np.float32)
    ang = (pos[:, None] * inv.astype(np.float32)[None, :]).astype(np.float64)
    c, s = np.cos(ang), np.sin(ang)
    return np.concatenate([c, c, -s, s], 1).astype(np.float32)


OUTS = {
    "y_prompt": (1, SEQ, D), "y_sample": (DB, DT, D),
    "cmp_prompt": (1, SEQ, 2, GA, E), "cmp_sample": (DB, DT, 2, GA, E),
    "slc_prompt": (1, SEQ, 2, GA, E), "slc_sample": (DB, DT, 2, GA, E),
    "win_prompt": (1, WIN, 2, GA, E), "win_sample": (DB, WIN, 2, GA, E),
    "dil_prompt": (1, SEQ, 2, HB, E), "dil_sample": (DB, PAST + DT, 2, HB, E),
    "conv_prompt": (1, CONV_W - 1, DFF), "conv_sample": (DB, CONV_W - 1, DFF),
}
SCRATCH = {"qa": (TOK, HA * E), "qb": (TOK, HB * E), "kvw": (TOK, 2 * GA * E), "gl": (TOK, 3 * HA), "kvc": (NS, 2, GA, E),
           "o": (SEQ, D), "oT": (P, KC, NS)}


def build(nc, t, o):
    scratch = {n: nc.dram_tensor("scratch_" + n, s, F32, kind="Internal").ap() for n, s in SCRATCH.items()}
    with ExitStack() as ctx:
        const = shared_constants(nc, t, ctx)
        project(nc, t, o, scratch, const)
        attend(nc, t, o, scratch, const)
    finish(nc, t, o, scratch)


def kernel(**inputs):
    import concourse.bacc as bacc
    from concourse.bass_utils import run_bass_kernel_spmd

    x = {n: np.asarray(a) for n, a in inputs.items()}
    masks, smask = tables()
    across = lambda a, n: np.broadcast_to(a, (n,) + a.shape)
    gains = np.stack([x[n] for n in ("gq_a", "gk_cmp", "gk_slc", "gk_win", "gq_b", "gk_b")])
    data = {n: x[n] for n in ("x_prompt", "x_sample", "cache_cmp", "cache_slc", "state_win", "state_dil", "state_conv", "page_table",
                              "w_in", "w1_cmp_k", "w2_cmp_k", "w1_cmp_v", "w2_cmp_v", "w_o", "w_gate", "w_up", "w_down")}
    data.update(
        ident=np.eye(P, dtype=np.float32), rope=rope_table(), masks=masks, smask=smask,
        g_attn=x["g_attn"].reshape(KC, P).T, gains=across(gains, P), g_ffn=across(x["g_ffn"], P),
        peT=np.stack([x["pe_cmp_" + n].reshape(CMP_LEN * E // P, P).T for n in "kv"], 1),
        taps=np.concatenate([x["conv_w"], x["conv_b"][None]], 0).reshape(CONV_W + 1, CHUNKS, P).transpose(2, 1, 0))
    data = {n: np.ascontiguousarray(a) for n, a in data.items()}
    nc = bacc.Bacc("TRN2", target_bir_lowering=False, num_devices=1)
    t = {n: nc.dram_tensor("in_" + n, a.shape, mybir.dt.from_np(a.dtype), kind="ExternalInput").ap() for n, a in data.items()}
    o = {n: nc.dram_tensor("out_" + n, s, F32, kind="ExternalOutput").ap() for n, s in OUTS.items()}
    build(nc, t, o)
    r = run_bass_kernel_spmd(nc, [{"in_" + n: a for n, a in data.items()}], core_ids=[0])
    return tuple(r.results[0]["out_" + n] for n in OUTS)
```
